# Optimizing a Trainium2 kernel written in Bass

```python
import jax, jax.numpy as jnp
from jax import lax
import numpy as np
import math

D_MODEL = 2048
BATCH = 1
SEQ = 256
DEPTH = 1

HEAD_DIM = 64
N_HEADS_SWA = 16
N_KV_SWA = 2
N_HEADS_FOX = 16
WINDOW = 128
BLOCK = 128
D_FF = 5632
CONV_WIDTH = 3
EPS = 1e-6
D_SWA = N_HEADS_SWA * HEAD_DIM
D_KV_SWA = N_KV_SWA * HEAD_DIM
D_FOX = N_HEADS_FOX * HEAD_DIM
D_MIX = D_SWA + D_FOX
D_IN = D_SWA + 2 * D_KV_SWA + 3 * D_FOX + N_HEADS_FOX


def rmsnorm(x, g):
    xf = x.astype(jnp.float32)
    y = xf * lax.rsqrt(jnp.mean(xf * xf, axis=-1, keepdims=True) + EPS)
    return (y * g.astype(jnp.float32)).astype(x.dtype)

def alibi_slopes(n):
    return jnp.asarray(2.0 ** (-8.0 * np.arange(1, n + 1) / n), dtype=jnp.float32)

def swa_sink_attention(q, k, v, sinks):
    B, S, H, D = q.shape
    KV = k.shape[2]
    G = H // KV
    nB = S // BLOCK
    scale = 1.0 / np.sqrt(D)
    qb = q.reshape(B, nB, BLOCK, KV, G, D)

    def band(t):
        tp = jnp.pad(t, ((0, 0), (BLOCK, 0), (0, 0), (0, 0)))[:, :S]
        return jnp.concatenate([tp.reshape(B, nB, BLOCK, KV, D), t.reshape(B, nB, BLOCK, KV, D)], axis=2)

    kb, vb = band(k), band(v)
    s = jnp.einsum('bnqkgd,bnskd->bnkgqs', qb, kb).astype(jnp.float32) * scale
    q_loc = BLOCK + jnp.arange(BLOCK)
    k_loc = jnp.arange(2 * BLOCK)
    dist = (q_loc[:, None] - k_loc[None, :]).astype(jnp.float32)
    blk_start = jnp.arange(nB) * BLOCK - BLOCK
    k_abs = blk_start[:, None] + k_loc[None, :]
    mask = (dist >= 0)[None] & (dist < WINDOW)[None] & (k_abs >= 0)[:, None, :]
    slopes = alibi_slopes(H).reshape(KV, G)
    s = s - slopes[:, :, None, None] * dist
    s = jnp.where(mask[None, :, None, None], s, -jnp.inf)
    sink = sinks.astype(jnp.float32).reshape(KV, G)[None, None, :, :, None, None]
    m = jnp.maximum(jnp.max(s, axis=-1, keepdims=True), sink)
    p = jnp.exp(s - m)
    p = p / (jnp.sum(p, axis=-1, keepdims=True) + jnp.exp(sink - m))
    o = jnp.einsum('bnkgqs,bnskd->bnqkgd', p.astype(v.dtype), vb)
    return o.reshape(B, S, H, D)

def forgetting_attention(q, k, v, log_f):
    B, S, H, D = q.shape
    nB = S // BLOCK
    scale = 1.0 / np.sqrt(D)
    c = lax.cumsum(log_f, axis=1)
    cT = jnp.transpose(c, (0, 2, 1))
    qb = jnp.moveaxis(q.reshape(B, nB, BLOCK, H, D), 1, 0)
    cb = jnp.moveaxis(cT.reshape(B, H, nB, BLOCK), 2, 0)
    k_pos = jnp.arange(S)

    def one_block(args):
        q_blk, c_blk, n = args
        s = jnp.einsum('bqhd,bshd->bhqs', q_blk, k).astype(jnp.float32) * scale
        s = s + c_blk[..., None] - cT[:, :, None, :]
        q_pos = n * BLOCK + jnp.arange(BLOCK)
        s = jnp.where((q_pos[:, None] >= k_pos[None, :])[None, None], s, -jnp.inf)
        p = jax.nn.softmax(s, axis=-1)
        return jnp.einsum('bhqs,bshd->bqhd', p.astype(v.dtype), v)

    o = lax.map(one_block, (qb, cb, jnp.arange(nB)))
    return jnp.moveaxis(o, 0, 1).reshape(B, S, H, D)

def causal_dwconv(u, w, b):
    S = u.shape[1]
    up = jnp.pad(u, ((0, 0), (CONV_WIDTH - 1, 0), (0, 0)))
    y = b
    for kk in range(CONV_WIDTH):
        y = y + up[:, kk:kk + S] * w[kk]
    return y

def first_inputs(seed: int = 0) -> dict:
    key = jax.random.key(seed)
    ks = jax.random.split(key, 17)
    f32 = jnp.float32
    nrm = lambda k, shape, s: jax.random.normal(k, shape, f32) * s
    gain = lambda k, n: 1.0 + 0.05 * jax.random.normal(k, (DEPTH, n), f32)
    return {
        "x": jax.random.normal(ks[0], (BATCH, SEQ, D_MODEL), f32),
        "pre_mix_g": gain(ks[1], D_MODEL),
        "w_in": nrm(ks[2], (DEPTH, D_MODEL, D_IN), D_MODEL ** -0.5),
        "b_forget": 2.0 + 0.5 * jax.random.normal(ks[3], (DEPTH, N_HEADS_FOX), f32),
        "sinks": nrm(ks[4], (DEPTH, N_HEADS_SWA), 1.0),
        "grp_swa_g": gain(ks[5], D_SWA),
        "grp_fox_g": gain(ks[6], D_FOX),
        "w_out": nrm(ks[7], (DEPTH, D_MIX, D_MODEL), D_MIX ** -0.5),
        "post_mix_g": gain(ks[8], D_MODEL),
        "pre_ffn_g": gain(ks[9], D_MODEL),
        "w_up": nrm(ks[10], (DEPTH, D_MODEL, 2 * D_FF), D_MODEL ** -0.5),
        "conv_w": nrm(ks[11], (DEPTH, CONV_WIDTH, 2 * D_FF), CONV_WIDTH ** -0.5),
        "conv_b": nrm(ks[12], (DEPTH, 2 * D_FF), 0.02),
        "w_down": nrm(ks[13], (DEPTH, D_FF, D_MODEL), D_FF ** -0.5),
        "post_ffn_g": gain(ks[14], D_MODEL),
    }

def first_block(x, pre_mix_g, w_in, b_forget, sinks, grp_swa_g, grp_fox_g, w_out, post_mix_g,
              pre_ffn_g, w_up, conv_w, conv_b, w_down, post_ffn_g):
    B, S, _ = x.shape
    cuts = np.cumsum([D_SWA, D_KV_SWA, D_KV_SWA, D_FOX, D_FOX, D_FOX])
    for l in range(DEPTH):
        h = rmsnorm(x, pre_mix_g[l])
        proj = h @ w_in[l]
        q_a, k_a, v_a, q_b, k_b, v_b, f_b = jnp.split(proj, cuts, axis=-1)
        o_a = swa_sink_attention(q_a.reshape(B, S, N_HEADS_SWA, HEAD_DIM),
                                 k_a.reshape(B, S, N_KV_SWA, HEAD_DIM),
                                 v_a.reshape(B, S, N_KV_SWA, HEAD_DIM), sinks[l])
        log_f = jax.nn.log_sigmoid(f_b.astype(jnp.float32) + b_forget[l].astype(jnp.float32))
        o_b = forgetting_attention(q_b.reshape(B, S, N_HEADS_FOX, HEAD_DIM),
                                   k_b.reshape(B, S, N_HEADS_FOX, HEAD_DIM),
                                   v_b.reshape(B, S, N_HEADS_FOX, HEAD_DIM), log_f)
        o_a = rmsnorm(o_a.reshape(B, S, D_SWA), grp_swa_g[l])
        o_b = rmsnorm(o_b.reshape(B, S, D_FOX), grp_fox_g[l])
        mix = jnp.concatenate([o_a, o_b], axis=-1) @ w_out[l]
        x = x + rmsnorm(mix, post_mix_g[l])
        h = rmsnorm(x, pre_ffn_g[l])
        u = causal_dwconv(h @ w_up[l], conv_w[l], conv_b[l])
        gate, val = jnp.split(u, 2, axis=-1)
        y = (jax.nn.gelu(gate, approximate=True) * val) @ w_down[l]
        x = x + rmsnorm(y, post_ffn_g[l])
    return x


HEAD_DIM_2 = 128
DIL_PATTERNS = ((128, 1), (512, 4), (2048, 16))
A_HEADS_PER_GROUP = 4
A_HEADS = A_HEADS_PER_GROUP * len(DIL_PATTERNS)
A_OUT = A_HEADS_PER_GROUP * HEAD_DIM_2
B_HEADS = 8
B_WIDTH = B_HEADS * HEAD_DIM_2
MOBA_BLOCK = 256
MOBA_TOPK = 3
MOBA_CHUNK = 32
N_HEADS_TOTAL = A_HEADS + B_HEADS
N_BUCKETS = 32
MAX_DISTANCE = 2048
D_FF_2 = 4 * D_MODEL
SCALE = HEAD_DIM_2 ** -0.5
A_QKV = 3 * A_HEADS * HEAD_DIM_2
B_QKV = 3 * B_WIDTH
IN_WIDTH = A_QKV + B_QKV + 2 * D_MODEL


def rms_norm(x, g):
    x32 = x.astype(jnp.float32)
    y = x32 * lax.rsqrt(jnp.mean(x32 * x32, axis=-1, keepdims=True) + EPS)
    return y.astype(x.dtype) * g

def rel_bucket(dist):
    max_exact = N_BUCKETS // 2
    d = jnp.maximum(dist, 0)
    df = jnp.maximum(d, 1).astype(jnp.float32)
    large = max_exact + (jnp.log(df / max_exact) / math.log(MAX_DISTANCE / max_exact)
                         * (N_BUCKETS - max_exact)).astype(jnp.int32)
    large = jnp.minimum(large, N_BUCKETS - 1)
    return jnp.where(d < max_exact, d, large)

def dilated_group(q, k, v, bias_tab, window, dilation):
    Bsz, H, S, hd = q.shape
    r = dilation
    W = window // r
    Q = W
    L = S // r
    nb = -(-L // Q)
    Lp = nb * Q

    def to_sub(t):
        t = t.reshape(Bsz, H, L, r, hd).transpose(0, 1, 3, 2, 4)
        t = jnp.pad(t, ((0, 0), (0, 0), (0, 0), (0, Lp - L), (0, 0)))
        return t.reshape(Bsz, H, r, nb, Q, hd)

    qs, ks, vs = to_sub(q), to_sub(k), to_sub(v)

    def with_prev(t):
        prev = jnp.pad(t, ((0, 0), (0, 0), (0, 0), (1, 0), (0, 0), (0, 0)))[:, :, :, :nb]
        return jnp.concatenate([prev, t], axis=4)

    kk, vv = with_prev(ks), with_prev(vs)
    a = jnp.arange(Q)[:, None]
    j = jnp.arange(2 * Q)[None, :]
    delta = a + Q - j
    in_band = (delta >= 0) & (delta <= W)
    valid_start = (jnp.arange(nb)[:, None, None] > 0) | (j[None] >= Q)
    mask = in_band[None] & valid_start
    bias = bias_tab[rel_bucket(delta * r)].transpose(2, 0, 1)

    logits = (jnp.einsum('bhrnqd,bhrnkd->bhrnqk', qs, kk).astype(jnp.float32) * SCALE
              + bias[:, None, None].astype(jnp.float32))
    logits = jnp.where(mask, logits, -jnp.inf)
    m = jnp.max(logits, axis=-1, keepdims=True)
    p = jnp.exp(logits - m)
    den = jnp.sum(p, axis=-1, keepdims=True)
    out = jnp.einsum('bhrnqk,bhrnkd->bhrnqd', (p / den).astype(v.dtype), vv)
    lse = (m + jnp.log(den))[..., 0]

    out = out.reshape(Bsz, H, r, Lp, hd)[:, :, :, :L].transpose(0, 1, 3, 2, 4).reshape(Bsz, H, S, hd)
    lse = lse.reshape(Bsz, H, r, Lp)[:, :, :, :L].transpose(0, 1, 3, 2).reshape(Bsz, H, S)
    return out, lse

def moba_attention(q, k, v, bias_tab):
    Bsz, H, S, hd = q.shape
    BS = MOBA_BLOCK
    nb = -(-S // BS)
    Sp = nb * BS
    pad = ((0, 0), (0, 0), (0, Sp - S), (0, 0))
    kb = jnp.pad(k, pad).reshape(Bsz, H, nb, BS, hd)
    vb = jnp.pad(v, pad).reshape(Bsz, H, nb, BS, hd)

    kmean = jnp.mean(kb.astype(jnp.float32), axis=3)
    gate = jnp.einsum('bhsd,bhnd->bhsn', q.astype(jnp.float32), kmean)
    pos = jnp.arange(S)
    past = jnp.arange(nb)[None, :] < (pos // BS)[:, None]
    gate = jnp.where(past, gate, -jnp.inf)
    n_sel = min(MOBA_TOPK, nb)
    top_s, top_i = lax.top_k(gate, n_sel)
    top_ok = top_s > -jnp.inf

    C = MOBA_CHUNK
    nc = S // C
    b_ix = jnp.arange(Bsz)[:, None, None, None]
    h_ix = jnp.arange(H)[None, :, None, None]
    bias_h = bias_tab.T

    def chunk(c):
        s0 = c * C
        qc = lax.dynamic_slice_in_dim(q, s0, C, axis=2)
        ic = lax.dynamic_slice_in_dim(top_i, s0, C, axis=2)
        okc = lax.dynamic_slice_in_dim(top_ok, s0, C, axis=2)
        qpos = s0 + jnp.arange(C)
        kg = kb[b_ix, h_ix, ic]
        vg = vb[b_ix, h_ix, ic]
        dist_sel = qpos[:, None, None] - (ic[..., None] * BS + jnp.arange(BS))
        l_sel = (jnp.einsum('bhcd,bhckjd->bhckj', qc, kg).astype(jnp.float32) * SCALE
                 + bias_h[h_ix[..., None], rel_bucket(dist_sel)].astype(jnp.float32))
        l_sel = jnp.where(okc[..., None], l_sel, -jnp.inf).reshape(Bsz, H, C, n_sel * BS)

        blk = s0 // BS
        ko = lax.dynamic_slice_in_dim(kb, blk, 1, axis=2)[:, :, 0]
        vo = lax.dynamic_slice_in_dim(vb, blk, 1, axis=2)[:, :, 0]
        dist_own = qpos[:, None] - (blk * BS + jnp.arange(BS))[None, :]
        l_own = (jnp.einsum('bhcd,bhjd->bhcj', qc, ko).astype(jnp.float32) * SCALE
                 + bias_h[:, rel_bucket(dist_own)][None].astype(jnp.float32))
        l_own = jnp.where(dist_own >= 0, l_own, -jnp.inf)

        p = jax.nn.softmax(jnp.concatenate([l_sel, l_own], axis=-1), axis=-1).astype(v.dtype)
        p_sel = p[..., :n_sel * BS].reshape(Bsz, H, C, n_sel, BS)
        p_own = p[..., n_sel * BS:]
        return (jnp.einsum('bhckj,bhckjd->bhcd', p_sel, vg)
                + jnp.einsum('bhcj,bhjd->bhcd', p_own, vo))

    out = lax.map(chunk, jnp.arange(nc))
    return out.transpose(1, 2, 0, 3, 4).reshape(Bsz, H, S, hd)

def head_rms(t, g):
    t32 = t.astype(jnp.float32)
    y = t32 * lax.rsqrt(jnp.mean(t32 * t32, axis=-1, keepdims=True) + EPS)
    return y.astype(t.dtype) * g

def second_inputs(seed: int = 0) -> dict:
    key = jax.random.key(seed)
    ks = jax.random.split(key, 16)
    f32 = jnp.float32
    nrm = lambda k, shape, fan: jax.random.normal(k, shape, f32) * (fan ** -0.5)
    gain = lambda k, n: 1.0 + 0.02 * jax.random.normal(k, (n,), f32)
    return {
        "x": jax.random.normal(ks[0], (BATCH, SEQ, D_MODEL), f32),
        "g_mix": gain(ks[1], D_MODEL),
        "w_in": nrm(ks[2], (D_MODEL, IN_WIDTH), D_MODEL),
        "q_norm_a": gain(ks[3], HEAD_DIM_2),
        "k_norm_a": gain(ks[4], HEAD_DIM_2),
        "q_norm_b": gain(ks[5], HEAD_DIM_2),
        "k_norm_b": gain(ks[6], HEAD_DIM_2),
        "rel_bias": 0.5 * jax.random.normal(ks[7], (N_BUCKETS, N_HEADS_TOTAL), f32),
        "w_branch_a": nrm(ks[8], (A_OUT, D_MODEL), A_OUT),
        "w_branch_b": nrm(ks[9], (B_WIDTH, D_MODEL), B_WIDTH),
        "w_out": nrm(ks[10], (D_MODEL, D_MODEL), D_MODEL),
        "g_mlp": gain(ks[11], D_MODEL),
        "w_up": nrm(ks[12], (D_MODEL, D_FF_2), D_MODEL),
        "w_down": nrm(ks[13], (D_FF_2, D_MODEL), D_FF_2),
    }

def second_block(x, g_mix, w_in, q_norm_a, k_norm_a, q_norm_b, k_norm_b, rel_bias,
              w_branch_a, w_branch_b, w_out, g_mlp, w_up, w_down):
    Bsz, S, D = x.shape
    for _ in range(DEPTH):
        h = rms_norm(x, g_mix)
        proj = h @ w_in
        a_qkv = proj[..., :A_QKV].reshape(Bsz, S, 3, A_HEADS, HEAD_DIM_2)
        b_qkv = proj[..., A_QKV:A_QKV + B_QKV].reshape(Bsz, S, 3, B_HEADS, HEAD_DIM_2)
        g_a = proj[..., A_QKV + B_QKV:A_QKV + B_QKV + D_MODEL]
        g_b = proj[..., A_QKV + B_QKV + D_MODEL:]

        qa = head_rms(a_qkv[:, :, 0], q_norm_a).transpose(0, 2, 1, 3)
        ka = head_rms(a_qkv[:, :, 1], k_norm_a).transpose(0, 2, 1, 3)
        va = a_qkv[:, :, 2].transpose(0, 2, 1, 3)
        outs, lses = [], []
        for gi, (win, dil) in enumerate(DIL_PATTERNS):
            hs = slice(gi * A_HEADS_PER_GROUP, (gi + 1) * A_HEADS_PER_GROUP)
            o, l = dilated_group(qa[:, hs], ka[:, hs], va[:, hs], rel_bias[:, hs], win, dil)
            outs.append(o)
            lses.append(l)
        wts = jax.nn.softmax(jnp.stack(lses, axis=0), axis=0)
        ya = jnp.sum(wts[..., None] * jnp.stack(outs, axis=0).astype(jnp.float32), axis=0).astype(x.dtype)
        ya = ya.transpose(0, 2, 1, 3).reshape(Bsz, S, A_OUT) @ w_branch_a

        qb = head_rms(b_qkv[:, :, 0], q_norm_b).transpose(0, 2, 1, 3)
        kb = head_rms(b_qkv[:, :, 1], k_norm_b).transpose(0, 2, 1, 3)
        vb = b_qkv[:, :, 2].transpose(0, 2, 1, 3)
        yb = moba_attention(qb, kb, vb, rel_bias[:, A_HEADS:])
        yb = yb.transpose(0, 2, 1, 3).reshape(Bsz, S, B_WIDTH) @ w_branch_b

        mixed = jax.nn.sigmoid(g_a) * ya + jax.nn.sigmoid(g_b) * yb
        x = x + mixed @ w_out

        h2 = rms_norm(x, g_mlp)
        x = x + jnp.square(jax.nn.relu(h2 @ w_up)) @ w_down
    return x


def setup_inputs(seed=0):
    out = dict(first_inputs(seed))
    for name, value in second_inputs(seed + 1).items():
        if name != "x":
            out[name + "_2"] = value
    return out


def reference(
    x, pre_mix_g, w_in, b_forget, sinks, grp_swa_g, grp_fox_g, w_out, post_mix_g, pre_ffn_g,
    w_up, conv_w, conv_b, w_down, post_ffn_g, g_mix_2, w_in_2, q_norm_a_2, k_norm_a_2,
    q_norm_b_2, k_norm_b_2, rel_bias_2, w_branch_a_2, w_branch_b_2, w_out_2, g_mlp_2, w_up_2,
    w_down_2,
):
    x = first_block(
        x, pre_mix_g, w_in, b_forget, sinks, grp_swa_g, grp_fox_g, w_out, post_mix_g, pre_ffn_g,
        w_up, conv_w, conv_b, w_down, post_ffn_g,
    )
    return second_block(
        x, g_mix_2, w_in_2, q_norm_a_2, k_norm_a_2, q_norm_b_2, k_norm_b_2, rel_bias_2,
        w_branch_a_2, w_branch_b_2, w_out_2, g_mlp_2, w_up_2, w_down_2,
    )


_drawn_inputs = setup_inputs


def setup_inputs(seed=0):
    import zlib

    import numpy as np

    out = dict(_drawn_inputs(seed))
    spreads = {}
    factors = {'conv_b': 3.313,
     'g_mix_2': 8.0,
     'q_norm_a_2': 8.0,
     'k_norm_a_2': 8.0,
     'q_norm_b_2': 8.0,
     'k_norm_b_2': 8.0,
     'g_mlp_2': 4.324}
    for name, (base, spread) in spreads.items():
        noise = np.random.default_rng([zlib.crc32(name.encode()), seed]).standard_normal(out[name].shape)
        drawn = base * np.exp(spread * noise) if base else spread * noise
        out[name] = __import__('jax').numpy.asarray(drawn.astype(out[name].dtype))
    for name, factor in factors.items():
        out[name] = (out[name] * factor).astype(out[name].dtype)
    return out
```

```python
from contextlib import ExitStack

import numpy as np

import concourse.bass as bass
from concourse import mybir

F32 = mybir.dt.float32
F32R = mybir.dt.float32r
ALU = mybir.AluOpType
ACT = mybir.ActivationFunctionType
AX = mybir.AxisListType

P = 128
T = 256
D = 2048
KT = D // P
EPS = 1e-6
BIG = 1e30
LOWEST = -3e38

HD1 = 64
N_SWA = 16
N_KV = 2
N_FOX = 16
WINDOW = 128
FF1 = 5632
F1T = FF1 // P
CHUNKS1 = (12, 12, 12, 8)
HD2 = 128
A_HEADS = 12
A_SLOTS = 4
GROUPS = ((128, 1), (512, 4), (2048, 16))
B_HEADS = 8
N_BUCKETS = 32
MAX_DISTANCE = 2048
FF2 = 4 * D
F2T = FF2 // P
N_DIST = 384

RAW_SLOTS = 4
W_SLOTS = 4
UNIT = 16
AHEAD = 3
WIDE = 3

PV = {}
_at = 0
for _name, _n in (("pre_mix", KT), ("grp", KT), ("post_mix", KT), ("pre_ffn", KT), ("post_ffn", KT),
                  ("g_mix2", KT), ("g_mlp2", KT), ("qa", 1), ("ka", 1), ("qb", 1), ("kb", 1),
                  ("bf", 1), ("sinks", N_SWA), ("conv", 2 * F1T * 4)):
    PV[_name] = _at
    _at += _n
N_PV = _at
CS = {}
_at = 0
for _name, _n in (("ident", P), ("ones", P), ("triu", P), ("causal", T), ("window", T),
                  ("lhs_swa", T), ("rhs_swa", T), ("slope", 8), ("pick", 8), ("mA", 1), ("cA", 1),
                  ("mB", 1), ("cB", 1), ("sgn", 1)):
    CS[_name] = _at
    _at += _n
N_CS = _at


class Stage:

    def __init__(self, name, iters, units, blocks, mtiles, prev):
        self.name, self.iters, self.units, self.blocks, self.mtiles = name, iters, units, blocks, mtiles
        assert sum(mtiles) == units * blocks and blocks <= UNIT
        self.start = [sum(mtiles[:p]) for p in range(len(mtiles))]
        self.nm = len(mtiles)
        self.ubase = prev.ubase + prev.iters * prev.units if prev else 0
        self.gbase = prev.gbase + prev.iters * prev.nm if prev else 0
        assert iters == 1 or units % W_SLOTS == 0
        self.prev = prev
        if prev:
            prev.next = self
        self.next = None
        self.bank0 = (prev.bank0 + prev.nm * (1 if prev.nm % 2 else 0)) % 2 if prev else 0
        self.half = (blocks + 1) // 2
        self.wide = name in ("pre", "up1_0", "in2", "up2_0")

    def g(self, it, p):
        return it * self.nm + (self.gbase + p)

    def u(self, it, k):
        return it * self.units + (self.ubase + k)

    def bank(self, p):
        return (self.bank0 + p) % 2

    def free_after(self, p):
        return 1 if p == 0 and self.nm % 2 and self.iters > 1 else 2

    def splits(self, p):
        until = self.start[p] // self.blocks + AHEAD if p < self.nm - 1 else self.units - 1 + AHEAD
        before = self.start[p - 1] // self.blocks + AHEAD if p else AHEAD - 1
        return range(before + 1, until + 1)


def make_stages():
    out = []

    def add(*a):
        out.append(Stage(*a, out[-1] if out else None))

    add("pre", 1, 3, 16, [16] * 3)
    add("in1", 8, 4, 16, [16] * 4)
    add("out1", 4, 4, 16, [8, 8] * 4)
    for c, n in enumerate(CHUNKS1):
        add(f"up1_{c}", n // 2, 4, 16, [16] * 4)
        add(f"dn1_{c}", 4, 4, n, [n] * 4)
    add("in2", A_SLOTS, 16, 15, [16] * 15)
    add("mix2", KT, 4, 11, [16, 16, 4, 8])
    add("out2", 4, 4, 16, [16] * 4)
    for c in range(F2T // KT):
        add(f"up2_{c}", 4, 4, 16, [16] * 4)
        add(f"dn2_{c}", 4, 4, 16, [16] * 4)
    return out


class Chain:

    def __init__(self, eng, sem, per, index):
        self.eng, self.sem, self.per, self.base, self.n = eng, sem, per, index * per, 0

    def __call__(self, ins):
        ins.then_inc(self.sem, 1)
        self.n += 1
        self.eng.wait_ge(self.sem, self.base + self.n)

    def end(self):
        assert self.n == self.per, (self.n, self.per)


def build(nc, dram, out):
    stages = make_stages()
    ST = {s.name: s for s in stages}
    pv_d, cs_d = dram["pv"], dram["cs"]
    xT_d = dram["xT"].rearrange("(k p) t -> p k t", p=P)
    out_d = out.rearrange("(k p) t -> p k t", p=P)
    bias_rows = nc.dram_tensor("bias_rows", [A_HEADS + B_HEADS, N_DIST], F32).ap()

    ctx = ExitStack()
    with ctx:
        def sb(name, shape, dt=F32):
            return ctx.enter_context(nc.sbuf_tensor(name, shape, dt))

        def sem(name):
            return ctx.enter_context(nc.semaphore(name))

        raw = sb("raw", [P, RAW_SLOTS, UNIT * P // 2])
        whi = sb("whi", [P, W_SLOTS, UNIT * P], F32R)
        wlo = sb("wlo", [P, W_SLOTS, UNIT * P], F32R)
        x = sb("x", [P, KT, T])
        y = sb("y", [P, KT, T])
        hS = sb("hS", [P, KT, 2 * T], F32R)
        aS = sb("aS", [P, KT, 2 * T], F32R)
        pv = sb("pv", [P, N_PV])
        cs = sb("cs", [P, N_CS])
        tab = sb("tab", [P, A_HEADS + B_HEADS + N_DIST])
        heads = sb("heads", [P, 5 * 2 * T])
        vN = sb("vN", [P, 5, 2, P])
        vT = sb("vT", [P, T])
        tmp = sb("tmp", [P, 2, T])
        bias5 = sb("bias5", [P, 5, T])
        sq = sb("sq", [P, 2 * T])
        sq2 = sb("sq2", [P, T])
        acc = sb("acc", [P, 2, T])
        rsb = sb("rsb", [P, 2, T])
        og = sb("og", [P, 2, T])
        ms = sb("ms", [P, 8])
        rs = sb("rs", [P, 8])
        ms5 = sb("ms5", [P, 5, 4])
        rs5 = sb("rs5", [P, 5, 4])
        nhalf = sb("nhalf", [P, 4])
        mx = sb("mx", [P, 5, 2])
        nm = sb("nm", [P, 5, 2])
        den = sb("den", [P, 5, 2])
        esk = sb("esk", [P, 2, 2])
        dsum = sb("dsum", [P, 5, 2])
        rden = sb("rden", [P, 5, 2])
        mjoin = sb("mjoin", [P, 2])
        nsink = sb("nsink", [P, N_SWA])
        carrier = sb("carrier", [P, 5])
        gqs = sb("gqs", [P, 2])

        def hb(i, n=T):
            return heads[:, i * T:i * T + n]

        q_swa, q_fox, k_fox, k_swa, r_swa, r_fox, l_fox, b_fox = (hb(i) for i in range(8))
        qk = [hb(2 * s, 2 * T) for s in range(5)]
        ub = [heads[:, i * 258:(i + 1) * 258] for i in range(4)]
        cv = [heads[:, 4 * 258 + i * T:4 * 258 + (i + 1) * T] for i in range(4)]
        yflat = y[:, :, :].rearrange("p k t -> p (k t)")
        probs = [yflat[:, s * 384:(s + 1) * 384] for s in range(5)]
        probsT = [yflat[:, (5 + s) * 384:(6 + s) * 384] for s in range(5)]
        ident = cs[:, CS["ident"]:CS["ident"] + P]
        ones = cs[:, CS["ones"]:CS["ones"] + P]
        triu = cs[:, CS["triu"]:CS["triu"] + P]

        def cst(name, n=1):
            return cs[:, CS[name]:CS[name] + n]

        def par(name, k=0, n=1):
            o = PV[name]
            if isinstance(k, int):
                return pv[:, o + k:o + k + n]
            return pv[:, bass.ds(k + o, n)]

        G = [ctx.enter_context(nc.psum_tensor(f"G{i}", [P, 512], F32)) for i in range(2)]
        SB = [ctx.enter_context(nc.psum_tensor(f"SB{i}", [P, 512], F32)) for i in range(5)]
        MB = ctx.enter_context(nc.psum_tensor("MB", [P, 512], F32))

        landed = [sem(f"landed{i}") for i in range(RAW_SLOTS)]
        hi_done, lo_done = sem("hi_done"), sem("lo_done")
        unit_used = sem("unit_used")
        mt_done = sem("mt_done")
        tmp_done = sem("tmp_done")
        ev_done = sem("ev_done")
        const_in, masks_in = sem("const_in"), sem("masks_in")
        x_in = [sem(f"x_in{j}") for j in range(4)]
        bias_in = [sem(f"bias_in{i}") for i in range(5)]
        prep = sem("prep")
        rows_in_sb, rows_out, rows_ps = sem("rows_in_sb"), sem("rows_out"), sem("rows_ps")
        bias_used = sem("bias_used")
        h_ready = sem("h_ready")
        a_ready = sem("a_ready")
        a_hi = sem("a_hi")
        h_hi = sem("h_hi")
        og_done = sem("og_done")
        nsq, nsum, nms, npow, nbc, ncopy = (sem(f"norm_{n}") for n in ("sq", "sum", "ms", "pow", "bc", "copy"))
        s_mm, s_exp, s_rden, s_norm, s_nm = sem("s_mm"), sem("s_exp"), sem("s_rden"), sem("s_norm"), sem("s_nm")
        t_mm, t_copy, o_mm, o_sq, o_acc = sem("t_mm"), sem("t_copy"), sem("o_mm"), sem("o_sq"), sem("o_acc")
        aug_done, v_mm, v_copy = sem("aug_done"), sem("v_mm"), sem("v_copy")
        smax_c, pre_c, z_c = sem("smax_c"), sem("pre_c"), sem("z_c")
        lf_mm, lf_copy, c_mm, c_done = sem("lf_mm"), sem("lf_copy"), sem("c_mm"), sem("c_done")
        S2, E2, R2, N2, T2, TC2, O2 = (sem(n) for n in ("S2", "E2", "R2", "N2", "T2", "TC2", "O2"))
        NM2, hn_sq, hn_mm, hn_v, hn_ms, hn_pow, hn_bc, hn_done = (
            sem(n) for n in ("NM2", "hn_sq", "hn_mm", "hn_v", "hn_ms", "hn_pow", "hn_bc", "hn_done"))
        A2c, B2c = sem("A2c"), sem("B2c")
        y_c, sqy, sqa, yg = sem("y_c"), sem("sqy"), sem("sqa"), sem("yg")
        u_c, gelu_done, u_used, u_done = sem("u_c"), sem("gelu_done"), sem("u_used"), sem("u_done")
        r_done = sem("r_done")
        sig_in, sig_done, mix_c = sem("sig_in"), sem("sig_done"), sem("mix_c")
        mixed_done = sem("mixed_done")
        x_c, bx = sem("x_c"), sem("bx")
        x_done = sem("x_done")
        stored = sem("stored")


        NORM_BEFORE = {"pre": (0,), "out1": (1, 2), "up1_0": (3, 4), "in2": (5, 6), "up2_0": (7,)}
        FILL = {"pre": 0, "up1_0": 1, "in2": 2, "out2": 3, "up2_0": 4}
        FILL_NORM = {0: 0, 1: 4, 2: 6, 4: 7}
        OG_BASE = {0: 0, 1: 2 * KT, 2: 3 * KT, 4: 4 * KT}
        ACC_DONE = {1: (o_acc, 16), 2: (o_acc, 16), 3: (sqa, KT), 5: (sqa, 2 * KT), 7: (sqa, 3 * KT)}
        AHI2 = 16 + A_SLOTS + B_HEADS
        GROUP = {"A": (0, (0, 1, 2)), "3": (1, (3,)), "4": (2, (4,))}
        ST_NOW = [None, None, None, None]
        r_half = sem("r_half")

        def tile_of(tensor, i):
            if isinstance(i, int):
                return tensor[:, i, :]
            return tensor[:, bass.ds(i, 1), :].rearrange("p a t -> p (a t)")

        def is_wide(st, it):
            return st.wide and isinstance(it, int) and it == 0

        def accumulator(st, it, p):
            return SB[p] if is_wide(st, it) and p in (2, 3) else G[st.bank(p)]

        def wait_x(eng, n, j):
            if n == 0:
                eng.wait_ge(x_in[j], 16)
            else:
                eng.wait_ge(bx, 8 * (n // 2 - 2) + 2 * j + 2)

        STEPS = {
            "in1": [("P1", 0, 2), ("P2", 1, 2), ("P3", 2, 2),
                    ("R0", 0, 0), ("S1", 0, 1), ("T0", 0, 1), ("V", 1, 1), ("D1", 1, 1), ("O0", 1, 1),
                    ("S0", 2, 0), ("T1", 2, 1), ("D0", 3, 0), ("R1", 3, 0), ("O1", 3, 1)],
            "in2": [("Q0", 2, 0), ("N0", 4, 0), ("Q1", 5, 0), ("B0", 5, 0), ("S0", 6, 0), ("N1", 7, 0),
                    ("Q2", 8, 0), ("B1", 8, 0), ("S1", 9, 0), ("N2", 10, 0), ("Q3", 11, 0),
                    ("B2", 11, 0), ("S2", 12, 0), ("DA", 13, 0), ("N3", 13, 0), ("B3", 14, 0), ("Q4", 14, 0), ("TA", 14, 0),
                    ("S3", 0, 1), ("OA", 0, 1), ("D3", 1, 1), ("N4", 1, 1), ("B4", 2, 1), ("T3", 2, 1),
                    ("O3", 3, 1), ("S4", 3, 1), ("D4", 4, 1), ("T4", 5, 1), ("O4", 6, 1)],
        }
        for _n in [s.name for s in stages if s.name.startswith("up")]:
            STEPS[_n] = [("F0", 1, 0), ("F1", 2, 0), ("G0", 2, 0), ("F2", 3, 0), ("M1", 3, 0),
                         ("F3", 0, 1), ("G2", 0, 1), ("M3", 1, 1)] if _n[2] == "1" else [
                             ("F0", 1, 0), ("F1", 2, 0), ("F2", 3, 0), ("F3", 0, 1)]
        STEPS["out1"] = [("Y0", 3, 0), ("Y1", 5, 0), ("Y2", 7, 0), ("Y3", 1, 1)]
        STEPS[f"dn1_{len(CHUNKS1) - 1}"] = STEPS["out2"] = [("Y0", 2, 0), ("Y1", 3, 0), ("Y2", 0, 1), ("Y3", 1, 1)]

        def run_stage(eng, st, step, mtile):
            steps = STEPS.get(st.name, [])
            wraps = any(w == 1 for _, _, w in steps)

            def body(it, first, last):
                for p in range(st.nm):
                    for name, pos, wrap in steps:
                        if pos == p and (wrap == 0 or (wrap == 1 and not first) or (wrap == 2 and first)):
                            step(name, it - 1 if wrap == 1 else it)
                    mtile(st, it, p, last)

            n = st.iters
            lo = 0
            if wraps or n == 1:
                body(0, True, n == 1)
                lo = 1
            if n - 1 > lo:
                with eng.Fori(lo, n - 1) as it:
                    body(it, False, False)
            if n > 1:
                body(n - 1, False, True)
            for name, pos, wrap in sorted(steps, key=lambda s: s[1]):
                if wrap == 1:
                    step(name, n - 1)

        block = ctx.enter_context(nc.Block())

        @block.sync
        def _(sp):
            for k in range(4):
                sp.dma_start(x[:, 4 * k:4 * k + 4, :], xT_d[:, 4 * k:4 * k + 4, :]).then_inc(x_in[k], 16)
            m0 = CS["causal"]
            sp.dma_start(cs[:, 0:m0], cs_d[:, 0:m0]).then_inc(const_in, 16)
            sp.dma_start(pv[:, :], pv_d).then_inc(const_in, 16)

            def load(st, it, k):
                for half in range(2):
                    h = 2 * st.u(it, k) + half
                    slot = (2 * (st.ubase + k) + half) % RAW_SLOTS
                    a, b = (0, st.half) if half == 0 else (st.half, st.blocks)
                    if not (isinstance(it, int) and 2 * st.u(it, k) + half < RAW_SLOTS):
                        sp.wait_ge(lo_done, h - (RAW_SLOTS - 1))
                    row = it * st.units + k
                    src = dram[st.name]
                    src = src[row] if isinstance(row, int) else src[bass.ds(row, 1)].rearrange("a p c -> (a p) c")
                    sp.dma_start(raw[:, slot, 0:(b - a) * P], src[:, a * P:b * P]).then_inc(landed[slot], 16)

            def load_bands(it, slots):
                for s in slots:
                    head = A_SLOTS * s + it if s < 3 else A_HEADS + 2 * it + s - 3
                    src = bass.AP(bias_rows.tensor, head * N_DIST, [[1, P], [1, T]])
                    sp.dma_start(bias5[:, s, :], src).then_inc(bias_in[s], 16)

            for st in stages:
                if st.name == "out1":
                    sp.wait_ge(rows_in_sb, 1)
                    sp.dma_start(bias_rows, bias5[0:A_HEADS + B_HEADS, :, :].rearrange(
                        "h a b -> h (a b)")[:, 0:N_DIST]).then_inc(rows_out, 16)
                    sp.wait_ge(rows_out, 16)

                def one(it):
                    if st.name == "in2":
                        if it:
                            sp.wait_ge(bias_used, 5 * (it - 1) + 3)
                        load_bands(it, range(3))
                    for k in range(st.units):
                        if st.name == "in2" and k == 10:
                            if it:
                                sp.wait_ge(bias_used, 5 * it)
                            load_bands(it, range(3, 5))
                        load(st, it, k)

                if st.iters == 1 or st.name == "in2":
                    for i in range(st.iters):
                        one(i)
                    if st.name == "pre":
                        sp.dma_start(cs[:, m0:], cs_d[:, m0:]).then_inc(masks_in, 16)
                        sp.dma_start(tab[:, :], dram["tab"]).then_inc(masks_in, 16)
                else:
                    with sp.Fori(0, st.iters) as it:
                        one(it)
            for m in range(KT):
                sp.wait_ge(x_done, m + 1)
                sp.dma_start(out_d[:, m, :], x[:, m, :]).then_inc(stored, 16)
            sp.wait_ge(stored, 16 * KT)

        FIRST_SPLITS = {0: 1, 3: 2}
        A_BASE = {"in1": 0}
        n_a = 2 * 8
        for c, n in enumerate(CHUNKS1):
            A_BASE[f"up1_{c}"] = n_a
            n_a += n
        A_BASE["in2"] = n_a
        n_a += A_SLOTS + B_HEADS
        for c in range(F2T // KT):
            A_BASE[f"up2_{c}"] = n_a
            n_a += KT
        last1, last2 = f"dn1_{len(CHUNKS1) - 1}", f"dn2_{F2T // KT - 1}"
        NORMS = [("x", D), (0, N_SWA * HD1), (1, N_FOX * HD1), (0, D), ("x", D), (0, D), ("x", D), (0, D)]
        NSQ = [4 * sum(1 for src, _ in NORMS[:n] if src == "x") for n in range(len(NORMS) + 1)]

        def w0(v):
            return not isinstance(v, int) or v > 0

        @block.tensor
        def _(pe):
            def mm(o, w, m, start, stop):
                return pe.matmul(o, w, m, start=start, stop=stop, skip_group_check=False)

            def wide_start(st):
                for p in range(2):
                    if st.g(0, p) > 1:
                        pe.wait_ge(ev_done, st.g(0, p) - 1)
                for kk in range(KT):
                    pe.wait_ge(h_ready, KT * FILL[st.name] + kk + 1)
                    act = hS[:, kk, :]
                    for p in range(WIDE):
                        flat = st.start[p] + kk
                        k, within = flat // st.blocks, flat % st.blocks
                        slot = (st.ubase + k) % W_SLOTS
                        if within in (0, st.half):
                            pe.wait_ge(lo_done, 2 * st.u(0, k) + (1 if within == 0 else 2))
                        bank = accumulator(st, 0, p)
                        h_w, l_w = (w[:, slot, within * P:(within + 1) * P] for w in (whi, wlo))
                        if kk < KT - 1:
                            one = mm(bank[:, :], h_w, act, kk == 0, False)
                            mm(bank[:, T:], l_w, act[:, 0:T], False, False)
                            if kk == 0 and p == 0 and st.prev:
                                one.then_inc(unit_used, 1)
                        else:
                            one = mm(bank[:, T:], l_w, act[:, 0:T], False, False)
                            mm(bank[:, :], h_w, act, False, True).then_inc(mt_done, 1)
                            if p:
                                one.then_inc(unit_used, 1)

            def mtile(st, it, p, last):
                if is_wide(st, it) and p < WIDE:
                    if p == 0:
                        wide_start(st)
                    return
                g = st.g(it, p)
                acc_bank = accumulator(st, it, p)
                X = aS if st.name in ("out1",) or st.name[:2] == "dn" or (st.name == "mix2" and p >= 2) else hS
                first_block = {("out1", 1): 8, ("mix2", 3): A_SLOTS}.get((st.name, p % 2 if st.name == "out1" else p), 0)
                f = g - st.free_after(p) + 1
                if w0(f) and not (is_wide(st, it) and p == WIDE):
                    pe.wait_ge(ev_done, f)
                n = st.mtiles[p]
                for kk in range(n):
                    flat = st.start[p] + kk
                    k, within = flat // st.blocks, flat % st.blocks
                    slot = (st.ubase + k) % W_SLOTS
                    if within in (0, st.half):
                        pe.wait_ge(lo_done, 2 * st.u(it, k) + (1 if within == 0 else 2))
                    if p == 0 and st.name in FILL and FILL[st.name] is not None:
                        pe.wait_ge(h_ready, KT * FILL[st.name] + kk + 1)
                    if st.name[:2] == "dn" and p == 0:
                        pe.wait_ge(a_ready, A_BASE["up" + st.name[2:]] + kk + 1)
                    if kk == 0 and (st.name, p) in (("out1", 0), ("mix2", 2)):
                        pe.wait_ge(a_ready, 16 if st.name == "out1" else A_BASE["in2"] + A_SLOTS + B_HEADS)
                    act = X[:, first_block + kk, :]
                    h_w, l_w = (w[:, slot, within * P:(within + 1) * P] for w in (whi, wlo))
                    if kk < n - 1:
                        one = mm(acc_bank[:, :], h_w, act, kk == 0, False)
                        mm(acc_bank[:, T:], l_w, act[:, 0:T], False, False)
                    else:
                        one = mm(acc_bank[:, T:], l_w, act[:, 0:T], False, False)
                        end = mm(acc_bank[:, :], h_w, act, False, True)
                        end.then_inc(mt_done, 1)
                    if kk == 0 and p == WIDE if is_wide(st, it) and k < W_SLOTS else within == 0 and (st.prev or k):
                        one.then_inc(unit_used, 1)

            def norm(n):
                src, _ = NORMS[n]
                if src == "x":
                    for t in range(KT):
                        if t % 4 == 0:
                            pe.wait_ge(nsq, NSQ[n] + t // 4 + 1)
                        for c in range(2):
                            end = mm(SB[2 * c][:, 0:1], y[:, t, c * P:(c + 1) * P], ones[:, 0:1], t == 0, t == KT - 1)
                else:
                    pe.wait_ge(*ACC_DONE[n])
                    for c in range(2):
                        end = mm(SB[2 * c][:, 0:1], acc[:, src, c * P:(c + 1) * P], ones[:, 0:1], True, True)
                end.then_inc(nsum, 1)
                pe.wait_ge(npow, n + 1)
                if n:
                    pe.wait_ge(ncopy, n)
                for c in range(2):
                    end = mm(SB[1][:, c * P:(c + 1) * P], rs[:, c:c + 1].to_broadcast([P, P]), ident, True, True)
                end.then_inc(nbc, 1)

            def scores(b, it):
                q = 2 * it + b
                pe.wait_ge(ev_done, ST["in1"].g(it, 0 if b == 0 else 2) + 1)
                pe.wait_ge(aug_done, q + 1)
                if w0(q - 1):
                    pe.wait_ge(t_copy, q - 1)
                qt, kt, lh, rh = (q_swa, k_swa, cst("lhs_swa", T), r_swa) if b == 0 else (q_fox, k_fox, l_fox, r_fox)
                for par_ in range(2):
                    at = slice(64 * par_, 64 * par_ + 64)
                    bank = SB[2 * b + par_]
                    for o, qs, nk in ((bank[:, 0:P], slice(0, P), P), (bank[:, P:P + T], slice(P, T), T)):
                        mm(o, qt[at, qs], kt[at, 0:nk], True, False)
                        end = mm(o, lh[at, qs], rh[at, 0:nk], False, True)
                end.then_inc(s_mm, 1)

            def turn(bank, pr):
                for a in range(3):
                    end = pe.transpose(bank[:, a * P:(a + 1) * P], pr[:, a * P:(a + 1) * P], ident)
                return end

            def step(name, it):
                if name == "P1":
                    pe.wait_ge(rows_in_sb, 1)
                    pe.wait_ge(ev_done, ST["pre"].g(0, 1) + 1)
                    for c in range(2):
                        end = pe.transpose(SB[4][:, c * P:(c + 1) * P], vT[:, c * P:(c + 1) * P], ident)
                    end.then_inc(v_mm, 1)
                elif name == "P2":
                    pe.wait_ge(z_c, 5)
                    pe.wait_ge(v_copy, 1)
                    for c in range(2):
                        end = pe.transpose(SB[4][:, c * P:(c + 1) * P], sq[:, T + c * P:T + (c + 1) * P], ident)
                    end.then_inc(lf_mm, 1)
                elif name == "P3":
                    pe.wait_ge(lf_copy, 1)
                    mm(SB[4][:, 0:P], og[:, 0, 0:P], triu, True, True)
                    mm(SB[4][:, P:T], og[:, 0, 0:P], ones, True, False)
                    mm(SB[4][:, P:T], og[:, 0, P:T], triu, False, True).then_inc(c_mm, 1)
                elif name in ("S0", "S1") and ST_NOW[0] == "in1":
                    scores(int(name[1]), it)
                elif name == "V":
                    pe.wait_ge(ev_done, ST["in1"].g(it, 3) + 1)
                    pe.wait_ge(c_done, 1)
                    pe.wait_ge(v_copy, it + 1)
                    for c in range(2):
                        end = pe.transpose(SB[4][:, c * P:(c + 1) * P], vT[:, c * P:(c + 1) * P], ident)
                    end.then_inc(v_mm, 1)
                elif name in ("T0", "T1"):
                    b = int(name[1])
                    pe.wait_ge(s_norm, 2 * it + b + 1)
                    for s in (2 * b, 2 * b + 1):
                        end = turn(SB[s], probs[s])
                    end.then_inc(t_mm, 1)
                elif name in ("O0", "O1"):
                    b = int(name[1])
                    q = 2 * it + b
                    pe.wait_ge(t_copy, q + 1)
                    pe.wait_ge(v_copy, 1 if b == 0 else it + 2)
                    if w0(q):
                        pe.wait_ge(o_sq, q)
                    for par_ in range(2):
                        at = slice(64 * par_, 64 * par_ + 64)
                        pt = probsT[2 * b + par_]
                        mm(MB[at, 0:T], vN[:, b, 0, at], pt[:, 0:T], True, False)
                        end = mm(MB[at, P:T], vN[:, b, 1, at], pt[:, T:T + P], False, True)
                    end.then_inc(o_mm, 1)
                elif name[0] == "N":
                    s = int(name[1])
                    h = 5 * it + s
                    pe.wait_ge(hn_sq, h + 1)
                    pe.wait_ge(ev_done, ST["in2"].g(it, 3 * s + 2) + 1)
                    if w0(it):
                        pe.wait_ge(TC2, 3 * (it - 1) + max(0, s - 2) + 1)
                    for c in range(4):
                        mm(SB[s][:, c:c + 1], sq[:, c * P:(c + 1) * P], ones[:, 0:1], True, True)
                    for c in range(2):
                        end = pe.transpose(SB[s][:, (1 + c) * P:(2 + c) * P], vT[:, c * P:(c + 1) * P], ident)
                    end.then_inc(hn_mm, 1)
                elif name[0] == "B":
                    s = int(name[1])
                    pe.wait_ge(hn_pow, 5 * it + s + 1)
                    for c in range(4):
                        end = mm(SB[s][:, c * P:(c + 1) * P], rs5[:, s, c:c + 1].to_broadcast([P, P]), ident, True, True)
                    end.then_inc(hn_bc, 1)
                elif name[0] == "S":
                    s = int(name[1])
                    pe.wait_ge(hn_done, 5 * it + s + 1)
                    mm(SB[s][:, 0:P], qk[s][:, 0:P], qk[s][:, T:T + P], True, True)
                    mm(SB[s][:, P:P + T], qk[s][:, P:T], qk[s][:, T:2 * T], True, True).then_inc(S2, 1)
                elif name[0] == "T":
                    b, ss = GROUP[name[1]]
                    pe.wait_ge(N2, 3 * it + b + 1)
                    for s in ss:
                        end = turn(SB[s], probs[s])
                    end.then_inc(T2, 1)
                elif name[0] == "O":
                    b, ss = GROUP[name[1]]
                    q = 3 * it + b
                    pe.wait_ge(TC2, q + 1)
                    pe.wait_ge(a_ready, A_BASE["in2"] + q)
                    for s in ss:
                        mm(MB[:, 0:T], vN[:, s, 0, :], probsT[s][:, 0:T], s == ss[0], False)
                        end = mm(MB[:, P:T], vN[:, s, 1, :], probsT[s][:, T:T + P], False, s == ss[-1])
                    end.then_inc(O2, 1)

            pe.wait_ge(const_in, 32)
            for st in stages:
                for n in NORM_BEFORE.get(st.name, ()):
                    norm(n)
                if st.name == "in1":
                    pe.wait_ge(masks_in, 32)
                    mm(SB[4][0:A_HEADS + B_HEADS, 0:N_DIST], tab[0:N_BUCKETS + 4, 0:A_HEADS + B_HEADS],
                       tab[0:N_BUCKETS + 4, A_HEADS + B_HEADS:], True, True).then_inc(rows_ps, 1)
                ST_NOW[0] = st.name
                run_stage(pe, st, step, mtile)

        @block.scalar
        def _(act):
            def split(st, it, k):
                slot = (st.ubase + k) % W_SLOTS
                u = st.u(it, k)
                if w0(u - W_SLOTS + 1) and not (isinstance(it, int) and u < W_SLOTS):
                    act.wait_ge(unit_used, u - W_SLOTS + 1)
                for half in range(2):
                    h0 = 2 * (st.ubase + k) + half
                    a, b = (0, st.half) if half == 0 else (st.half, st.blocks)
                    act.wait_ge(landed[h0 % RAW_SLOTS],
                                16 * (h0 // RAW_SLOTS + 1) + it * (16 * 2 * st.units // RAW_SLOTS))
                    act.activation(whi[:, slot, a * P:b * P], raw[:, h0 % RAW_SLOTS, 0:(b - a) * P],
                                   ACT.Copy).then_inc(hi_done, 1)

            def splits(st, it, p, last):
                for v in st.splits(p):
                    if v < st.units:
                        split(st, it, v)
                    elif not last:
                        split(st, it + 1, v - st.units)
                    elif st.next:
                        split(st.next, 0, v - st.units)

            def mtile(st, it, p, last):
                splits(st, it, p, last)
                g = st.g(it, p)
                act.wait_ge(mt_done, g + 1)
                if w0(g - 1):
                    act.wait_ge(ev_done, g - 1)
                scale = HD1 ** -0.5 if st.name == "in1" and p < 2 else 1.0
                act.activation(tmp[:, st.bank(p), :], accumulator(st, it, p)[:, T:], ACT.Copy, scale=scale).then_inc(tmp_done, 1)
                if st.name == "pre" and p == 2:
                    act.wait_ge(z_c, 1)
                    act.activation(sq2[:, :], sq2[:, :], ACT.Exp).then_inc(z_c, 1)
                    act.wait_ge(z_c, 2)
                    act.activation(sq2[:, :], sq2[:, :], ACT.Ln, bias=1.0).then_inc(z_c, 1)
                if st.name[:3] == "up2":
                    c = int(st.name[4])
                    i = KT * c + it * 4 + p
                    act.wait_ge(r_done, i + 1)
                    act.activation(tile_of(aS, it * 4 + p)[:, 0:T], cv[p], ACT.Copy).then_inc(a_hi, 1)
                if st.name == "mix2" and p < 2:
                    act.wait_ge(ev_done, g + 1)
                    act.activation(og[:, p, :], og[:, p, :], ACT.Sigmoid).then_inc(sig_done, 1)

            def exps(slots, nms_, wait):
                for s, m in zip(slots, nms_):
                    for n, cols in ((0, slice(0, P)), (1, slice(P, P + T))):
                        end = act.activation(probs[s][:, cols], probs[s][:, cols], ACT.Exp, bias=nm[:, m, n:n + 1],
                                             accum_out=den[:, s, n:n + 1])
                return end

            def scales(slots, nms_):
                for s, m in zip(slots, nms_):
                    for n, cols in ((0, slice(0, P)), (1, slice(P, P + T))):
                        end = act.activation(probs[s][:, cols], probs[s][:, cols], ACT.Copy, scale=rden[:, m, n:n + 1])
                return end

            def step(name, it):
                if name[0] == "Y":
                    stage = ST_NOW[1]
                    m = it * 4 + int(name[1])
                    i = m + KT * {"out1": 0, last1: 1, "out2": 2}[stage]
                    if stage == "out2":
                        act.wait_ge(x_c, m + 1)
                    else:
                        act.wait_ge(y_c, 3 * (m + 1) if stage == "out1" else m + (len(CHUNKS1) + 1) * KT + 1)
                    if w0(i):
                        act.wait_ge(sqa, i)
                    act.activation(sq2[:, :], tile_of(x if stage == "out2" else y, m), ACT.Square).then_inc(sqy, 1)
                    if stage != "out2":
                        act.activation(tile_of(y, m), tile_of(y, m), ACT.Copy,
                                       scale=par("post_mix" if stage == "out1" else "post_ffn", m)).then_inc(yg, 1)
                elif name == "P1":
                    act.wait_ge(v_mm, 1)
                    act.activation(vN[:, 0, :, :].rearrange("p a b -> p (a b)"), SB[4][:, 0:T], ACT.Copy).then_inc(v_copy, 1)
                elif name == "V":
                    act.wait_ge(v_mm, it + 2)
                    act.activation(vN[:, 1, :, :].rearrange("p a b -> p (a b)"), SB[4][:, 0:T], ACT.Copy).then_inc(v_copy, 1)
                elif ST_NOW[1] == "in1" and name[0] == "S":
                    b = int(name[1])
                    q = 2 * it + b
                    act.wait_ge(s_nm, q + 1)
                    if b == 0:
                        for j in range(2):
                            act.activation(esk[:, j, :], nm[:, j, :], ACT.Exp, bias=par("sinks", 8 * j + it))
                    exps((2 * b, 2 * b + 1), (2 * b, 2 * b + 1), None).then_inc(s_exp, 1)
                elif ST_NOW[1] == "in1" and name[0] == "D":
                    b = int(name[1])
                    act.wait_ge(s_rden, 2 * it + b + 1)
                    scales((2 * b, 2 * b + 1), (2 * b, 2 * b + 1)).then_inc(s_norm, 1)
                elif ST_NOW[1] == "in1" and name[0] == "O":
                    b = int(name[1])
                    q = 2 * it + b
                    act.wait_ge(og_done, KT + q + 1)
                    if w0(q):
                        act.wait_ge(o_acc, q)
                    act.activation(sq2[:, :], MB[:, 0:T], ACT.Square).then_inc(o_sq, 1)
                    act.activation(tile_of(aS, 8 * b + it)[:, 0:T], og[:, b, :], ACT.Copy).then_inc(a_hi, 1)
                elif name[0] == "G":
                    p = int(name[1])
                    c = int(ST_NOW[1][4])
                    i = 2 * sum(CHUNKS1[:c]) + it * 4 + p
                    act.wait_ge(u_c, 3 * i + 3)
                    act.activation(cv[p], cv[p], ACT.Gelu_apprx_tanh).then_inc(gelu_done, 1)
                elif name[0] == "Q":
                    s = int(name[1])
                    h = 5 * it + s
                    act.wait_ge(ev_done, ST["in2"].g(it, 3 * s + 1) + 1)
                    if w0(h):
                        act.wait_ge(hn_mm, h)
                    act.activation(sq[:, :], qk[s], ACT.Square).then_inc(hn_sq, 1)
                elif name[0] == "N":
                    s = int(name[1])
                    act.wait_ge(hn_mm, 5 * it + s + 1)
                    act.activation(vN[:, s, :, :].rearrange("p a b -> p (a b)"), SB[s][:, P:P + T], ACT.Copy).then_inc(hn_v, 1)
                elif name in ("S2", "S3", "S4"):
                    b, ss = GROUP["A" if name == "S2" else name[1]]
                    act.wait_ge(NM2, 3 * it + b + 1)
                    exps(ss, [ss[0]] * len(ss), None).then_inc(E2, 1)
                elif name[0] == "D":
                    b, ss = GROUP[name[1]]
                    act.wait_ge(R2, 3 * it + b + 1)
                    scales(ss, [ss[0]] * len(ss)).then_inc(N2, 1)
                elif name[0] == "O":
                    b, ss = GROUP[name[1]]
                    act.wait_ge(O2, 3 * it + b + 1)
                    act.activation(tile_of(aS, it if b == 0 else A_SLOTS + 2 * it + b - 1)[:, 0:T], MB[:, 0:T],
                                   ACT.Copy).then_inc(a_hi, 1)

            def norm(n):
                src, _ = NORMS[n]
                if src == "x":
                    for j in range(4):
                        wait_x(act, n, j)
                        act.activation(y[:, 4 * j:4 * j + 4, :], x[:, 4 * j:4 * j + 4, :], ACT.Square).then_inc(nsq, 1)
                if n == 0:
                    split(stages[0], 0, 0)
                act.wait_ge(nbc, n + 1)
                act.activation(rsb[:, src if n in (1, 2) else 0, :], SB[1][:, 0:T], ACT.Copy).then_inc(ncopy, 1)

            def fill(f):
                for t in range(KT):
                    if f == 0 and t in FIRST_SPLITS:
                        split(stages[0], 0, FIRST_SPLITS[t])
                    if f == 3:
                        act.wait_ge(mixed_done, t + 1)
                        src = y[:, t, :]
                    else:
                        act.wait_ge(og_done, OG_BASE[f] + t + 1)
                        src = og[:, t % 2, :]
                    act.activation(hS[:, t, 0:T], src, ACT.Copy).then_inc(h_hi, 1)

            for st in stages:
                for n in NORM_BEFORE.get(st.name, ()):
                    norm(n)
                if FILL.get(st.name) is not None:
                    fill(FILL[st.name])
                if st.name == "in1":
                    act.wait_ge(rows_ps, 1)
                    act.activation(bias5[0:A_HEADS + B_HEADS, :, :].rearrange("h a b -> h (a b)")[:, 0:N_DIST],
                                   SB[4][0:A_HEADS + B_HEADS, 0:N_DIST], ACT.Copy).then_inc(rows_in_sb, 1)
                ST_NOW[1] = st.name
                run_stage(act, st, step, mtile)

        @block.vector
        def _(dve):
            def split(st, it, k):
                slot = (st.ubase + k) % W_SLOTS
                for half in range(2):
                    h0 = 2 * (st.ubase + k) + half
                    a, b = (0, st.half) if half == 0 else (st.half, st.blocks)
                    dve.wait_ge(hi_done, 2 * st.u(it, k) + half + 1)
                    dve.tensor_tensor(wlo[:, slot, a * P:b * P], raw[:, h0 % RAW_SLOTS, 0:(b - a) * P],
                                      whi[:, slot, a * P:b * P].bitcast(F32), ALU.subtract).then_inc(lo_done, 1)

            def splits(st, it, p, last):
                for v in st.splits(p):
                    if v < st.units:
                        split(st, it, v)
                    elif not last:
                        split(st, it + 1, v - st.units)
                    elif st.next:
                        split(st.next, 0, v - st.units)

            def mtile(st, it, p, last):
                splits(st, it, p, last)
                g = st.g(it, p)
                A = accumulator(st, it, p)[:, 0:T]
                B = tmp[:, st.bank(p), :]
                dve.wait_ge(tmp_done, g + 1)

                def add_to(dest):
                    dve.tensor_tensor(dest, A, B, ALU.add).then_inc(ev_done, 1)

                def self_wait():
                    dve.wait_ge(ev_done, g + 1)

                name = st.name
                if name == "pre":
                    if p < 2:
                        add_to((k_swa, vT[:, :])[p])
                    else:
                        z, lf = sq[:, 0:T], sq[:, T:2 * T]
                        dve.scalar_tensor_tensor(z, A, par("bf"), B, ALU.add, ALU.add).then_inc(ev_done, 1)
                        self_wait()
                        dve.scalar_tensor_tensor(sq2[:, :], z, -1.0, z, ALU.mult, ALU.min).then_inc(z_c, 1)
                        dve.wait_ge(z_c, 3)
                        dve.scalar_tensor_tensor(lf, z, 0.0, sq2[:, :], ALU.min, ALU.subtract).then_inc(z_c, 1)
                        dve.wait_ge(z_c, 4)
                        dve.tensor_scalar(lf, lf, cst("sgn"), None, ALU.mult).then_inc(z_c, 1)
                elif name == "in1":
                    if p < 2:
                        dve.scalar_tensor_tensor((q_swa, q_fox)[p], A, HD1 ** -0.5, B, ALU.mult, ALU.add).then_inc(ev_done, 1)
                    else:
                        add_to((k_fox, vT[:, :])[p - 2])
                elif name == "out1":
                    half = og[:, p % 2, :]
                    add_to(half)
                    self_wait()
                    m = it * 4 + p // 2
                    c = Chain(dve, y_c, 3, m)
                    c.n = p % 2
                    c(dve.tensor_tensor(half, half, rsb[:, p % 2, :], ALU.mult))
                    if p % 2:
                        c(dve.tensor_tensor(tile_of(y, m), og[:, 0, :], og[:, 1, :], ALU.add))
                        c.end()
                elif name[:3] == "up1":
                    add_to(ub[p][:, 2:2 + T])
                elif name[:3] == "dn1":
                    c = int(name[4])
                    m = it * 4 + p
                    if c == 0:
                        add_to(tile_of(y, m))
                    else:
                        add_to(og[:, p % 2, :])
                        self_wait()
                        i = 3 * KT + (c - 1) * KT + m
                        dve.tensor_tensor(tile_of(y, m), tile_of(y, m), og[:, p % 2, :], ALU.add).then_inc(y_c, 1)
                elif name == "in2":
                    s, part = divmod(p, 3)
                    add_to((qk[s][:, 0:T], qk[s][:, T:2 * T], vT[:, :])[part])
                elif name == "mix2":
                    if p < 2:
                        add_to(og[:, p, :])
                    else:
                        br = sq[:, (p - 2) * T:(p - 1) * T]
                        add_to(br)
                        self_wait()
                        dve.wait_ge(sig_done, 2 * it + p - 1)
                        c = Chain(dve, mix_c, 2, it)
                        c.n = p - 2
                        c(dve.tensor_tensor(br, br, og[:, p - 2, :], ALU.mult))
                        if p == 3:
                            dve.tensor_tensor(tile_of(y, it), sq[:, 0:T], sq[:, T:2 * T], ALU.add).then_inc(mixed_done, 1)
                elif name == "out2" or name[:3] == "dn2":
                    m = it * 4 + p
                    add_to(og[:, p % 2, :])
                    self_wait()
                    dve.tensor_tensor(tile_of(x, m), tile_of(x, m), og[:, p % 2, :], ALU.add).then_inc(
                        x_done if name == last2 else x_c, 1)
                elif name[:3] == "up2":
                    add_to(ub[p][:, 0:T])
                    self_wait()
                    dve.scalar_tensor_tensor(cv[p], ub[p][:, 0:T], 0.0, ub[p][:, 0:T], ALU.max, ALU.mult).then_inc(r_done, 1)

            def carry_waits(i):
                dve.memset(carrier[:, i:i + 1], 0.0)

            def logits(s, mask, bank):
                for n, o, m in ((0, slice(0, P), mask[:, P:T]), (1, slice(P, P + T), mask[:, 0:T])):
                    end = dve.tensor_tensor_reduce(probs[s][:, o], bank[:, o], m, 1.0, LOWEST, ALU.add, ALU.max,
                                                   mx[:, s, n:n + 1])
                return end

            def step(name, it):
                st = ST_NOW[2]
                if name == "P2":
                    dve.wait_ge(lf_mm, 1)
                    dve.tensor_copy(og[:, 0, :], SB[4][:, 0:T]).then_inc(lf_copy, 1)
                elif name == "P3":
                    dve.wait_ge(c_mm, 1)
                    dve.tensor_scalar(l_fox, SB[4][:, 0:T], cst("mA"), cst("cA"), ALU.mult, ALU.add)
                    dve.tensor_scalar(b_fox, SB[4][:, 0:T], cst("mB"), cst("cB"), ALU.mult, ALU.add).then_inc(c_done, 1)
                elif name == "R0":
                    o = CS["slope"]
                    col = cs[:, o + it:o + it + 1] if isinstance(it, int) else cs[:, bass.ds(it + o, 1)]
                    dve.tensor_scalar(r_swa, cst("rhs_swa", T), col, None, ALU.mult).then_inc(aug_done, 1)
                elif name == "R1":
                    o = CS["pick"]
                    col = cs[:, o + it:o + it + 1] if isinstance(it, int) else cs[:, bass.ds(it + o, 1)]
                    if isinstance(it, int) and it == 0:
                        dve.wait_ge(c_done, 1)
                    dve.tensor_scalar(r_fox, b_fox, col, None, ALU.mult).then_inc(aug_done, 1)
                elif st == "in1" and name[0] == "S":
                    b = int(name[1])
                    q = 2 * it + b
                    dve.wait_ge(s_mm, q + 1)
                    carry_waits(b)
                    mask = cst("window" if b == 0 else "causal", T)
                    c = Chain(dve, smax_c, 1, q)
                    logits(2 * b, mask, SB[2 * b])
                    c(logits(2 * b + 1, mask, SB[2 * b + 1]))
                    c.end()
                    for s in (2 * b, 2 * b + 1):
                        if b == 0:
                            k = 8 * s + it
                            ns = nsink[:, k:k + 1] if isinstance(k, int) else nsink[:, bass.ds(k, 1)]
                            end = dve.tensor_scalar(nm[:, s, :], mx[:, s, :], -1.0, ns, ALU.mult, ALU.min)
                        else:
                            end = dve.tensor_scalar(nm[:, s, :], mx[:, s, :], -1.0, None, ALU.mult)
                    end.then_inc(s_nm, 1)
                elif st == "in1" and name[0] == "D":
                    b = int(name[1])
                    q = 2 * it + b
                    ss = slice(2 * b, 2 * b + 2)
                    dve.wait_ge(s_exp, q + 1)
                    src = den
                    if b == 0:
                        dve.tensor_tensor(dsum[:, ss, :], den[:, ss, :], esk[:, :, :], ALU.add).then_inc(pre_c, 1)
                        dve.wait_ge(pre_c, it + 1)
                        src = dsum
                    dve.reciprocal(rden[:, ss, :], src[:, ss, :]).then_inc(s_rden, 1)
                elif name in ("T0", "T1"):
                    b = int(name[1])
                    dve.wait_ge(t_mm, 2 * it + b + 1)
                    dve.tensor_copy(probsT[2 * b], SB[2 * b][:, 0:384])
                    dve.tensor_copy(probsT[2 * b + 1], SB[2 * b + 1][:, 0:384]).then_inc(t_copy, 1)
                elif name in ("O0", "O1"):
                    b = int(name[1])
                    q = 2 * it + b
                    dve.wait_ge(o_mm, q + 1)
                    dve.tensor_scalar(og[:, b, :], MB[:, 0:T], par("grp", 8 * b + it), None, ALU.mult).then_inc(og_done, 1)
                    dve.wait_ge(o_sq, q + 1)
                    dve.tensor_tensor(acc[:, b, :], acc[:, b, :], sq2[:, :], ALU.add).then_inc(o_acc, 1)
                    dve.wait_ge(a_hi, q + 1)
                    dst = tile_of(aS, 8 * b + it)
                    dve.tensor_tensor(dst[:, T:], og[:, b, :], dst[:, 0:T].bitcast(F32), ALU.subtract).then_inc(a_ready, 1)
                elif name[0] == "F" and st[:3] == "up1":
                    p = int(name[1])
                    c0 = int(st[4])
                    first = 2 * sum(CHUNKS1[:c0])
                    i = first + it * 4 + p
                    c = Chain(dve, u_c, 3, i)

                    def w(k):
                        return par("conv", (it * 4 + (first + p)) * 4 + k)

                    n_used = sum(CHUNKS1[:c0]) + it * 2 + p // 2 - 1
                    if w0(n_used):
                        dve.wait_ge(u_used, n_used)
                    dve.wait_ge(ev_done, ST[st].g(it, p) + 1)
                    c(dve.tensor_scalar(cv[p], ub[p][:, 0:T], w(0), w(3), ALU.mult, ALU.add))
                    c(dve.scalar_tensor_tensor(cv[p], ub[p][:, 1:1 + T], w(1), cv[p], ALU.mult, ALU.add))
                    c(dve.scalar_tensor_tensor(cv[p], ub[p][:, 2:2 + T], w(2), cv[p], ALU.mult, ALU.add))
                    c.end()
                elif name[0] == "F":
                    p = int(name[1])
                    i = KT * int(st[4]) + it * 4 + p
                    dst = tile_of(aS, it * 4 + p)
                    dve.wait_ge(a_hi, AHI2 + i + 1)
                    dve.tensor_tensor(dst[:, T:], cv[p], dst[:, 0:T].bitcast(F32), ALU.subtract).then_inc(a_ready, 1)
                elif name[0] == "N":
                    s = int(name[1])
                    h = 5 * it + s
                    dve.wait_ge(hn_v, h + 1)
                    dve.tensor_scalar(ms5[:, s, :], SB[s][:, 0:4], 1.0 / HD2, EPS, ALU.mult, ALU.add).then_inc(hn_ms, 1)
                elif name[0] == "B":
                    s = int(name[1])
                    dve.wait_ge(hn_bc, 5 * it + s + 1)
                    gq, gk = (gqs[:, 0:1], par("ka")) if s < 3 else (gqs[:, 1:2], par("kb"))
                    dve.scalar_tensor_tensor(qk[s][:, 0:T], qk[s][:, 0:T], gq, SB[s][:, 0:T], ALU.mult, ALU.mult)
                    dve.scalar_tensor_tensor(qk[s][:, T:], qk[s][:, T:], gk, SB[s][:, T:], ALU.mult, ALU.mult).then_inc(hn_done, 1)
                elif name[0] == "S":
                    s = int(name[1])
                    h = 5 * it + s
                    dve.wait_ge(S2, h + 1)
                    dve.wait_ge(bias_in[s], 16 * it + 16)
                    carry_waits(s)
                    logits(s, bias5[:, s, ::-1], SB[s]).then_inc(bias_used, 1)
                    if s >= 2:
                        b, ss = GROUP["A" if s == 2 else str(s)]
                        q = 3 * it + b
                        dve.wait_ge(bias_used, h + 1)
                        src = mx[:, s, :]
                        if s == 2:
                            dve.tensor_reduce(mjoin[:, :], mx[:, 0:3, :].rearrange("p s n -> p n s"), AX.X, ALU.max).then_inc(A2c, 1)
                            dve.wait_ge(A2c, 2 * it + 1)
                            src = mjoin[:, :]
                        dve.tensor_scalar(nm[:, ss[0], :], src, -1.0, None, ALU.mult).then_inc(NM2, 1)
                elif name[0] == "D":
                    b, ss = GROUP[name[1]]
                    q = 3 * it + b
                    dve.wait_ge(E2, q + 1)
                    src = den[:, ss[0], :]
                    if b == 0:
                        dve.tensor_reduce(dsum[:, 0, :], den[:, 0:3, :].rearrange("p s n -> p n s"), AX.X, ALU.add).then_inc(A2c, 1)
                        dve.wait_ge(A2c, 2 * it + 2)
                        src = dsum[:, 0, :]
                    dve.reciprocal(rden[:, ss[0], :], src).then_inc(R2, 1)
                elif name[0] == "T":
                    b, ss = GROUP[name[1]]
                    dve.wait_ge(T2, 3 * it + b + 1)
                    for s in ss:
                        end = dve.tensor_copy(probsT[s], SB[s][:, 0:384])
                    end.then_inc(TC2, 1)
                elif name[0] == "O":
                    b, ss = GROUP[name[1]]
                    q = 3 * it + b
                    dst = tile_of(aS, it if b == 0 else A_SLOTS + 2 * it + b - 1)
                    dve.wait_ge(a_hi, KT + q + 1)
                    dve.tensor_tensor(dst[:, T:], MB[:, 0:T], dst[:, 0:T].bitcast(F32), ALU.subtract).then_inc(a_ready, 1)

            def norm(n):
                src, width = NORMS[n]
                if n in (4, 6):
                    dve.wait_ge(ncopy, n)
                    dve.wait_ge(yg, KT * (n // 2 - 1))
                    i = n // 2 - 2
                    c = Chain(dve, bx, 8, i)
                    for j in range(4):
                        tiles = slice(4 * j, 4 * j + 4)
                        r = rsb[:, 0:1, :].to_broadcast([P, 4, T])
                        c(dve.tensor_tensor(y[:, tiles, :], y[:, tiles, :], r, ALU.mult))
                        c(dve.tensor_tensor(x[:, tiles, :], x[:, tiles, :], y[:, tiles, :], ALU.add))
                    c.end()
                dve.wait_ge(nsum, n + 1)
                for c in range(2):
                    end = dve.tensor_scalar(ms[:, c:c + 1], SB[2 * c][:, 0:1], 1.0 / width, EPS, ALU.mult, ALU.add)
                end.then_inc(nms, 1)

            def fill(f):
                gain = {0: "pre_mix", 1: "pre_ffn", 2: "g_mix2", 4: "g_mlp2"}.get(f)
                if gain:
                    dve.wait_ge(ncopy, FILL_NORM[f] + 1)

                def scaled(t):
                    if t > 1:
                        dve.wait_ge(h_hi, KT * f + t - 1)
                        dve.wait_ge(h_ready, KT * f + t - 1)
                    dve.scalar_tensor_tensor(og[:, t % 2, :], x[:, t, :], par(gain, t), rsb[:, 0, :], ALU.mult,
                                             ALU.mult).then_inc(og_done, 1)

                if gain:
                    scaled(0)
                for t in range(KT):
                    if f == 0 and t in FIRST_SPLITS:
                        split(stages[0], 0, FIRST_SPLITS[t])
                    if gain and t + 1 < KT:
                        scaled(t + 1)
                    dve.wait_ge(h_hi, KT * f + t + 1)
                    if gain:
                        dve.wait_ge(og_done, OG_BASE[f] + t + 1)
                    src = og[:, t % 2, :] if gain else y[:, t, :]
                    dve.tensor_tensor(hS[:, t, T:], src, hS[:, t, 0:T].bitcast(F32), ALU.subtract).then_inc(h_ready, 1)

            dve.wait_ge(const_in, 32)
            dve.tensor_scalar(nsink[:, :], par("sinks", 0, N_SWA), -1.0, None, ALU.mult)
            dve.tensor_scalar(gqs[:, 0:1], par("qa"), HD2 ** -0.5, None, ALU.mult)
            dve.tensor_scalar(gqs[:, 1:2], par("qb"), HD2 ** -0.5, None, ALU.mult)
            dve.memset(acc[:, :, :], 0.0).then_inc(prep, 1)
            dve.wait_ge(prep, 1)
            n_memset = 1
            for st in stages:
                for n in NORM_BEFORE.get(st.name, ()):
                    norm(n)
                if st.name == "pre":
                    split(st, 0, 0)
                if st.name == "in1":
                    dve.wait_ge(masks_in, 32)
                if FILL.get(st.name) is not None:
                    fill(FILL[st.name])
                if st.name in ("out1", last1, "out2"):
                    dve.wait_ge(nsum, {"out1": 3, last1: 4, "out2": 6}[st.name])
                    if st.name == "out1":
                        dve.wait_ge(ncopy, 3)
                    n_memset += 1
                    dve.memset(acc[:, 0, :], 0.0).then_inc(prep, 1)
                    dve.wait_ge(prep, n_memset)
                if st.name == "up1_0":
                    for i in range(4):
                        end = dve.memset(ub[i][:, 0:2], 0.0)
                    n_memset += 1
                    end.then_inc(prep, 1)
                    dve.wait_ge(prep, n_memset)
                ST_NOW[2] = st.name
                run_stage(dve, st, step, mtile)

        @block.gpsimd
        def _(pool):
            pool.memset(nhalf[:, :], -0.5).then_inc(r_half, 1)
            pool.wait_ge(r_half, 1)

            def mtile(st, it, p, last):
                pass

            def step(name, it):
                st = ST_NOW[3]
                if st == "in2":
                    if name[0] == "N":
                        s = int(name[1])
                        pool.wait_ge(hn_ms, it * 5 + (s + 1))
                        pool.tensor_tensor(rs5[:, s, :], ms5[:, s, :], nhalf[:, 0:4], ALU.pow).then_inc(hn_pow, 1)
                elif name[0] == "Y":
                    i = it * 4 + (int(name[1]) + KT * {"out1": 0, last1: 1, "out2": 2}[st])
                    pool.wait_ge(sqy, i + 1)
                    if w0(i):
                        pool.wait_ge(sqa, i)
                    pool.tensor_tensor(acc[:, 0, :], acc[:, 0, :], sq2[:, :], ALU.add).then_inc(sqa, 1)
                elif name[0] == "M":
                    p = int(name[1])
                    c0 = int(st[4])
                    j = sum(CHUNKS1[:c0]) + it * 2 + p // 2
                    dst = tile_of(aS, it * 2 + p // 2)
                    o = og[:, p // 2, :]
                    pool.wait_ge(gelu_done, j + 1)
                    pool.wait_ge(u_c, 3 * (2 * j + 2))
                    pool.tensor_tensor(o, cv[p - 1], cv[p], ALU.mult).then_inc(u_used, 1)
                    pool.wait_ge(u_used, j + 1)
                    pool.tensor_copy(dst[:, 0:T], o).then_inc(u_done, 1)
                    pool.wait_ge(u_done, j + 1)
                    pool.tensor_tensor(dst[:, T:], o, dst[:, 0:T].bitcast(F32), ALU.subtract).then_inc(a_ready, 1)

            for st in stages:
                for n in NORM_BEFORE.get(st.name, ()):
                    pool.wait_ge(nms, n + 1)
                    pool.tensor_tensor(rs[:, 0:2], ms[:, 0:2], nhalf[:, 0:2], ALU.pow).then_inc(npow, 1)
                ST_NOW[3] = st.name
                if st.name in ("out1", last1, "in2", "out2") or st.name[:3] == "up1":
                    run_stage(pool, st, step, mtile)


def rel_bucket(d):
    exact = N_BUCKETS // 2
    df = np.maximum(d, 1).astype(np.float32)
    large = exact + (np.log(df / np.float32(exact)) / np.float32(np.log(MAX_DISTANCE / exact))
                     * np.float32(N_BUCKETS - exact)).astype(np.int32)
    return np.where(d < exact, d, np.minimum(large, N_BUCKETS - 1))


def constants():
    c = np.zeros((P, N_CS), np.float32)
    p = np.arange(P)
    row = p % 64
    c[:, CS["ident"]:CS["ident"] + P] = np.eye(P)
    c[:, CS["ones"]:CS["ones"] + P] = 1
    c[:, CS["triu"]:CS["triu"] + P] = p[:, None] <= p[None, :]
    t, j = p[:, None], np.arange(T)[None, :]
    dist = P + t - j
    c[:, CS["causal"]:CS["causal"] + T] = np.where(dist >= 0, 0, -BIG)
    c[:, CS["window"]:CS["window"] + T] = np.where((dist >= 0) & (dist < WINDOW), 0, -BIG)
    s = np.arange(T)
    slopes = 2.0 ** (-8.0 * np.arange(1, N_SWA + 1) / N_SWA)
    for half in range(2):
        r = 64 * half
        c[r, CS["lhs_swa"]:CS["lhs_swa"] + T] = s
        c[r + 1, CS["lhs_swa"]:CS["lhs_swa"] + T] = 1
        c[r, CS["rhs_swa"]:CS["rhs_swa"] + T] = 1
        c[r + 1, CS["rhs_swa"]:CS["rhs_swa"] + T] = -s
        for i in range(8):
            c[r:r + 2, CS["slope"] + i] = -slopes[8 * half + i]
            for q in (0, 32):
                c[r + q + 2 * i + half, CS["pick"] + i] = 1
    c[:, CS["mA"]] = (row >= 32) & (row < 48)
    c[:, CS["cA"]] = row < 16
    c[:, CS["mB"]] = row < 16
    c[:, CS["cB"]] = (row >= 32) & (row < 48)
    c[:, CS["sgn"]] = np.where(row < 16, -1.0, np.where((row >= 32) & (row < 48), 1.0, 0.0))
    return c


def distance_rows():
    dist = np.arange(N_DIST) - (P - 1)
    out = np.zeros((N_BUCKETS + 4, N_DIST), np.float32)
    ok = dist >= 0
    out[rel_bucket(np.maximum(dist, 0))[ok], np.arange(N_DIST)[ok]] = 1
    for g, (window, r) in enumerate(GROUPS):
        out[N_BUCKETS + g] = np.where(ok & (dist % r == 0) & (dist <= window), 0, -BIG)
    out[N_BUCKETS + 3] = np.where(ok, 0, -BIG)
    return out


def group_rows():
    out = np.zeros((4, A_HEADS + B_HEADS), np.float32)
    for h in range(A_HEADS + B_HEADS):
        out[min(h // A_SLOTS, 3), h] = 1
    return out


def as_units(parts, blocks):
    b = np.concatenate([w.reshape(-1, P, P) for w in parts])
    return np.ascontiguousarray(b.reshape(-1, blocks, P, P).transpose(0, 2, 1, 3)).reshape(-1, P, blocks * P)


def cols(w, i):
    return w[:, i * P:(i + 1) * P]


def swa_tile(j):
    return np.concatenate([np.arange(HD1) + HD1 * j, np.arange(HD1) + HD1 * (8 + j)])


def lay_out(a):
    w_in, w_out, w_up, w_down = (np.asarray(a[n])[0] for n in ("w_in", "w_out", "w_up", "w_down"))
    o_k = N_SWA * HD1
    o_v = o_k + N_KV * HD1
    o_qf = o_v + N_KV * HD1
    o_kf, o_vf, o_f = o_qf + N_FOX * HD1, o_qf + 2 * N_FOX * HD1, o_qf + 3 * N_FOX * HD1
    gate_cols = np.zeros((D, P), np.float32)
    b_f = np.zeros((P, 1), np.float32)
    for r in (0, 32, 64, 96):
        gate_cols[:, r:r + N_FOX] = w_in[:, o_f:]
        b_f[r:r + N_FOX, 0] = np.asarray(a["b_forget"])[0]
    d = {"pre": as_units([w_in[:, o_k:o_v], w_in[:, o_v:o_qf], gate_cols], 16)}
    d["in1"] = as_units([w for j in range(8) for w in (
        w_in[:, swa_tile(j)], cols(w_in[:, o_qf:], j), cols(w_in[:, o_kf:], j), cols(w_in[:, o_vf:], j))], 16)
    rows = np.concatenate([swa_tile(j) for j in range(8)] + [np.arange(o_k, D)])
    wo = w_out[rows]
    d["out1"] = as_units([cols(wo, m) for m in range(KT)], 16)
    at = 0
    for c, n in enumerate(CHUNKS1):
        d[f"up1_{c}"] = as_units([cols(w_up, i + half * F1T) for i in range(at, at + n) for half in range(2)], 16)
        d[f"dn1_{c}"] = as_units([cols(w_down[at * P:(at + n) * P], m) for m in range(KT)], n)
        at += n
    w2 = np.asarray(a["w_in_2"])
    o_b = 3 * A_HEADS * HD2
    o_ga = o_b + 3 * B_HEADS * HD2
    o_gb = o_ga + D
    d["in2"] = as_units([cols(w2, part * A_HEADS + A_SLOTS * g + i) if g < 3
                         else cols(w2[:, o_b:], part * B_HEADS + 2 * i + g - 3)
                         for i in range(A_SLOTS) for g in range(5) for part in range(3)], 15)
    wa, wb = np.asarray(a["w_branch_a_2"]), np.asarray(a["w_branch_b_2"])
    d["mix2"] = as_units([w for m in range(KT) for w in (
        cols(w2[:, o_ga:], m), cols(w2[:, o_gb:], m), cols(wa, m), cols(wb, m))], 11)
    w_out2, w_up2, w_down2 = (np.asarray(a[n]) for n in ("w_out_2", "w_up_2", "w_down_2"))
    d["out2"] = as_units([cols(w_out2, m) for m in range(KT)], 16)
    for c in range(F2T // KT):
        d[f"up2_{c}"] = as_units([cols(w_up2, c * KT + i) for i in range(KT)], 16)
        d[f"dn2_{c}"] = as_units([cols(w_down2[c * D:(c + 1) * D], m) for m in range(KT)], 16)

    def tiles(v):
        return np.asarray(v).reshape(-1, P).T

    grp = np.concatenate([np.asarray(a["grp_swa_g"])[0], np.asarray(a["grp_fox_g"])[0]])[rows]
    conv = np.concatenate([np.asarray(a["conv_w"])[0], np.asarray(a["conv_b"])])
    conv = conv.reshape(4, 2, F1T, P).transpose(3, 2, 1, 0).reshape(P, -1)
    d["pv"] = np.ascontiguousarray(np.concatenate([
        tiles(a["pre_mix_g"]), tiles(grp), tiles(a["post_mix_g"]), tiles(a["pre_ffn_g"]), tiles(a["post_ffn_g"]),
        tiles(a["g_mix_2"]), tiles(a["g_mlp_2"]), tiles(a["q_norm_a_2"]), tiles(a["k_norm_a_2"]),
        tiles(a["q_norm_b_2"]), tiles(a["k_norm_b_2"]), b_f,
        np.broadcast_to(np.asarray(a["sinks"]), (P, N_SWA)), conv], axis=1))
    d["cs"] = constants()
    tab = np.zeros((P, A_HEADS + B_HEADS + N_DIST), np.float32)
    tab[:N_BUCKETS, :A_HEADS + B_HEADS] = np.asarray(a["rel_bias_2"])
    tab[N_BUCKETS:N_BUCKETS + 4, :A_HEADS + B_HEADS] = group_rows()
    tab[:N_BUCKETS + 4, A_HEADS + B_HEADS:] = distance_rows()
    d["tab"] = tab
    d["xT"] = np.ascontiguousarray(np.asarray(a["x"])[0].T)
    return d


def kernel(**inputs):
    import concourse.bacc as bacc
    from concourse.bass_utils import run_bass_kernel_spmd

    nc = bacc.Bacc("TRN2", target_bir_lowering=False, num_devices=1, dynamic_dma_scratch_size=1024)
    arrays = lay_out(inputs)
    dram = {n: nc.dram_tensor(f"in_{n}", v.shape, F32, kind="ExternalInput").ap() for n, v in arrays.items()}
    out = nc.dram_tensor("out_T", (D, T), F32, kind="ExternalOutput").ap()
    build(nc, dram, out)
    r = run_bass_kernel_spmd(nc, [{f"in_{n}": v for n, v in arrays.items()}], core_ids=[0])
    return np.ascontiguousarray(r.results[0]["out_T"].T)[None]
```

```python
from contextlib import ExitStack

import numpy as np

import concourse.bass as bass
from concourse import mybir

F32 = mybir.dt.float32
F32R = mybir.dt.float32r
ALU = mybir.AluOpType
ACT = mybir.ActivationFunctionType
AX = mybir.AxisListType

P = 128
T = 256
D = 2048
KT = D // P
EPS = 1e-6
BIG = 1e30
LOWEST = -3e38

HD1 = 64
N_SWA = 16
N_KV = 2
N_FOX = 16
WINDOW = 128
FF1 = 5632
F1T = FF1 // P
CHUNKS1 = (16, 16, 12)
HD2 = 128
A_HEADS = 12
A_SLOTS = 4
GROUPS = ((128, 1), (512, 4), (2048, 16))
B_HEADS = 8
N_BUCKETS = 32
MAX_DISTANCE = 2048
FF2 = 4 * D
F2T = FF2 // P
N_DIST = 384

RAW_SLOTS = 4
W_SLOTS = 4
UNIT = 16
AHEAD = 3
WIDE = 3

PV = {}
_at = 0
for _name, _n in (("pre_mix", KT), ("grp", KT), ("post_mix", KT), ("pre_ffn", KT), ("post_ffn", KT),
                  ("g_mix2", KT), ("g_mlp2", KT), ("qa", 1), ("ka", 1), ("qb", 1), ("kb", 1),
                  ("bf", 1), ("sinks", N_SWA), ("conv", 2 * F1T * 4)):
    PV[_name] = _at
    _at += _n
N_PV = _at
CS = {}
_at = 0
for _name, _n in (("ident", P), ("ones", P), ("triu", P), ("causal", T), ("window", T),
                  ("lhs_swa", T), ("rhs_swa", T), ("slope", 8), ("pick", 8), ("mA", 1), ("cA", 1),
                  ("mB", 1), ("cB", 1), ("sgn", 1)):
    CS[_name] = _at
    _at += _n
N_CS = _at


class Stage:

    def __init__(self, name, iters, units, blocks, mtiles, prev):
        self.name, self.iters, self.units, self.blocks, self.mtiles = name, iters, units, blocks, mtiles
        assert sum(mtiles) == units * blocks and blocks <= UNIT
        self.start = [sum(mtiles[:p]) for p in range(len(mtiles))]
        self.nm = len(mtiles)
        self.ubase = prev.ubase + prev.iters * prev.units if prev else 0
        self.gbase = prev.gbase + prev.iters * prev.nm if prev else 0
        assert iters == 1 or units % W_SLOTS == 0
        self.prev = prev
        if prev:
            prev.next = self
        self.next = None
        self.bank0 = (prev.bank0 + prev.nm * (1 if prev.nm % 2 else 0)) % 2 if prev else 0
        self.half = (blocks + 1) // 2
        self.wide = name in ("up1_0", "in2", "up2_0")
        self.scaled = {"pre": 3, "in1": 4, "in2": 15, "mix2": 2}.get(name, 4 if name[:3] == "up2" else 0)
        self.sbase = prev.sbase + prev.iters * prev.scaled if prev else 0

    def g(self, it, p):
        return it * self.nm + (self.gbase + p)

    def u(self, it, k):
        return it * self.units + (self.ubase + k)

    def bank(self, p):
        return (self.bank0 + p) % 2

    def free_after(self, p):
        return 1 if p == 0 and self.nm % 2 and self.iters > 1 else 2

    def splits(self, p):
        until = self.start[p] // self.blocks + AHEAD if p < self.nm - 1 else self.units - 1 + AHEAD
        before = self.start[p - 1] // self.blocks + AHEAD if p else AHEAD - 1
        return range(before + 1, until + 1)


def make_stages():
    out = []

    def add(*a):
        out.append(Stage(*a, out[-1] if out else None))

    add("pre", 1, 3, 16, [16] * 3)
    add("in1", 8, 4, 16, [16] * 4)
    add("out1", 4, 4, 16, [8, 8] * 4)
    for c, n in enumerate(CHUNKS1):
        add(f"up1_{c}", n // 2, 4, 16, [16] * 4)
        add(f"dn1_{c}", 4, 4, n, [n] * 4)
    add("in2", A_SLOTS, 16, 15, [16] * 15)
    add("mix2", KT, 4, 11, [16, 16, 4, 8])
    add("out2", 4, 4, 16, [16] * 4)
    for c in range(F2T // KT):
        add(f"up2_{c}", 4, 4, 16, [16] * 4)
        add(f"dn2_{c}", 4, 4, 16, [16] * 4)
    return out


class Chain:

    def __init__(self, eng, sem, per, index):
        self.eng, self.sem, self.per, self.base, self.n = eng, sem, per, index * per, 0

    def __call__(self, ins):
        ins.then_inc(self.sem, 1)
        self.n += 1
        self.eng.wait_ge(self.sem, self.base + self.n)

    def end(self):
        assert self.n == self.per, (self.n, self.per)


def build(nc, dram, out):
    stages = make_stages()
    ST = {s.name: s for s in stages}
    pv_d, cs_d = dram["pv"], dram["cs"]
    xT_d = dram["xT"].rearrange("(k p) t -> p k t", p=P)
    out_d = out.rearrange("(k p) t -> p k t", p=P)
    bias_rows = nc.dram_tensor("bias_rows", [A_HEADS + B_HEADS, N_DIST], F32).ap()

    ctx = ExitStack()
    with ctx:
        def sb(name, shape, dt=F32):
            return ctx.enter_context(nc.sbuf_tensor(name, shape, dt))

        def sem(name):
            return ctx.enter_context(nc.semaphore(name))

        raw = sb("raw", [P, RAW_SLOTS, UNIT * P // 2])
        whi = sb("whi", [P, W_SLOTS, UNIT * P], F32R)
        wlo = sb("wlo", [P, W_SLOTS, UNIT * P], F32R)
        x = sb("x", [P, KT, T])
        y = sb("y", [P, KT, T])
        hS = sb("hS", [P, KT, 2 * T], F32R)
        aS = sb("aS", [P, KT, 2 * T], F32R)
        pv = sb("pv", [P, N_PV])
        cs = sb("cs", [P, N_CS])
        tab = sb("tab", [P, A_HEADS + B_HEADS + N_DIST])
        heads = sb("heads", [P, 5 * 2 * T])
        vN = sb("vN", [P, 5, 2, P])
        vT = sb("vT", [P, T])
        tmp = sb("tmp", [P, 2, T])
        bias5 = sb("bias5", [P, 5, T])
        sq = sb("sq", [P, 2 * T])
        sq2 = sb("sq2", [P, T])
        acc = sb("acc", [P, 2, T])
        rsb = sb("rsb", [P, 2, T])
        og = sb("og", [P, 2, T])
        ms = sb("ms", [P, 8])
        rs = sb("rs", [P, 8])
        ms5 = sb("ms5", [P, 5, 4])
        rs5 = sb("rs5", [P, 5, 4])
        nhalf = sb("nhalf", [P, 4])
        mx = sb("mx", [P, 5, 2])
        nm = sb("nm", [P, 5, 2])
        den = sb("den", [P, 5, 2])
        esk = sb("esk", [P, 2, 2])
        dsum = sb("dsum", [P, 5, 2])
        rden = sb("rden", [P, 5, 2])
        mjoin = sb("mjoin", [P, 2])
        nsink = sb("nsink", [P, N_SWA])
        carrier = sb("carrier", [P, 5])
        gqs = sb("gqs", [P, 2])

        def hb(i, n=T):
            return heads[:, i * T:i * T + n]

        q_swa, q_fox, k_fox, k_swa, r_swa, r_fox, l_fox, b_fox = (hb(i) for i in range(8))
        qk = [hb(2 * s, 2 * T) for s in range(5)]
        ub = [heads[:, i * 258:(i + 1) * 258] for i in range(4)]
        cv = [heads[:, 4 * 258 + i * T:4 * 258 + (i + 1) * T] for i in range(4)]
        yflat = y[:, :, :].rearrange("p k t -> p (k t)")
        probs = [yflat[:, s * 384:(s + 1) * 384] for s in range(5)]
        probsT = [yflat[:, (5 + s) * 384:(6 + s) * 384] for s in range(5)]
        ident = cs[:, CS["ident"]:CS["ident"] + P]
        ones = cs[:, CS["ones"]:CS["ones"] + P]
        triu = cs[:, CS["triu"]:CS["triu"] + P]

        def cst(name, n=1):
            return cs[:, CS[name]:CS[name] + n]

        def par(name, k=0, n=1):
            o = PV[name]
            if isinstance(k, int):
                return pv[:, o + k:o + k + n]
            return pv[:, bass.ds(k + o, n)]

        G = [ctx.enter_context(nc.psum_tensor(f"G{i}", [P, 512], F32)) for i in range(2)]
        SB = [ctx.enter_context(nc.psum_tensor(f"SB{i}", [P, 512], F32)) for i in range(5)]
        MB = ctx.enter_context(nc.psum_tensor("MB", [P, 512], F32))

        landed = [sem(f"landed{i}") for i in range(RAW_SLOTS)]
        hi_done, lo_done = sem("hi_done"), sem("lo_done")
        unit_used = sem("unit_used")
        mt_done = sem("mt_done")
        tmp_done = sem("tmp_done")
        summed = sem("summed")
        ev_done = sem("ev_done")
        const_in, masks_in = sem("const_in"), sem("masks_in")
        x_in = [sem(f"x_in{j}") for j in range(4)]
        bias_in = [sem(f"bias_in{i}") for i in range(5)]
        prep = sem("prep")
        rows_in_sb, rows_out, rows_ps = sem("rows_in_sb"), sem("rows_out"), sem("rows_ps")
        bias_used = sem("bias_used")
        h_ready = sem("h_ready")
        a_ready = sem("a_ready")
        a_hi = sem("a_hi")
        h_hi = sem("h_hi")
        og_done = sem("og_done")
        nfold = sem("norm_fold")
        nsq, nsum, nms, npow, nbc, ncopy = (sem(f"norm_{n}") for n in ("sq", "sum", "ms", "pow", "bc", "copy"))
        s_mm, s_exp, s_rden, s_norm, s_nm = sem("s_mm"), sem("s_exp"), sem("s_rden"), sem("s_norm"), sem("s_nm")
        t_mm, t_copy, o_mm, o_sq, o_acc = sem("t_mm"), sem("t_copy"), sem("o_mm"), sem("o_sq"), sem("o_acc")
        aug_done, v_mm, v_copy = sem("aug_done"), sem("v_mm"), sem("v_copy")
        smax_c, pre_c, z_c = sem("smax_c"), sem("pre_c"), sem("z_c")
        lf_mm, lf_copy, c_mm, c_done = sem("lf_mm"), sem("lf_copy"), sem("c_mm"), sem("c_done")
        S2, E2, R2, N2, T2, TC2, O2 = (sem(n) for n in ("S2", "E2", "R2", "N2", "T2", "TC2", "O2"))
        NM2, hn_sq, hn_mm, hn_v, hn_ms, hn_pow, hn_bc, hn_done = (
            sem(n) for n in ("NM2", "hn_sq", "hn_mm", "hn_v", "hn_ms", "hn_pow", "hn_bc", "hn_done"))
        A2c, B2c = sem("A2c"), sem("B2c")
        y_c, sqy, sqa, yg = sem("y_c"), sem("sqy"), sem("sqa"), sem("yg")
        u_scaled, u_c, gelu_done, u_used, u_done = sem("u_scaled"), sem("u_c"), sem("gelu_done"), sem("u_used"), sem("u_done")
        r_done = sem("r_done")
        sig_in, sig_done, mix_c = sem("sig_in"), sem("sig_done"), sem("mix_c")
        mixed_done = sem("mixed_done")
        x_c, bx, bx_pool = sem("x_c"), sem("bx"), sem("bx_pool")
        x_done = sem("x_done")
        stored = sem("stored")


        NORM_BEFORE = {"out1": (1, 2), "up1_0": (3,), "in2": (5,)}
        NORM_IN = {"pre": 0, "up1_0": 4, "in2": 6, "up2_0": 7}
        GAIN = {0: "pre_mix", 1: "pre_ffn", 2: "g_mix2", 4: "g_mlp2"}
        FILL = {"pre": 0, "up1_0": 1, "in2": 2, "out2": 3, "up2_0": 4}
        ACC_DONE = {0: (nfold, 5), 4: (nfold, 10), 6: (nfold, 15), 1: (o_acc, 16), 2: (o_acc, 16), 3: (sqa, KT), 5: (sqa, 2 * KT), 7: (sqa, 3 * KT)}
        AHI2 = 16 + A_SLOTS + B_HEADS
        GROUP = {"A": (0, (0, 1, 2)), "3": (1, (3,)), "4": (2, (4,))}
        ST_NOW = [None, None, None, None]
        r_half = sem("r_half")

        def tile_of(tensor, i):
            if isinstance(i, int):
                return tensor[:, i, :]
            return tensor[:, bass.ds(i, 1), :].rearrange("p a t -> p (a t)")

        SPLIT_LATER = (f"dn1_{len(CHUNKS1) - 1}", "mix2")

        def splits_when(st, it, p, last):
            if last and p == st.nm - 1 and st.name in SPLIT_LATER:
                return "later"
            return "after" if is_wide(st, it) and p == WIDE - 1 and st.nm > WIDE else "before"

        def input_of(st, p):
            on_a = st.name == "out1" or st.name[:3] in ("dn1", "up2") or (st.name == "mix2" and p >= 2)
            return aS if on_a else hS

        def is_wide(st, it):
            return st.wide and isinstance(it, int) and it == 0

        def accumulator(st, it, p):
            return SB[p] if is_wide(st, it) and p in (2, 3) else G[st.bank(p)]

        def wait_x(eng, n, j):
            if n == 0:
                eng.wait_ge(x_in[j], 16)
            elif j == 3:
                eng.wait_ge(bx_pool, 2 * (n // 2 - 2) + 2)
            else:
                eng.wait_ge(bx, 6 * (n // 2 - 2) + 2 * j + 2)

        def residual(eng, chain, n, j):
            tiles = slice(4 * j, 4 * j + 4)
            r = rsb[:, 0:1, :].to_broadcast([P, 4, T])
            chain(eng.tensor_tensor(y[:, tiles, :], y[:, tiles, :], r, ALU.mult))
            chain(eng.tensor_tensor(x[:, tiles, :], x[:, tiles, :], y[:, tiles, :], ALU.add))

        FOLD_BASE = {0: 0, 4: 5, 6: 10}

        def fold(eng, n, first, last):
            for i in range(first, last):
                if i:
                    eng.wait_ge(nfold, FOLD_BASE[n] + i)
                if i < 3:
                    eng.wait_ge(nsq, 4 * (n // 2 - 1 if n else 0) + i + 2)
                    dst, src = y[:, 0:4, :], y[:, 4 * i + 4:4 * i + 8, :]
                else:
                    h = 2 if i == 3 else 1
                    dst, src = y[:, 0:h, :], y[:, h:2 * h, :]
                eng.tensor_tensor(dst, dst, src, ALU.add).then_inc(nfold, 1)

        STEPS = {
            "in1": [("P1", 1, 2), ("P2", 2, 2), ("P3", 3, 2),
                    ("R0", 0, 0), ("S1", 0, 1), ("T0", 0, 1), ("V", 1, 1), ("D1", 1, 1), ("O0", 1, 1),
                    ("S0", 2, 0), ("T1", 2, 1), ("D0", 3, 0), ("R1", 3, 0), ("O1", 3, 1)],
            "in2": [("Q0", 2, 0), ("N0", 4, 0), ("Q1", 5, 0), ("B0", 5, 0), ("S0", 6, 0), ("N1", 7, 0),
                    ("Q2", 8, 0), ("B1", 8, 0), ("S1", 9, 0), ("N2", 10, 0), ("Q3", 11, 0),
                    ("B2", 11, 0), ("S2", 12, 0), ("DA", 13, 0), ("N3", 13, 0), ("B3", 14, 0), ("Q4", 14, 0), ("TA", 14, 0),
                    ("S3", 0, 1), ("OA", 0, 1), ("D3", 1, 1), ("N4", 1, 1), ("B4", 2, 1), ("T3", 2, 1),
                    ("O3", 3, 1), ("S4", 3, 1), ("D4", 4, 1), ("T4", 5, 1), ("O4", 6, 1)],
        }
        for _n in [s.name for s in stages if s.name.startswith("up")]:
            STEPS[_n] = [("X0", 1, 0), ("X1", 2, 0), ("F0", 2, 0), ("X2", 3, 0), ("F1", 3, 0), ("G0", 3, 0),
                         ("X3", 0, 1), ("F2", 0, 1), ("M1", 0, 1), ("F3", 1, 1), ("G2", 1, 1), ("M3", 2, 1)
                         ] if _n[2] == "1" else [("F0", 2, 0), ("F1", 3, 0), ("F2", 0, 1), ("F3", 1, 1)]
        STEPS["out1"] = [("Y0", 3, 0), ("Y1", 5, 0), ("Y2", 7, 0), ("Y3", 1, 1)]
        STEPS[f"dn1_{len(CHUNKS1) - 1}"] = [("Y0", 2, 0), ("Y1", 3, 0), ("Y2", 0, 1), ("Y3", 1, 1)]
        STEPS["out2"] = [(a + s[1], p, w) for s, p, w in STEPS[f"dn1_{len(CHUNKS1) - 1}"] for a in "YH"]

        def run_stage(eng, st, step, mtile):
            steps = STEPS.get(st.name, [])
            wraps = any(w == 1 for _, _, w in steps)

            def body(it, first, last):
                for p in range(st.nm):
                    for name, pos, wrap in steps:
                        if pos == p and (wrap == 0 or (wrap == 1 and not first) or (wrap == 2 and first)):
                            step(name, it - 1 if wrap == 1 else it)
                    mtile(st, it, p, last)

            n = st.iters
            lo = 0
            if wraps or n == 1:
                body(0, True, n == 1)
                lo = 1
            if n - 1 > lo:
                with eng.Fori(lo, n - 1) as it:
                    body(it, False, False)
            if n > 1:
                body(n - 1, False, True)
            for name, pos, wrap in sorted(steps, key=lambda s: s[1]):
                if wrap == 1:
                    step(name, n - 1)

        block = ctx.enter_context(nc.Block())

        @block.sync
        def _(sp):
            sp.dma_start(pv[:, :], pv_d).then_inc(const_in, 16)
            m0 = CS["causal"]
            sp.dma_start(cs[:, 0:m0], cs_d[:, 0:m0]).then_inc(const_in, 16)
            for k in range(4):
                sp.dma_start(x[:, 4 * k:4 * k + 4, :], xT_d[:, 4 * k:4 * k + 4, :]).then_inc(x_in[k], 16)

            def load(st, it, k):
                for half in range(2):
                    h = 2 * st.u(it, k) + half
                    slot = (2 * (st.ubase + k) + half) % RAW_SLOTS
                    a, b = (0, st.half) if half == 0 else (st.half, st.blocks)
                    if not (isinstance(it, int) and 2 * st.u(it, k) + half < RAW_SLOTS):
                        sp.wait_ge(lo_done, h - (RAW_SLOTS - 1))
                    row = it * st.units + k
                    src = dram[st.name]
                    src = src[row] if isinstance(row, int) else src[bass.ds(row, 1)].rearrange("a p c -> (a p) c")
                    sp.dma_start(raw[:, slot, 0:(b - a) * P], src[:, a * P:b * P]).then_inc(landed[slot], 16)

            def load_bands(it, slots):
                for s in slots:
                    head = A_SLOTS * s + it if s < 3 else A_HEADS + 2 * it + s - 3
                    src = bass.AP(bias_rows.tensor, head * N_DIST, [[1, P], [1, T]])
                    sp.dma_start(bias5[:, s, :], src).then_inc(bias_in[s], 16)

            for st in stages:
                if st.name == "out1":
                    sp.wait_ge(rows_in_sb, 1)
                    sp.dma_start(bias_rows, bias5[0:A_HEADS + B_HEADS, :, :].rearrange(
                        "h a b -> h (a b)")[:, 0:N_DIST]).then_inc(rows_out, 16)
                    sp.wait_ge(rows_out, 16)

                def one(it):
                    if st.name == "in2":
                        if it:
                            sp.wait_ge(bias_used, 5 * (it - 1) + 3)
                        load_bands(it, range(3))
                    for k in range(st.units):
                        if st.name == "in2" and k == 10:
                            if it:
                                sp.wait_ge(bias_used, 5 * it)
                            load_bands(it, range(3, 5))
                        load(st, it, k)

                if st.iters == 1 or st.name == "in2":
                    for i in range(st.iters):
                        one(i)
                    if st.name == "pre":
                        sp.dma_start(cs[:, m0:], cs_d[:, m0:]).then_inc(masks_in, 16)
                        sp.dma_start(tab[:, :], dram["tab"]).then_inc(masks_in, 16)
                else:
                    with sp.Fori(0, st.iters) as it:
                        one(it)
            for m in range(KT):
                sp.wait_ge(x_done, m + 1)
                sp.dma_start(out_d[:, m, :], x[:, m, :]).then_inc(stored, 16)
            sp.wait_ge(stored, 16 * KT)

        EARLY_TILES = {2: range(0, 7), 3: range(7, 14)}
        LAST_TILES = range(14, KT)
        A_BASE = {"in1": 0}
        n_a = 2 * 8
        for c, n in enumerate(CHUNKS1):
            A_BASE[f"up1_{c}"] = n_a
            n_a += n
        A_BASE["in2"] = n_a
        n_a += A_SLOTS + B_HEADS
        for c in range(F2T // KT):
            A_BASE[f"up2_{c}"] = n_a
            n_a += KT
        last1, last2 = f"dn1_{len(CHUNKS1) - 1}", f"dn2_{F2T // KT - 1}"
        AFTER = {5: last1}
        NORMS = [("x", D), (0, N_SWA * HD1), (1, N_FOX * HD1), (0, D), ("x", D), (0, D), ("x", D), (0, D)]

        def w0(v):
            return not isinstance(v, int) or v > 0

        @block.tensor
        def _(pe):
            def mm(o, w, m, start, stop):
                return pe.matmul(o, w, m, start=start, stop=stop, skip_group_check=False)

            def wide_start(st):
                for p in range(2):
                    if st.g(0, p) > 1:
                        pe.wait_ge(ev_done, st.g(0, p) - 1)
                for kk in range(KT):
                    pe.wait_ge(h_ready, KT * FILL[st.name] + kk + 1)
                    act = input_of(st, 0)[:, kk, :]
                    for p in range(WIDE):
                        flat = st.start[p] + kk
                        k, within = flat // st.blocks, flat % st.blocks
                        slot = (st.ubase + k) % W_SLOTS
                        if within in (0, st.half):
                            pe.wait_ge(lo_done, 2 * st.u(0, k) + (1 if within == 0 else 2))
                        bank = accumulator(st, 0, p)
                        h_w, l_w = (w[:, slot, within * P:(within + 1) * P] for w in (whi, wlo))
                        if kk < KT - 1:
                            one = mm(bank[:, :], h_w, act, kk == 0, False)
                            mm(bank[:, T:], l_w, act[:, 0:T], False, False)
                            if kk == 0 and p == 0 and st.prev:
                                one.then_inc(unit_used, 1)
                        else:
                            one = mm(bank[:, T:], l_w, act[:, 0:T], False, False)
                            mm(bank[:, :], h_w, act, False, True).then_inc(mt_done, 1)
                            if p:
                                one.then_inc(unit_used, 1)

            def mtile(st, it, p, last):
                if is_wide(st, it) and p < WIDE:
                    if p == 0:
                        wide_start(st)
                        norm_sums(NORM_IN[st.name])
                    return
                g = st.g(it, p)
                acc_bank = accumulator(st, it, p)
                X = input_of(st, p)
                first_block = {("out1", 1): 8, ("mix2", 3): A_SLOTS}.get((st.name, p % 2 if st.name == "out1" else p), 0)
                f = g - st.free_after(p) + 1
                if w0(f) and not (is_wide(st, it) and p == WIDE):
                    pe.wait_ge(ev_done, f)
                n = st.mtiles[p]
                spreads = st.name in NORM_IN and isinstance(it, int) and it == 0 and p == (WIDE if st.wide else 1)
                for kk in range(n):
                    if spreads and kk == 4:
                        norm_spread(NORM_IN[st.name])
                    flat = st.start[p] + kk
                    k, within = flat // st.blocks, flat % st.blocks
                    slot = (st.ubase + k) % W_SLOTS
                    if within in (0, st.half):
                        pe.wait_ge(lo_done, 2 * st.u(it, k) + (1 if within == 0 else 2))
                    if p == 0 and st.name in FILL and FILL[st.name] is not None:
                        pe.wait_ge(h_ready, KT * FILL[st.name] + kk + 1)
                    if st.name[:2] == "dn" and p == 0:
                        pe.wait_ge(a_ready, A_BASE["up" + st.name[2:]] + kk + 1)
                    if kk == 0 and (st.name, p) in (("out1", 0), ("mix2", 2)):
                        pe.wait_ge(a_ready, 16 if st.name == "out1" else A_BASE["in2"] + A_SLOTS + B_HEADS)
                    act = X[:, first_block + kk, :]
                    h_w, l_w = (w[:, slot, within * P:(within + 1) * P] for w in (whi, wlo))
                    if kk < n - 1:
                        one = mm(acc_bank[:, :], h_w, act, kk == 0, False)
                        mm(acc_bank[:, T:], l_w, act[:, 0:T], False, False)
                    else:
                        one = mm(acc_bank[:, T:], l_w, act[:, 0:T], False, False)
                        end = mm(acc_bank[:, :], h_w, act, False, True)
                        end.then_inc(mt_done, 1)
                    if kk == 0 and p == WIDE if is_wide(st, it) and k < W_SLOTS else within == 0 and (st.prev or k):
                        one.then_inc(unit_used, 1)

                if st.name in NORM_IN and not st.wide and p == 0:
                    norm_sums(NORM_IN[st.name])

            def norm_sums(n):
                src, _ = NORMS[n]
                pe.wait_ge(*ACC_DONE[n])
                for c in range(2):
                    total = y[:, 0, c * P:(c + 1) * P] if src == "x" else acc[:, src, c * P:(c + 1) * P]
                    end = mm(SB[4 * c][:, 0:1], total, ones[:, 0:1], True, True)
                end.then_inc(nsum, 1)

            def norm_spread(n):
                pe.wait_ge(npow, n + 1)
                if n:
                    pe.wait_ge(ncopy, n)
                for c in range(2):
                    end = mm(SB[1][:, c * P:(c + 1) * P], rs[:, c:c + 1].to_broadcast([P, P]), ident, True, True)
                end.then_inc(nbc, 1)

            def scores(b, it):
                q = 2 * it + b
                pe.wait_ge(ev_done, ST["in1"].g(it, 0 if b == 0 else 2) + 1)
                pe.wait_ge(aug_done, q + 1)
                if w0(q - 1):
                    pe.wait_ge(t_copy, q - 1)
                qt, kt, lh, rh = (q_swa, k_swa, cst("lhs_swa", T), r_swa) if b == 0 else (q_fox, k_fox, l_fox, r_fox)
                for par_ in range(2):
                    at = slice(64 * par_, 64 * par_ + 64)
                    bank = SB[2 * b + par_]
                    for o, qs, nk in ((bank[:, 0:P], slice(0, P), P), (bank[:, P:P + T], slice(P, T), T)):
                        mm(o, qt[at, qs], kt[at, 0:nk], True, False)
                        end = mm(o, lh[at, qs], rh[at, 0:nk], False, True)
                end.then_inc(s_mm, 1)

            def turn(bank, pr):
                for a in range(3):
                    end = pe.transpose(bank[:, a * P:(a + 1) * P], pr[:, a * P:(a + 1) * P], ident)
                return end

            def step(name, it):
                if name == "P1":
                    pe.wait_ge(rows_in_sb, 1)
                    pe.wait_ge(ev_done, ST["pre"].g(0, 1) + 1)
                    for c in range(2):
                        end = pe.transpose(SB[4][:, c * P:(c + 1) * P], vT[:, c * P:(c + 1) * P], ident)
                    end.then_inc(v_mm, 1)
                elif name == "P2":
                    pe.wait_ge(z_c, 6)
                    pe.wait_ge(v_copy, 1)
                    for c in range(2):
                        end = pe.transpose(SB[4][:, c * P:(c + 1) * P], sq[:, T + c * P:T + (c + 1) * P], ident)
                    end.then_inc(lf_mm, 1)
                elif name == "P3":
                    pe.wait_ge(lf_copy, 1)
                    mm(SB[4][:, 0:P], og[:, 0, 0:P], triu, True, True)
                    mm(SB[4][:, P:T], og[:, 0, 0:P], ones, True, False)
                    mm(SB[4][:, P:T], og[:, 0, P:T], triu, False, True).then_inc(c_mm, 1)
                elif name in ("S0", "S1") and ST_NOW[0] == "in1":
                    scores(int(name[1]), it)
                elif name == "V":
                    pe.wait_ge(ev_done, ST["in1"].g(it, 3) + 1)
                    pe.wait_ge(c_done, 1)
                    pe.wait_ge(v_copy, it + 1)
                    for c in range(2):
                        end = pe.transpose(SB[4][:, c * P:(c + 1) * P], vT[:, c * P:(c + 1) * P], ident)
                    end.then_inc(v_mm, 1)
                elif name in ("T0", "T1"):
                    b = int(name[1])
                    pe.wait_ge(s_norm, 2 * it + b + 1)
                    for s in (2 * b, 2 * b + 1):
                        end = turn(SB[s], probs[s])
                    end.then_inc(t_mm, 1)
                elif name in ("O0", "O1"):
                    b = int(name[1])
                    q = 2 * it + b
                    pe.wait_ge(t_copy, q + 1)
                    pe.wait_ge(v_copy, 1 if b == 0 else it + 2)
                    if w0(q):
                        pe.wait_ge(o_sq, q)
                    for par_ in range(2):
                        at = slice(64 * par_, 64 * par_ + 64)
                        pt = probsT[2 * b + par_]
                        mm(MB[at, 0:T], vN[:, b, 0, at], pt[:, 0:T], True, False)
                        end = mm(MB[at, P:T], vN[:, b, 1, at], pt[:, T:T + P], False, True)
                    end.then_inc(o_mm, 1)
                elif name[0] == "N":
                    s = int(name[1])
                    h = 5 * it + s
                    pe.wait_ge(hn_sq, h + 1)
                    pe.wait_ge(ev_done, ST["in2"].g(it, 3 * s + 2) + 1)
                    if w0(it):
                        pe.wait_ge(TC2, 3 * (it - 1) + max(0, s - 2) + 1)
                    for c in range(4):
                        mm(SB[s][:, c:c + 1], sq[:, c * P:(c + 1) * P], ones[:, 0:1], True, True)
                    for c in range(2):
                        end = pe.transpose(SB[s][:, (1 + c) * P:(2 + c) * P], vT[:, c * P:(c + 1) * P], ident)
                    end.then_inc(hn_mm, 1)
                elif name[0] == "B":
                    s = int(name[1])
                    pe.wait_ge(hn_pow, 5 * it + s + 1)
                    for c in range(4):
                        end = mm(SB[s][:, c * P:(c + 1) * P], rs5[:, s, c:c + 1].to_broadcast([P, P]), ident, True, True)
                    end.then_inc(hn_bc, 1)
                elif name[0] == "S":
                    s = int(name[1])
                    pe.wait_ge(hn_done, 5 * it + s + 1)
                    mm(SB[s][:, 0:P], qk[s][:, 0:P], qk[s][:, T:T + P], True, True)
                    mm(SB[s][:, P:P + T], qk[s][:, P:T], qk[s][:, T:2 * T], True, True).then_inc(S2, 1)
                elif name[0] == "T":
                    b, ss = GROUP[name[1]]
                    pe.wait_ge(N2, 3 * it + b + 1)
                    for s in ss:
                        end = turn(SB[s], probs[s])
                    end.then_inc(T2, 1)
                elif name[0] == "O":
                    b, ss = GROUP[name[1]]
                    q = 3 * it + b
                    pe.wait_ge(TC2, q + 1)
                    pe.wait_ge(a_ready, A_BASE["in2"] + q)
                    for s in ss:
                        mm(MB[:, 0:T], vN[:, s, 0, :], probsT[s][:, 0:T], s == ss[0], False)
                        end = mm(MB[:, P:T], vN[:, s, 1, :], probsT[s][:, T:T + P], False, s == ss[-1])
                    end.then_inc(O2, 1)

            pe.wait_ge(const_in, 32)
            for st in stages:
                for n in NORM_BEFORE.get(st.name, ()):
                    norm_sums(n)
                    norm_spread(n)
                if st.name == "in1":
                    pe.wait_ge(masks_in, 32)
                    mm(SB[4][0:A_HEADS + B_HEADS, 0:N_DIST], tab[0:N_BUCKETS + 4, 0:A_HEADS + B_HEADS],
                       tab[0:N_BUCKETS + 4, A_HEADS + B_HEADS:], True, True).then_inc(rows_ps, 1)
                ST_NOW[0] = st.name
                run_stage(pe, st, step, mtile)

        @block.scalar
        def _(act):
            def split(st, it, k):
                slot = (st.ubase + k) % W_SLOTS
                u = st.u(it, k)
                if w0(u - W_SLOTS + 1) and not (isinstance(it, int) and u < W_SLOTS):
                    act.wait_ge(unit_used, u - W_SLOTS + 1)
                for half in range(2):
                    h0 = 2 * (st.ubase + k) + half
                    a, b = (0, st.half) if half == 0 else (st.half, st.blocks)
                    act.wait_ge(landed[h0 % RAW_SLOTS],
                                16 * (h0 // RAW_SLOTS + 1) + it * (16 * 2 * st.units // RAW_SLOTS))
                    act.activation(whi[:, slot, a * P:b * P], raw[:, h0 % RAW_SLOTS, 0:(b - a) * P],
                                   ACT.Copy).then_inc(hi_done, 1)

            def splits(st, it, p, last):
                for v in st.splits(p):
                    if v < st.units:
                        split(st, it, v)
                    elif not last:
                        split(st, it + 1, v - st.units)
                    elif st.next:
                        split(st.next, 0, v - st.units)

            def mtile(st, it, p, last):
                when = splits_when(st, it, p, last)
                if when == "before":
                    splits(st, it, p, last)
                if st.name in NORM_IN and isinstance(it, int) and it == 0 and p == 1:
                    spread(NORM_IN[st.name])
                if st.name == "mix2" and last and p in EARLY_TILES:
                    act.wait_ge(mt_done, st.g(it, 1) + 1)
                    fill_mixed(EARLY_TILES[p])
                g = st.g(it, p)
                act.wait_ge(mt_done, g + 1)
                if w0(g - 1):
                    act.wait_ge(ev_done, g - 1)
                scale = HD1 ** -0.5 if st.name == "in1" and p < 2 else 1.0
                act.activation(tmp[:, st.bank(p), :], accumulator(st, it, p)[:, T:], ACT.Copy, scale=scale).then_inc(tmp_done, 1)
                if when == "after":
                    splits(st, it, p, last)
                if st.name == "pre" and p == 2:
                    act.wait_ge(z_c, 2)
                    act.activation(sq2[:, :], sq2[:, :], ACT.Exp).then_inc(z_c, 1)
                    act.wait_ge(z_c, 3)
                    act.activation(sq2[:, :], sq2[:, :], ACT.Ln, bias=1.0).then_inc(z_c, 1)
                if st.name == "mix2" and p < 2:
                    act.wait_ge(ev_done, g + 1)
                    act.activation(og[:, p, :], og[:, p, :], ACT.Sigmoid).then_inc(sig_done, 1)

            def exps(slots, nms_, wait):
                for s, m in zip(slots, nms_):
                    for n, cols in ((0, slice(0, P)), (1, slice(P, P + T))):
                        end = act.activation(probs[s][:, cols], probs[s][:, cols], ACT.Exp, bias=nm[:, m, n:n + 1],
                                             accum_out=den[:, s, n:n + 1])
                return end

            def scales(slots, nms_):
                for s, m in zip(slots, nms_):
                    for n, cols in ((0, slice(0, P)), (1, slice(P, P + T))):
                        end = act.activation(probs[s][:, cols], probs[s][:, cols], ACT.Copy, scale=rden[:, m, n:n + 1])
                return end

            def step(name, it):
                if name[0] == "Y":
                    stage = ST_NOW[1]
                    m = it * 4 + int(name[1])
                    i = m + KT * {"out1": 0, last1: 1, "out2": 2}[stage]
                    if stage == "out2":
                        act.wait_ge(x_c, m + 1)
                    else:
                        act.wait_ge(y_c, 3 * (m + 1) if stage == "out1" else m + (len(CHUNKS1) + 1) * KT + 1)
                    if w0(i):
                        act.wait_ge(sqa, i)
                    act.activation(sq2[:, :], tile_of(x if stage == "out2" else y, m), ACT.Square).then_inc(sqy, 1)
                    if stage != "out2":
                        act.activation(tile_of(y, m), tile_of(y, m), ACT.Copy,
                                       scale=par("post_mix" if stage == "out1" else "post_ffn", m)).then_inc(yg, 1)
                elif name[0] == "H":
                    m = it * 4 + int(name[1])
                    act.wait_ge(x_c, m + 1)
                    act.activation(tile_of(aS, m)[:, 0:T], tile_of(x, m), ACT.Copy, scale=par("g_mlp2", m)).then_inc(h_hi, 1)
                elif name[0] == "F":
                    if ST_NOW[1][:3] == "up2":
                        p = int(name[1])
                        i = KT * int(ST_NOW[1][4]) + it * 4 + p
                        act.wait_ge(r_done, i + 1)
                        act.activation(tile_of(hS, it * 4 + p)[:, 0:T], cv[p], ACT.Copy).then_inc(a_hi, 1)
                elif name == "P1":
                    act.wait_ge(v_mm, 1)
                    act.activation(vN[:, 0, :, :].rearrange("p a b -> p (a b)"), SB[4][:, 0:T], ACT.Copy).then_inc(v_copy, 1)
                elif name == "V":
                    act.wait_ge(v_mm, it + 2)
                    act.activation(vN[:, 1, :, :].rearrange("p a b -> p (a b)"), SB[4][:, 0:T], ACT.Copy).then_inc(v_copy, 1)
                elif ST_NOW[1] == "in1" and name[0] == "S":
                    b = int(name[1])
                    q = 2 * it + b
                    act.wait_ge(s_nm, q + 1)
                    if b == 0:
                        for j in range(2):
                            act.activation(esk[:, j, :], nm[:, j, :], ACT.Exp, bias=par("sinks", 8 * j + it))
                    exps((2 * b, 2 * b + 1), (2 * b, 2 * b + 1), None).then_inc(s_exp, 1)
                elif ST_NOW[1] == "in1" and name[0] == "D":
                    b = int(name[1])
                    act.wait_ge(s_rden, 2 * it + b + 1)
                    scales((2 * b, 2 * b + 1), (2 * b, 2 * b + 1)).then_inc(s_norm, 1)
                elif ST_NOW[1] == "in1" and name[0] == "O":
                    b = int(name[1])
                    q = 2 * it + b
                    act.wait_ge(og_done, q + 1)
                    if w0(q):
                        act.wait_ge(o_acc, q)
                    act.activation(sq2[:, :], MB[:, 0:T], ACT.Square).then_inc(o_sq, 1)
                    act.activation(tile_of(aS, 8 * b + it)[:, 0:T], og[:, b, :], ACT.Copy).then_inc(a_hi, 1)
                elif name[0] == "G":
                    p = int(name[1])
                    c = int(ST_NOW[1][4])
                    i = 2 * sum(CHUNKS1[:c]) + it * 4 + p
                    act.wait_ge(u_c, 3 * i + 3)
                    act.activation(cv[p], cv[p], ACT.Gelu_apprx_tanh).then_inc(gelu_done, 1)
                elif name[0] == "Q":
                    s = int(name[1])
                    h = 5 * it + s
                    act.wait_ge(ev_done, ST["in2"].g(it, 3 * s + 1) + 1)
                    if w0(h):
                        act.wait_ge(hn_mm, h)
                    act.activation(sq[:, :], qk[s], ACT.Square).then_inc(hn_sq, 1)
                elif name[0] == "N":
                    s = int(name[1])
                    act.wait_ge(hn_mm, 5 * it + s + 1)
                    act.activation(vN[:, s, :, :].rearrange("p a b -> p (a b)"), SB[s][:, P:P + T], ACT.Copy).then_inc(hn_v, 1)
                elif name in ("S2", "S3", "S4"):
                    b, ss = GROUP["A" if name == "S2" else name[1]]
                    act.wait_ge(NM2, 3 * it + b + 1)
                    exps(ss, [ss[0]] * len(ss), None).then_inc(E2, 1)
                elif name[0] == "D":
                    b, ss = GROUP[name[1]]
                    act.wait_ge(R2, 3 * it + b + 1)
                    scales(ss, [ss[0]] * len(ss)).then_inc(N2, 1)
                elif name[0] == "O":
                    b, ss = GROUP[name[1]]
                    act.wait_ge(O2, 3 * it + b + 1)
                    act.activation(tile_of(aS, it if b == 0 else A_SLOTS + 2 * it + b - 1)[:, 0:T], MB[:, 0:T],
                                   ACT.Copy).then_inc(a_hi, 1)

            def spread(n):
                src, _ = NORMS[n]
                act.wait_ge(nbc, n + 1)
                act.activation(rsb[:, src if n in (1, 2) else 0, :], SB[1][:, 0:T], ACT.Copy).then_inc(ncopy, 1)

            def norm(n):
                if n in AFTER:
                    splits(ST[AFTER[n]], ST[AFTER[n]].iters - 1, ST[AFTER[n]].nm - 1, True)
                spread(n)

            def fill_x(f, n):
                for j in range(4):
                    wait_x(act, n, j)
                    if f == 0 and j == 0:
                        act.wait_ge(const_in, 32)
                    if f == 0 and j == 3:
                        split(stages[0], 0, 0)
                    for t in range(4 * j, 4 * j + 4):
                        act.activation(hS[:, t, 0:T], x[:, t, :], ACT.Copy, scale=par(GAIN[f], t)).then_inc(h_hi, 1)
                    act.activation(y[:, 4 * j:4 * j + 4, :], x[:, 4 * j:4 * j + 4, :], ACT.Square).then_inc(nsq, 1)

            def fill_mixed(tiles):
                for t in tiles:
                    act.wait_ge(mixed_done, t + 1)
                    act.activation(hS[:, t, 0:T], y[:, t, :], ACT.Copy).then_inc(h_hi, 1)

            for st in stages:
                for n in NORM_BEFORE.get(st.name, ()):
                    norm(n)
                if st.name in ("pre", "up1_0", "in2"):
                    fill_x(FILL[st.name], NORM_IN[st.name])
                if st.name == "pre":
                    for k in range(1, AHEAD):
                        split(st, 0, k)
                if st.name == "out2":
                    fill_mixed(LAST_TILES)
                    splits(ST["mix2"], KT - 1, 3, True)
                if st.name == "in1":
                    act.wait_ge(rows_ps, 1)
                    act.activation(bias5[0:A_HEADS + B_HEADS, :, :].rearrange("h a b -> h (a b)")[:, 0:N_DIST],
                                   SB[4][0:A_HEADS + B_HEADS, 0:N_DIST], ACT.Copy).then_inc(rows_in_sb, 1)
                ST_NOW[1] = st.name
                run_stage(act, st, step, mtile)

        @block.vector
        def _(dve):
            def split(st, it, k):
                slot = (st.ubase + k) % W_SLOTS
                for half in range(2):
                    h0 = 2 * (st.ubase + k) + half
                    a, b = (0, st.half) if half == 0 else (st.half, st.blocks)
                    dve.wait_ge(hi_done, 2 * st.u(it, k) + half + 1)
                    dve.tensor_tensor(wlo[:, slot, a * P:b * P], raw[:, h0 % RAW_SLOTS, 0:(b - a) * P],
                                      whi[:, slot, a * P:b * P].bitcast(F32), ALU.subtract).then_inc(lo_done, 1)

            def splits(st, it, p, last):
                for v in st.splits(p):
                    if v < st.units:
                        split(st, it, v)
                    elif not last:
                        split(st, it + 1, v - st.units)
                    elif st.next:
                        split(st.next, 0, v - st.units)

            def mtile(st, it, p, last):
                when = splits_when(st, it, p, last)
                first = st.name in NORM_IN and isinstance(it, int) and it == 0
                if when == "before" and not (first and (p == 1 or p == 0 and st.name == "in2")):
                    splits(st, it, p, last)
                if first and p == 0:
                    norm(NORM_IN[st.name])
                    splits(st, it, 1, last)
                if st.name == "mix2" and last and p in EARLY_TILES:
                    dve.wait_ge(mt_done, st.g(it, 1) + 1)
                    fill_mixed(EARLY_TILES[p])
                read_out(st, it, p)
                if when == "after":
                    splits(st, it, p, last)

            def read_out(st, it, p):
                g = st.g(it, p)
                A = accumulator(st, it, p)[:, 0:T]
                B = tmp[:, st.bank(p), :]
                dve.wait_ge(tmp_done, g + 1)

                def add_to(dest):
                    dve.tensor_tensor(dest, A, B, ALU.add).then_inc(ev_done, 1)

                def times_rms(dest):
                    if st.name in NORM_IN and isinstance(it, int) and it == 0 and p == 0:
                        dve.wait_ge(ncopy, NORM_IN[st.name] + 1)
                    dve.wait_ge(summed, it * st.scaled + (st.sbase + p + 1))
                    dve.tensor_tensor(dest, dest, rsb[:, 0, :], ALU.mult).then_inc(ev_done, 1)

                def scaled_to(dest):
                    dve.tensor_tensor(dest, A, B, ALU.add).then_inc(summed, 1)
                    times_rms(dest)

                def self_wait():
                    dve.wait_ge(ev_done, g + 1)

                name = st.name
                if name == "pre":
                    if p < 2:
                        scaled_to((k_swa, vT[:, :])[p])
                    else:
                        z, lf = sq[:, 0:T], sq[:, T:2 * T]
                        scaled_to(z)
                        self_wait()
                        dve.tensor_scalar(z, z, par("bf"), None, ALU.add).then_inc(z_c, 1)
                        dve.wait_ge(z_c, 1)
                        dve.scalar_tensor_tensor(sq2[:, :], z, -1.0, z, ALU.mult, ALU.min).then_inc(z_c, 1)
                        dve.wait_ge(z_c, 4)
                        dve.scalar_tensor_tensor(lf, z, 0.0, sq2[:, :], ALU.min, ALU.subtract).then_inc(z_c, 1)
                        dve.wait_ge(z_c, 5)
                        dve.tensor_scalar(lf, lf, cst("sgn"), None, ALU.mult).then_inc(z_c, 1)
                elif name == "in1":
                    if p < 2:
                        dve.scalar_tensor_tensor((q_swa, q_fox)[p], A, HD1 ** -0.5, B, ALU.mult, ALU.add).then_inc(summed, 1)
                        times_rms((q_swa, q_fox)[p])
                    else:
                        scaled_to((k_fox, vT[:, :])[p - 2])
                elif name == "out1":
                    half = og[:, p % 2, :]
                    add_to(half)
                    self_wait()
                    m = it * 4 + p // 2
                    c = Chain(dve, y_c, 3, m)
                    c.n = p % 2
                    c(dve.tensor_tensor(half, half, rsb[:, p % 2, :], ALU.mult))
                    if p % 2:
                        c(dve.tensor_tensor(tile_of(y, m), og[:, 0, :], og[:, 1, :], ALU.add))
                        c.end()
                elif name[:3] == "up1":
                    i = 2 * sum(CHUNKS1[:int(name[4])]) + it * 4 + p
                    if w0(i - 1):
                        dve.wait_ge(u_scaled, i - 1)
                    add_to(sq[:, p % 2 * T:(p % 2 + 1) * T])
                elif name[:3] == "dn1":
                    c = int(name[4])
                    m = it * 4 + p
                    if c == 0:
                        add_to(tile_of(y, m))
                    else:
                        add_to(og[:, p % 2, :])
                        self_wait()
                        i = 3 * KT + (c - 1) * KT + m
                        dve.tensor_tensor(tile_of(y, m), tile_of(y, m), og[:, p % 2, :], ALU.add).then_inc(y_c, 1)
                elif name == "in2":
                    s, part = divmod(p, 3)
                    scaled_to((qk[s][:, 0:T], qk[s][:, T:2 * T], vT[:, :])[part])
                elif name == "mix2":
                    if p < 2:
                        scaled_to(og[:, p, :])
                    else:
                        br = sq[:, (p - 2) * T:(p - 1) * T]
                        add_to(br)
                        self_wait()
                        dve.wait_ge(sig_done, 2 * it + p - 1)
                        c = Chain(dve, mix_c, 2, it)
                        c.n = p - 2
                        c(dve.tensor_tensor(br, br, og[:, p - 2, :], ALU.mult))
                        if p == 3:
                            dve.tensor_tensor(tile_of(y, it), sq[:, 0:T], sq[:, T:2 * T], ALU.add).then_inc(mixed_done, 1)
                elif name == "out2" or name[:3] == "dn2":
                    m = it * 4 + p
                    add_to(og[:, p % 2, :])
                    self_wait()
                    dve.tensor_tensor(tile_of(x, m), tile_of(x, m), og[:, p % 2, :], ALU.add).then_inc(
                        x_done if name == last2 else x_c, 1)
                elif name[:3] == "up2":
                    scaled_to(ub[p][:, 0:T])
                    self_wait()
                    dve.scalar_tensor_tensor(cv[p], ub[p][:, 0:T], 0.0, ub[p][:, 0:T], ALU.max, ALU.mult).then_inc(r_done, 1)

            def carry_waits(i):
                dve.memset(carrier[:, i:i + 1], 0.0)

            def logits(s, mask, bank):
                for n, o, m in ((0, slice(0, P), mask[:, P:T]), (1, slice(P, P + T), mask[:, 0:T])):
                    end = dve.tensor_tensor_reduce(probs[s][:, o], bank[:, o], m, 1.0, LOWEST, ALU.add, ALU.max,
                                                   mx[:, s, n:n + 1])
                return end

            def step(name, it):
                st = ST_NOW[2]
                if name[0] == "H":
                    m = it * 4 + int(name[1])
                    low_part(tile_of(aS, m), m, 4)
                elif name == "P2":
                    dve.wait_ge(lf_mm, 1)
                    dve.tensor_copy(og[:, 0, :], SB[4][:, 0:T]).then_inc(lf_copy, 1)
                elif name == "P3":
                    dve.wait_ge(c_mm, 1)
                    dve.tensor_scalar(l_fox, SB[4][:, 0:T], cst("mA"), cst("cA"), ALU.mult, ALU.add)
                    dve.tensor_scalar(b_fox, SB[4][:, 0:T], cst("mB"), cst("cB"), ALU.mult, ALU.add).then_inc(c_done, 1)
                elif name == "R0":
                    o = CS["slope"]
                    col = cs[:, o + it:o + it + 1] if isinstance(it, int) else cs[:, bass.ds(it + o, 1)]
                    dve.tensor_scalar(r_swa, cst("rhs_swa", T), col, None, ALU.mult).then_inc(aug_done, 1)
                elif name == "R1":
                    o = CS["pick"]
                    col = cs[:, o + it:o + it + 1] if isinstance(it, int) else cs[:, bass.ds(it + o, 1)]
                    if isinstance(it, int) and it == 0:
                        dve.wait_ge(c_done, 1)
                    dve.tensor_scalar(r_fox, b_fox, col, None, ALU.mult).then_inc(aug_done, 1)
                elif st == "in1" and name[0] == "S":
                    b = int(name[1])
                    q = 2 * it + b
                    dve.wait_ge(s_mm, q + 1)
                    carry_waits(b)
                    mask = cst("window" if b == 0 else "causal", T)
                    c = Chain(dve, smax_c, 1, q)
                    logits(2 * b, mask, SB[2 * b])
                    c(logits(2 * b + 1, mask, SB[2 * b + 1]))
                    c.end()
                    for s in (2 * b, 2 * b + 1):
                        if b == 0:
                            k = 8 * s + it
                            ns = nsink[:, k:k + 1] if isinstance(k, int) else nsink[:, bass.ds(k, 1)]
                            end = dve.tensor_scalar(nm[:, s, :], mx[:, s, :], -1.0, ns, ALU.mult, ALU.min)
                        else:
                            end = dve.tensor_scalar(nm[:, s, :], mx[:, s, :], -1.0, None, ALU.mult)
                    end.then_inc(s_nm, 1)
                elif st == "in1" and name[0] == "D":
                    b = int(name[1])
                    q = 2 * it + b
                    ss = slice(2 * b, 2 * b + 2)
                    dve.wait_ge(s_exp, q + 1)
                    src = den
                    if b == 0:
                        dve.tensor_tensor(dsum[:, ss, :], den[:, ss, :], esk[:, :, :], ALU.add).then_inc(pre_c, 1)
                        dve.wait_ge(pre_c, it + 1)
                        src = dsum
                    dve.reciprocal(rden[:, ss, :], src[:, ss, :]).then_inc(s_rden, 1)
                elif name in ("T0", "T1"):
                    b = int(name[1])
                    dve.wait_ge(t_mm, 2 * it + b + 1)
                    dve.tensor_copy(probsT[2 * b], SB[2 * b][:, 0:384])
                    dve.tensor_copy(probsT[2 * b + 1], SB[2 * b + 1][:, 0:384]).then_inc(t_copy, 1)
                elif name in ("O0", "O1"):
                    b = int(name[1])
                    q = 2 * it + b
                    dve.wait_ge(o_mm, q + 1)
                    dve.tensor_scalar(og[:, b, :], MB[:, 0:T], par("grp", 8 * b + it), None, ALU.mult).then_inc(og_done, 1)
                    dve.wait_ge(o_sq, q + 1)
                    dve.tensor_tensor(acc[:, b, :], acc[:, b, :], sq2[:, :], ALU.add).then_inc(o_acc, 1)
                    dve.wait_ge(a_hi, q + 1)
                    dst = tile_of(aS, 8 * b + it)
                    dve.tensor_tensor(dst[:, T:], og[:, b, :], dst[:, 0:T].bitcast(F32), ALU.subtract).then_inc(a_ready, 1)
                elif name[0] == "F" and st[:3] == "up1":
                    p = int(name[1])
                    c0 = int(st[4])
                    first = 2 * sum(CHUNKS1[:c0])
                    i = first + it * 4 + p
                    c = Chain(dve, u_c, 3, i)

                    def w(k):
                        return par("conv", (it * 4 + (first + p)) * 4 + k)

                    n_used = sum(CHUNKS1[:c0]) + it * 2 + p // 2 - 1
                    if w0(n_used):
                        dve.wait_ge(u_used, n_used)
                    dve.wait_ge(u_scaled, i + 1)
                    c(dve.tensor_scalar(cv[p], ub[p][:, 0:T], w(0), w(3), ALU.mult, ALU.add))
                    c(dve.scalar_tensor_tensor(cv[p], ub[p][:, 1:1 + T], w(1), cv[p], ALU.mult, ALU.add))
                    c(dve.scalar_tensor_tensor(cv[p], ub[p][:, 2:2 + T], w(2), cv[p], ALU.mult, ALU.add))
                    c.end()
                elif name[0] == "F":
                    p = int(name[1])
                    i = KT * int(st[4]) + it * 4 + p
                    dst = tile_of(hS, it * 4 + p)
                    dve.wait_ge(a_hi, AHI2 + i + 1)
                    dve.tensor_tensor(dst[:, T:], cv[p], dst[:, 0:T].bitcast(F32), ALU.subtract).then_inc(a_ready, 1)
                elif name[0] == "N":
                    s = int(name[1])
                    h = 5 * it + s
                    dve.wait_ge(hn_v, h + 1)
                    dve.tensor_scalar(ms5[:, s, :], SB[s][:, 0:4], 1.0 / HD2, EPS, ALU.mult, ALU.add).then_inc(hn_ms, 1)
                elif name[0] == "B":
                    s = int(name[1])
                    dve.wait_ge(hn_bc, 5 * it + s + 1)
                    gq, gk = (gqs[:, 0:1], par("ka")) if s < 3 else (gqs[:, 1:2], par("kb"))
                    dve.scalar_tensor_tensor(qk[s][:, 0:T], qk[s][:, 0:T], gq, SB[s][:, 0:T], ALU.mult, ALU.mult)
                    dve.scalar_tensor_tensor(qk[s][:, T:], qk[s][:, T:], gk, SB[s][:, T:], ALU.mult, ALU.mult).then_inc(hn_done, 1)
                elif name[0] == "S":
                    s = int(name[1])
                    h = 5 * it + s
                    dve.wait_ge(S2, h + 1)
                    dve.wait_ge(bias_in[s], 16 * it + 16)
                    carry_waits(s)
                    logits(s, bias5[:, s, ::-1], SB[s]).then_inc(bias_used, 1)
                    if s >= 2:
                        b, ss = GROUP["A" if s == 2 else str(s)]
                        q = 3 * it + b
                        dve.wait_ge(bias_used, h + 1)
                        src = mx[:, s, :]
                        if s == 2:
                            dve.tensor_reduce(mjoin[:, :], mx[:, 0:3, :].rearrange("p s n -> p n s"), AX.X, ALU.max).then_inc(A2c, 1)
                            dve.wait_ge(A2c, 2 * it + 1)
                            src = mjoin[:, :]
                        dve.tensor_scalar(nm[:, ss[0], :], src, -1.0, None, ALU.mult).then_inc(NM2, 1)
                elif name[0] == "D":
                    b, ss = GROUP[name[1]]
                    q = 3 * it + b
                    dve.wait_ge(E2, q + 1)
                    src = den[:, ss[0], :]
                    if b == 0:
                        dve.tensor_reduce(dsum[:, 0, :], den[:, 0:3, :].rearrange("p s n -> p n s"), AX.X, ALU.add).then_inc(A2c, 1)
                        dve.wait_ge(A2c, 2 * it + 2)
                        src = dsum[:, 0, :]
                    dve.reciprocal(rden[:, ss[0], :], src).then_inc(R2, 1)
                elif name[0] == "T":
                    b, ss = GROUP[name[1]]
                    dve.wait_ge(T2, 3 * it + b + 1)
                    for s in ss:
                        end = dve.tensor_copy(probsT[s], SB[s][:, 0:384])
                    end.then_inc(TC2, 1)
                elif name[0] == "O":
                    b, ss = GROUP[name[1]]
                    q = 3 * it + b
                    dst = tile_of(aS, it if b == 0 else A_SLOTS + 2 * it + b - 1)
                    dve.wait_ge(a_hi, KT + q + 1)
                    dve.tensor_tensor(dst[:, T:], MB[:, 0:T], dst[:, 0:T].bitcast(F32), ALU.subtract).then_inc(a_ready, 1)

            def norm(n):
                _, width = NORMS[n]
                dve.wait_ge(nsum, n + 1)
                for c in range(2):
                    end = dve.tensor_scalar(ms[:, c:c + 1], SB[4 * c][:, 0:1], 1.0 / width, EPS, ALU.mult, ALU.add)
                end.then_inc(nms, 1)
                if n in AFTER:
                    splits(ST[AFTER[n]], ST[AFTER[n]].iters - 1, ST[AFTER[n]].nm - 1, True)

            def low_part(dst, t, f):
                dve.wait_ge(h_hi, t + (KT * f + 1))
                dve.scalar_tensor_tensor(dst[:, T:], tile_of(x, t), par(GAIN[f], t), dst[:, 0:T].bitcast(F32),
                                         ALU.mult, ALU.subtract).then_inc(h_ready, 1)

            def fill_x(f, n):
                if n:
                    dve.wait_ge(ncopy, n)
                    dve.wait_ge(yg, KT * (n // 2 - 1))
                    c = Chain(dve, bx, 6, n // 2 - 2)
                for j in range(4):
                    if n and j < 3:
                        residual(dve, c, n, j)
                    for t in range(4 * j, 4 * j + 4):
                        low_part(hS[:, t, :], t, f)

            def fill_mixed(tiles):
                for t in tiles:
                    dve.wait_ge(h_hi, KT * FILL["out2"] + t + 1)
                    dve.tensor_tensor(hS[:, t, T:], y[:, t, :], hS[:, t, 0:T].bitcast(F32), ALU.subtract).then_inc(h_ready, 1)

            dve.wait_ge(const_in, 32)
            dve.tensor_scalar(nsink[:, :], par("sinks", 0, N_SWA), -1.0, None, ALU.mult)
            dve.tensor_scalar(gqs[:, 0:1], par("qa"), HD2 ** -0.5, None, ALU.mult)
            dve.tensor_scalar(gqs[:, 1:2], par("qb"), HD2 ** -0.5, None, ALU.mult)
            dve.memset(acc[:, :, :], 0.0).then_inc(prep, 1)
            dve.wait_ge(prep, 1)
            n_memset = 1
            for st in stages:
                for n in NORM_BEFORE.get(st.name, ()):
                    norm(n)
                if st.name == "in1":
                    dve.wait_ge(masks_in, 32)
                if st.name in ("pre", "up1_0", "in2"):
                    n = NORM_IN[st.name]
                    fill_x(FILL[st.name], n)
                    if st.name == "pre":
                        split(st, 0, 0)
                    if st.name == "in2":
                        splits(st, 0, 0, False)
                    fold(dve, n, 2, 5)
                    if st.name == "pre":
                        for k in range(1, AHEAD):
                            split(st, 0, k)
                if st.name == "out2":
                    fill_mixed(LAST_TILES)
                    splits(ST["mix2"], KT - 1, 3, True)
                if st.name in ("out1", last1, "out2"):
                    dve.wait_ge(nsum, {"out1": 3, last1: 4, "out2": 6}[st.name])
                    if st.name == "out1":
                        dve.wait_ge(ncopy, 3)
                    n_memset += 1
                    dve.memset(acc[:, 0, :], 0.0).then_inc(prep, 1)
                    dve.wait_ge(prep, n_memset)
                if st.name == "up1_0":
                    for i in range(4):
                        end = dve.memset(ub[i][:, 0:2], 0.0)
                    n_memset += 1
                    end.then_inc(prep, 1)
                    dve.wait_ge(prep, n_memset)
                ST_NOW[2] = st.name
                run_stage(dve, st, step, mtile)

        @block.gpsimd
        def _(pool):
            pool.memset(nhalf[:, :], -0.5).then_inc(r_half, 1)
            pool.wait_ge(r_half, 1)

            def mtile(st, it, p, last):
                pass

            def power(n):
                pool.wait_ge(nms, n + 1)
                pool.tensor_tensor(rs[:, 0:2], ms[:, 0:2], nhalf[:, 0:2], ALU.pow).then_inc(npow, 1)

            def step(name, it):
                st = ST_NOW[3]
                if st == "in2":
                    if name[0] == "N":
                        s = int(name[1])
                        pool.wait_ge(hn_ms, it * 5 + (s + 1))
                        pool.tensor_tensor(rs5[:, s, :], ms5[:, s, :], nhalf[:, 0:4], ALU.pow).then_inc(hn_pow, 1)
                elif name[0] == "Y":
                    i = it * 4 + (int(name[1]) + KT * {"out1": 0, last1: 1, "out2": 2}[st])
                    pool.wait_ge(sqy, i + 1)
                    if w0(i):
                        pool.wait_ge(sqa, i)
                    pool.tensor_tensor(acc[:, 0, :], acc[:, 0, :], sq2[:, :], ALU.add).then_inc(sqa, 1)
                elif name[0] == "X":
                    p = int(name[1])
                    first = 2 * sum(CHUNKS1[:int(st[4])])
                    i = first + it * 4 + p
                    if isinstance(i, int) and i == 0:
                        pool.wait_ge(ncopy, NORM_IN["up1_0"] + 1)
                    pool.wait_ge(ev_done, ST[st].g(it, p) + 1)
                    if w0(i - 3):
                        pool.wait_ge(u_c, 3 * (i - 3))
                    pool.tensor_tensor(ub[p][:, 2:2 + T], sq[:, p % 2 * T:(p % 2 + 1) * T], rsb[:, 0, :],
                                       ALU.mult).then_inc(u_scaled, 1)
                elif name[0] == "M":
                    p = int(name[1])
                    c0 = int(st[4])
                    j = sum(CHUNKS1[:c0]) + it * 2 + p // 2
                    dst = tile_of(aS, it * 2 + p // 2)
                    o = og[:, p // 2, :]
                    pool.wait_ge(gelu_done, j + 1)
                    pool.wait_ge(u_c, 3 * (2 * j + 2))
                    pool.tensor_tensor(o, cv[p - 1], cv[p], ALU.mult).then_inc(u_used, 1)
                    pool.wait_ge(u_used, j + 1)
                    pool.tensor_copy(dst[:, 0:T], o).then_inc(u_done, 1)
                    pool.wait_ge(u_done, j + 1)
                    pool.tensor_tensor(dst[:, T:], o, dst[:, 0:T].bitcast(F32), ALU.subtract).then_inc(a_ready, 1)

            for st in stages:
                for n in NORM_BEFORE.get(st.name, ()):
                    power(n)
                if st.name in NORM_IN:
                    n = NORM_IN[st.name]
                    if n in (4, 6):
                        pool.wait_ge(ncopy, n)
                        pool.wait_ge(yg, KT * (n // 2 - 1))
                        residual(pool, Chain(pool, bx_pool, 2, n // 2 - 2), n, 3)
                    if n != 7:
                        fold(pool, n, 0, 2)
                    power(n)
                ST_NOW[3] = st.name
                if st.name in ("out1", last1, "in2", "out2") or st.name[:3] == "up1":
                    run_stage(pool, st, step, mtile)


def rel_bucket(d):
    exact = N_BUCKETS // 2
    df = np.maximum(d, 1).astype(np.float32)
    large = exact + (np.log(df / np.float32(exact)) / np.float32(np.log(MAX_DISTANCE / exact))
                     * np.float32(N_BUCKETS - exact)).astype(np.int32)
    return np.where(d < exact, d, np.minimum(large, N_BUCKETS - 1))


def constants():
    c = np.zeros((P, N_CS), np.float32)
    p = np.arange(P)
    row = p % 64
    c[:, CS["ident"]:CS["ident"] + P] = np.eye(P)
    c[:, CS["ones"]:CS["ones"] + P] = 1
    c[:, CS["triu"]:CS["triu"] + P] = p[:, None] <= p[None, :]
    t, j = p[:, None], np.arange(T)[None, :]
    dist = P + t - j
    c[:, CS["causal"]:CS["causal"] + T] = np.where(dist >= 0, 0, -BIG)
    c[:, CS["window"]:CS["window"] + T] = np.where((dist >= 0) & (dist < WINDOW), 0, -BIG)
    s = np.arange(T)
    slopes = 2.0 ** (-8.0 * np.arange(1, N_SWA + 1) / N_SWA)
    for half in range(2):
        r = 64 * half
        c[r, CS["lhs_swa"]:CS["lhs_swa"] + T] = s
        c[r + 1, CS["lhs_swa"]:CS["lhs_swa"] + T] = 1
        c[r, CS["rhs_swa"]:CS["rhs_swa"] + T] = 1
        c[r + 1, CS["rhs_swa"]:CS["rhs_swa"] + T] = -s
        for i in range(8):
            c[r:r + 2, CS["slope"] + i] = -slopes[8 * half + i]
            for q in (0, 32):
                c[r + q + 2 * i + half, CS["pick"] + i] = 1
    c[:, CS["mA"]] = (row >= 32) & (row < 48)
    c[:, CS["cA"]] = row < 16
    c[:, CS["mB"]] = row < 16
    c[:, CS["cB"]] = (row >= 32) & (row < 48)
    c[:, CS["sgn"]] = np.where(row < 16, -1.0, np.where((row >= 32) & (row < 48), 1.0, 0.0))
    return c


def distance_rows():
    dist = np.arange(N_DIST) - (P - 1)
    out = np.zeros((N_BUCKETS + 4, N_DIST), np.float32)
    ok = dist >= 0
    out[rel_bucket(np.maximum(dist, 0))[ok], np.arange(N_DIST)[ok]] = 1
    for g, (window, r) in enumerate(GROUPS):
        out[N_BUCKETS + g] = np.where(ok & (dist % r == 0) & (dist <= window), 0, -BIG)
    out[N_BUCKETS + 3] = np.where(ok, 0, -BIG)
    return out


def group_rows():
    out = np.zeros((4, A_HEADS + B_HEADS), np.float32)
    for h in range(A_HEADS + B_HEADS):
        out[min(h // A_SLOTS, 3), h] = 1
    return out


def as_units(parts, blocks):
    b = np.concatenate([w.reshape(-1, P, P) for w in parts])
    return np.ascontiguousarray(b.reshape(-1, blocks, P, P).transpose(0, 2, 1, 3)).reshape(-1, P, blocks * P)


def cols(w, i):
    return w[:, i * P:(i + 1) * P]


def swa_tile(j):
    return np.concatenate([np.arange(HD1) + HD1 * j, np.arange(HD1) + HD1 * (8 + j)])


def lay_out(a):
    w_in, w_out, w_up, w_down = (np.asarray(a[n])[0] for n in ("w_in", "w_out", "w_up", "w_down"))
    o_k = N_SWA * HD1
    o_v = o_k + N_KV * HD1
    o_qf = o_v + N_KV * HD1
    o_kf, o_vf, o_f = o_qf + N_FOX * HD1, o_qf + 2 * N_FOX * HD1, o_qf + 3 * N_FOX * HD1
    gate_cols = np.zeros((D, P), np.float32)
    b_f = np.zeros((P, 1), np.float32)
    for r in (0, 32, 64, 96):
        gate_cols[:, r:r + N_FOX] = w_in[:, o_f:]
        b_f[r:r + N_FOX, 0] = np.asarray(a["b_forget"])[0]
    d = {"pre": as_units([w_in[:, o_k:o_v], w_in[:, o_v:o_qf], gate_cols], 16)}
    d["in1"] = as_units([w for j in range(8) for w in (
        w_in[:, swa_tile(j)], cols(w_in[:, o_qf:], j), cols(w_in[:, o_kf:], j), cols(w_in[:, o_vf:], j))], 16)
    rows = np.concatenate([swa_tile(j) for j in range(8)] + [np.arange(o_k, D)])
    wo = w_out[rows]
    d["out1"] = as_units([cols(wo, m) for m in range(KT)], 16)
    at = 0
    for c, n in enumerate(CHUNKS1):
        d[f"up1_{c}"] = as_units([cols(w_up, i + half * F1T) for i in range(at, at + n) for half in range(2)], 16)
        d[f"dn1_{c}"] = as_units([cols(w_down[at * P:(at + n) * P], m) for m in range(KT)], n)
        at += n
    w2 = np.asarray(a["w_in_2"])
    o_b = 3 * A_HEADS * HD2
    o_ga = o_b + 3 * B_HEADS * HD2
    o_gb = o_ga + D
    d["in2"] = as_units([cols(w2, part * A_HEADS + A_SLOTS * g + i) if g < 3
                         else cols(w2[:, o_b:], part * B_HEADS + 2 * i + g - 3)
                         for i in range(A_SLOTS) for g in range(5) for part in range(3)], 15)
    wa, wb = np.asarray(a["w_branch_a_2"]), np.asarray(a["w_branch_b_2"])
    d["mix2"] = as_units([w for m in range(KT) for w in (
        cols(w2[:, o_ga:], m), cols(w2[:, o_gb:], m), cols(wa, m), cols(wb, m))], 11)
    w_out2, w_up2, w_down2 = (np.asarray(a[n]) for n in ("w_out_2", "w_up_2", "w_down_2"))
    d["out2"] = as_units([cols(w_out2, m) for m in range(KT)], 16)
    for c in range(F2T // KT):
        d[f"up2_{c}"] = as_units([cols(w_up2, c * KT + i) for i in range(KT)], 16)
        d[f"dn2_{c}"] = as_units([cols(w_down2[c * D:(c + 1) * D], m) for m in range(KT)], 16)

    def tiles(v):
        return np.asarray(v).reshape(-1, P).T

    grp = np.concatenate([np.asarray(a["grp_swa_g"])[0], np.asarray(a["grp_fox_g"])[0]])[rows]
    conv = np.concatenate([np.asarray(a["conv_w"])[0], np.asarray(a["conv_b"])])
    conv = conv.reshape(4, 2, F1T, P).transpose(3, 2, 1, 0).reshape(P, -1)
    d["pv"] = np.ascontiguousarray(np.concatenate([
        tiles(a["pre_mix_g"]), tiles(grp), tiles(a["post_mix_g"]), tiles(a["pre_ffn_g"]), tiles(a["post_ffn_g"]),
        tiles(a["g_mix_2"]), tiles(a["g_mlp_2"]), tiles(a["q_norm_a_2"]), tiles(a["k_norm_a_2"]),
        tiles(a["q_norm_b_2"]), tiles(a["k_norm_b_2"]), b_f,
        np.broadcast_to(np.asarray(a["sinks"]), (P, N_SWA)), conv], axis=1))
    d["cs"] = constants()
    tab = np.zeros((P, A_HEADS + B_HEADS + N_DIST), np.float32)
    tab[:N_BUCKETS, :A_HEADS + B_HEADS] = np.asarray(a["rel_bias_2"])
    tab[N_BUCKETS:N_BUCKETS + 4, :A_HEADS + B_HEADS] = group_rows()
    tab[:N_BUCKETS + 4, A_HEADS + B_HEADS:] = distance_rows()
    d["tab"] = tab
    d["xT"] = np.ascontiguousarray(np.asarray(a["x"])[0].T)
    return d


def kernel(**inputs):
    import concourse.bacc as bacc
    from concourse.bass_utils import run_bass_kernel_spmd

    nc = bacc.Bacc("TRN2", target_bir_lowering=False, num_devices=1, dynamic_dma_scratch_size=1024)
    arrays = lay_out(inputs)
    dram = {n: nc.dram_tensor(f"in_{n}", v.shape, F32, kind="ExternalInput").ap() for n, v in arrays.items()}
    out = nc.dram_tensor("out_T", (D, T), F32, kind="ExternalOutput").ap()
    build(nc, dram, out)
    r = run_bass_kernel_spmd(nc, [{f"in_{n}": v for n, v in arrays.items()}], core_ids=[0])
    return np.ascontiguousarray(r.results[0]["out_T"].T)[None]
```

```python
from contextlib import ExitStack

import numpy as np

import concourse.bass as bass
from concourse import mybir

F32 = mybir.dt.float32
F32R = mybir.dt.float32r
ALU = mybir.AluOpType
ACT = mybir.ActivationFunctionType
AX = mybir.AxisListType

P = 128
T = 256
D = 2048
KT = D // P
EPS = 1e-6
BIG = 1e30
LOWEST = -3e38

HD1 = 64
N_SWA = 16
N_KV = 2
N_FOX = 16
WINDOW = 128
FF1 = 5632
F1T = FF1 // P
CHUNKS1 = (14, 14, 16)
HD2 = 128
A_HEADS = 12
A_SLOTS = 4
GROUPS = ((128, 1), (512, 4), (2048, 16))
B_HEADS = 8
N_BUCKETS = 32
MAX_DISTANCE = 2048
FF2 = 4 * D
F2T = FF2 // P
N_DIST = 384

RAW_SLOTS = 4
W_SLOTS = 4
UNIT = 16
AHEAD = 3
WIDE = 3

PV = {}
_at = 0
for _name, _n in (("pre_mix", KT), ("grp", KT), ("post_mix", KT), ("pre_ffn", KT), ("post_ffn", KT),
                  ("g_mix2", KT), ("g_mlp2", KT), ("qa", 1), ("ka", 1), ("qb", 1), ("kb", 1),
                  ("bf", 1), ("sinks", N_SWA), ("conv", 2 * F1T * 4)):
    PV[_name] = _at
    _at += _n
N_PV = _at
CS = {}
_at = 0
for _name, _n in (("ident", P), ("ones", P), ("triu", P), ("causal", T), ("window", T),
                  ("dist", T), ("slope", N_SWA), ("pick", 8), ("mA", 1), ("cA", 1),
                  ("mB", 1), ("cB", 1), ("sgn", 1)):
    CS[_name] = _at
    _at += _n
N_CS = _at


class Stage:

    def __init__(self, name, iters, units, blocks, mtiles, prev):
        self.name, self.iters, self.units, self.blocks, self.mtiles = name, iters, units, blocks, mtiles
        assert sum(mtiles) == units * blocks and blocks <= UNIT
        self.start = [sum(mtiles[:p]) for p in range(len(mtiles))]
        self.nm = len(mtiles)
        self.ubase = prev.ubase + prev.iters * prev.units if prev else 0
        self.gbase = prev.gbase + prev.iters * prev.nm if prev else 0
        assert iters == 1 or units % W_SLOTS == 0
        self.prev = prev
        if prev:
            prev.next = self
        self.next = None
        self.bank0 = (prev.bank0 + prev.nm * (1 if prev.nm % 2 and prev.iters == 1 else 0)) % 2 if prev else 0
        self.half = (blocks + 1) // 2
        self.wide = name in ("up1_0", "in2", "up2_0")
        self.scaled = {"pre": 3, "in1": 4, "in2": 15, "mix2": 2}.get(name, 4 if name[:3] == "up2" else 0)
        self.sbase = prev.sbase + prev.iters * prev.scaled if prev else 0

    def g(self, it, p):
        return it * self.nm + (self.gbase + p)

    def u(self, it, k):
        return it * self.units + (self.ubase + k)

    def bank(self, p):
        return (self.bank0 + p) % 2

    def splits(self, p):
        until = self.start[p] // self.blocks + AHEAD if p < self.nm - 1 else self.units - 1 + AHEAD
        before = self.start[p - 1] // self.blocks + AHEAD if p else AHEAD - 1
        return range(before + 1, until + 1)


def make_stages():
    out = []

    def add(*a):
        out.append(Stage(*a, out[-1] if out else None))

    add("pre", 1, 3, 16, [16] * 3)
    add("in1", 8, 4, 16, [16] * 4)
    add("out1", 4, 4, 16, [8, 8] * 4)
    for c, n in enumerate(CHUNKS1):
        add(f"up1_{c}", n // 2, 4, 16, [16] * 4)
        add(f"dn1_{c}", 4, 4, n, [n] * 4)
    add("in2", A_SLOTS, 16, 15, [16] * 15)
    add("mix2", KT, 4, 11, [16, 16, 4, 8])
    add("out2", 4, 4, 16, [16] * 4)
    for c in range(F2T // KT):
        add(f"up2_{c}", 4, 4, 16, [16] * 4)
        add(f"dn2_{c}", 4, 4, 16, [16] * 4)
    return out


class Chain:

    def __init__(self, eng, sem, per, index):
        self.eng, self.sem, self.per, self.base, self.n = eng, sem, per, index * per, 0

    def __call__(self, ins):
        ins.then_inc(self.sem, 1)
        self.n += 1
        self.eng.wait_ge(self.sem, self.base + self.n)

    def end(self):
        assert self.n == self.per, (self.n, self.per)


def build(nc, dram, out):
    stages = make_stages()
    ST = {s.name: s for s in stages}
    pv_d, cs_d = dram["pv"], dram["cs"]
    xT_d = dram["xT"].rearrange("(k p) t -> p k t", p=P)
    out_d = out.rearrange("(k p) t -> p k t", p=P)
    bias_rows = nc.dram_tensor("bias_rows", [A_HEADS + B_HEADS, N_DIST], F32).ap()

    ctx = ExitStack()
    with ctx:
        def sb(name, shape, dt=F32):
            return ctx.enter_context(nc.sbuf_tensor(name, shape, dt))

        def sem(name):
            return ctx.enter_context(nc.semaphore(name))

        raw = sb("raw", [P, RAW_SLOTS, UNIT * P // 2])
        whi = sb("whi", [P, W_SLOTS, UNIT * P], F32R)
        wlo = sb("wlo", [P, W_SLOTS, UNIT * P], F32R)
        x = sb("x", [P, KT, T])
        y = sb("y", [P, KT, T])
        hS = sb("hS", [P, KT, 2 * T], F32R)
        aS = sb("aS", [P, KT, 2 * T], F32R)
        pv = sb("pv", [P, N_PV])
        cs = sb("cs", [P, N_CS])
        tab = sb("tab", [P, A_HEADS + B_HEADS + N_DIST])
        heads = sb("heads", [P, 5 * 2 * T])
        vN = sb("vN", [P, 5, 2, P])
        vT = sb("vT", [P, T])
        tmp = sb("tmp", [P, 2, T])
        bias5 = sb("bias5", [P, 5, T])
        sq = sb("sq", [P, 2 * T])
        sq2 = sb("sq2", [P, T])
        acc = sb("acc", [P, 2, T])
        rsb = sb("rsb", [P, 2, T])
        og = sb("og", [P, 2, T])
        ms = sb("ms", [P, 8])
        rs = sb("rs", [P, 8])
        ms5 = sb("ms5", [P, 5, 4])
        rs5 = sb("rs5", [P, 5, 4])
        nhalf = sb("nhalf", [P, 4])
        mx = sb("mx", [P, 5, 2])
        nm = sb("nm", [P, 5, 2])
        den = sb("den", [P, 5, 2])
        esk = sb("esk", [P, 2, 2])
        dsum = sb("dsum", [P, 5, 2])
        rden = sb("rden", [P, 5, 2])
        mjoin = sb("mjoin", [P, 2])
        nsink = sb("nsink", [P, N_SWA])
        carrier = sb("carrier", [P, 5])
        warm = sb("warm", [P, 1])
        gqs = sb("gqs", [P, 2])

        def hb(i, n=T):
            return heads[:, i * T:i * T + n]

        q_swa, q_fox, k_fox, k_swa, r_fox, l_fox, b_fox = (hb(i) for i in range(7))
        bias_swa = [hb(7), hb(8)]
        qk = [hb(2 * s, 2 * T) for s in range(5)]
        ub = [heads[:, i * 258:(i + 1) * 258] for i in range(4)]
        cv = [heads[:, 4 * 258 + i * T:4 * 258 + (i + 1) * T] for i in range(4)]
        yflat = y[:, :, :].rearrange("p k t -> p (k t)")
        probs = [yflat[:, s * 384:(s + 1) * 384] for s in range(5)]
        probsT = [yflat[:, (5 + s) * 384:(6 + s) * 384] for s in range(5)]
        ident = cs[:, CS["ident"]:CS["ident"] + P]
        ones = cs[:, CS["ones"]:CS["ones"] + P]
        triu = cs[:, CS["triu"]:CS["triu"] + P]

        def cst(name, n=1):
            return cs[:, CS[name]:CS[name] + n]

        def par(name, k=0, n=1):
            o = PV[name]
            if isinstance(k, int):
                return pv[:, o + k:o + k + n]
            return pv[:, bass.ds(k + o, n)]

        G = [ctx.enter_context(nc.psum_tensor(f"G{i}", [P, 512], F32)) for i in range(2)]
        SB = [ctx.enter_context(nc.psum_tensor(f"SB{i}", [P, 512], F32)) for i in range(5)]
        MB = ctx.enter_context(nc.psum_tensor("MB", [P, 512], F32))

        landed = [sem(f"landed{i}") for i in range(RAW_SLOTS)]
        hi_done, lo_done = sem("hi_done"), sem("lo_done")
        unit_used = sem("unit_used")
        mt_done = sem("mt_done")
        tmp_done = sem("tmp_done")
        summed = sem("summed")
        ev_done = sem("ev_done")
        gains_in, const_in, masks_in = sem("gains_in"), sem("const_in"), sem("masks_in")
        x_in = [sem(f"x_in{j}") for j in range(4)]
        bias_in = [sem(f"bias_in{i}") for i in range(5)]
        prep = sem("prep")
        rows_in_sb, rows_out, rows_ps = sem("rows_in_sb"), sem("rows_out"), sem("rows_ps")
        bias_used = sem("bias_used")
        h_ready, h_hi = sem("h_ready"), sem("h_hi")
        a_ready, a_hi = sem("a_ready"), sem("a_hi")
        half_set = sem("half_set")
        nsq, nfold, nsum, nms, npow, nbc, ncopy = (
            sem(f"norm_{n}") for n in ("sq", "fold", "sum", "ms", "pow", "spread", "copied"))
        s_mm, s_nm, s_exp, s_rden, s_norm = (sem(f"att1_{n}") for n in ("scores", "maxima", "exps", "recips", "probs"))
        t_mm, t_copy, o_mm, o_sq, o_acc, og_done = (
            sem(f"att1_{n}") for n in ("turned", "copied", "outputs", "squares", "added", "gained"))
        pos_done, v_mm, v_copy = sem("pos_done"), sem("v_turned"), sem("v_copied")
        smax_c, pre_c = sem("maxima_step"), sem("sink_added")
        z_c, lf_mm, lf_copy, c_mm, c_done = (sem(f"forget_{n}") for n in ("step", "turned", "copied", "summed", "ready"))
        maxima2, exps2, recips2, probs2, turned2, copied2, outputs2, join2 = (
            sem(f"att2_{n}") for n in ("maxima", "exps", "recips", "probs", "turned", "copied", "outputs", "join"))
        scores2 = sem("att2_scores")
        hn_sq, hn_mm, hn_v, hn_ms, hn_pow, hn_bc, hn_done = (
            sem(f"head_norm_{n}") for n in ("sq", "sum", "v", "ms", "pow", "spread", "done"))
        y_step, sqy, sqa, yg = sem("y_step"), sem("y_squared"), sem("squares_added"), sem("y_gained")
        u_scaled, conv_step, gelu_done, u_used, u_done = (
            sem(f"hidden_{n}") for n in ("scaled", "conv", "gelu", "product", "copied"))
        r_done = sem("relu_squared")
        sig_done, mix_c, mixed_done = sem("sigmoid_done"), sem("gated"), sem("mixed_done")
        x_added, res_dve, res_pool, x_done = (sem(f"x_{n}") for n in ("added", "residual", "residual_pool", "done"))
        stored = sem("stored")

        NORM_BEFORE = {"up1_0": (3,), "in2": (5,)}
        NORM_IN = {"pre": 0, "up1_0": 4, "in2": 6, "up2_0": 7}
        GAIN = {0: "pre_mix", 1: "pre_ffn", 2: "g_mix2", 4: "g_mlp2"}
        FILL = {"pre": 0, "up1_0": 1, "in2": 2, "out2": 3, "up2_0": 4}
        ACC_DONE = {0: (nfold, 5), 4: (nfold, 10), 6: (nfold, 15), 1: (o_acc, 15), 2: (o_acc, 16),
                    3: (sqa, KT - 1), 5: (sqa, 2 * (KT - 1)), 7: (sqa, 3 * (KT - 1))}
        ATTENTION_TILES = 16 + A_SLOTS + B_HEADS
        GROUP = {"A": (0, (0, 1, 2)), "3": (1, (3,)), "4": (2, (4,))}
        stage_of = {"pe": None, "act": None, "dve": None, "pool": None}

        def tile_of(tensor, i):
            if isinstance(i, int):
                return tensor[:, i, :]
            return tensor[:, bass.ds(i, 1), :].rearrange("p a t -> p (a t)")

        SPLIT_LATER = ("mix2",)

        def splits_when(st, it, p, last):
            if last and (p == st.nm - 1 and st.name in SPLIT_LATER or p == 2 and st.name == "mix2"):
                return "later"
            if isinstance(it, int) and it == 0 and (st.name, p) in (("out1", 0), ("out1", 1), ("out1", 2), ("mix2", 2)):
                return "later" if (st.name, p) == ("out1", 0) else "after"
            return "after" if is_wide(st, it) and p == WIDE - 1 or st.name == "pre" and p else "before"

        def input_of(st, p):
            on_a = st.name == "out1" or st.name[:3] in ("dn1", "up2") or (st.name == "mix2" and p >= 2)
            return aS if on_a else hS

        def is_wide(st, it):
            return st.wide and isinstance(it, int) and it == 0

        def accumulator(st, it, p):
            if st.name == "mix2" and p >= 2:
                return SB[p - 2]
            if st.name == "in2" and p == st.nm - 1:
                return MB
            if st.name == "pre" and p == 2:
                return SB[2]
            return SB[p] if is_wide(st, it) and p in (2, 3) else G[st.bank(p)]

        RESIDUAL = {0: (1, "dve"), 1: (4, "dve"), 4: (8, "pool"), 8: (12, "dve"), 12: (16, "pool")}

        def residual_done(n, t):
            engine = RESIDUAL[t][1]
            of_engine = [a for a, (_, e) in RESIDUAL.items() if e == engine]
            per = 2 * len(of_engine)
            return {"dve": res_dve, "pool": res_pool}[engine], per * (n // 2 - 2) + 2 * of_engine.index(t) + 2

        def wait_x(eng, n, t):
            if n == 0 and t % 4 == 0:
                eng.wait_ge(x_in[t // 4], 16)
            elif n and t in RESIDUAL:
                eng.wait_ge(*residual_done(n, t))

        def residual(eng, chain, t):
            b = RESIDUAL[t][0]
            tiles = slice(t, b)
            r = rsb[:, 0:1, :].to_broadcast([P, b - t, T])
            chain(eng.tensor_tensor(y[:, tiles, :], y[:, tiles, :], r, ALU.mult))
            chain(eng.tensor_tensor(x[:, tiles, :], x[:, tiles, :], y[:, tiles, :], ALU.add))

        FOLD_BASE = {0: 0, 4: 5, 6: 10}

        def last_product(st, name, it):
            return name == "M3" and isinstance(it, int) and it == ST[st].iters - 1

        def product(eng, st, name, it):
            p = int(name[1])
            j = sum(CHUNKS1[:int(st[4])]) + it * 2 + p // 2
            dst = tile_of(aS, it * 2 + p // 2)
            o = og[:, p // 2, :]
            eng.wait_ge(gelu_done, j + 1)
            eng.wait_ge(conv_step, 3 * (2 * j + 2))
            if last_product(st, name, it):
                eng.wait_ge(a_ready, 16 + j)
            eng.tensor_tensor(o, cv[p - 1], cv[p], ALU.mult).then_inc(u_used, 1)
            eng.wait_ge(u_used, j + 1)
            eng.tensor_copy(dst[:, 0:T], o).then_inc(u_done, 1)
            eng.wait_ge(u_done, j + 1)
            eng.tensor_tensor(dst[:, T:], o, dst[:, 0:T].bitcast(F32), ALU.subtract).then_inc(a_ready, 1)

        def fold(eng, n, first, last):
            for i in range(first, last):
                if i:
                    eng.wait_ge(nfold, FOLD_BASE[n] + i)
                if i < 3:
                    eng.wait_ge(nsq, 4 * (n // 2 - 1 if n else 0) + i + 2)
                    dst, src = y[:, 0:4, :], y[:, 4 * i + 4:4 * i + 8, :]
                else:
                    h = 2 if i == 3 else 1
                    dst, src = y[:, 0:h, :], y[:, h:2 * h, :]
                eng.tensor_tensor(dst, dst, src, ALU.add).then_inc(nfold, 1)

        STEPS = {
            "in1": [("P1", 1, 2), ("P2", 2, 2), ("P3", 3, 2),
                    ("S1", 0, 1), ("T0", 0, 1), ("E1", 0, 1), ("V", 1, 1), ("D1", 1, 1), ("O0", 1, 1),
                    ("R0", 1, 0), ("S0", 2, 0), ("T1", 2, 1), ("E0", 2, 0), ("D0", 3, 0), ("R1", 3, 0),
                    ("O1", 3, 1)],
            "in2": [("Q0", 2, 0), ("N0", 4, 0), ("Q1", 5, 0), ("B0", 5, 0), ("S0", 6, 0), ("N1", 7, 0),
                    ("Q2", 8, 0), ("B1", 8, 0), ("S1", 9, 0), ("N2", 10, 0), ("Q3", 11, 0),
                    ("B2", 11, 0), ("S2", 12, 0), ("N3", 13, 0), ("DA", 13, 0), ("B3", 14, 0), ("Q4", 14, 0), ("TA", 14, 0),
                    ("S3", 0, 1), ("D3", 1, 1), ("N4", 1, 1), ("OA", 1, 1), ("B4", 2, 1), ("T3", 2, 1),
                    ("O3", 3, 1), ("S4", 3, 1), ("D4", 4, 1), ("T4", 5, 1), ("O4", 6, 1)],
        }
        CARRIED = {
            "out1": ("in1", {0: ("S1", "T0", "E1", "V"), 0.5: ("D1", "O0"), 1: ("sums1", "T1"), 1.5: ("spread1", "O1"),
                             2: ("sums2",), 2.5: ("spread2",)}),
            "mix2": ("in2", {0: ("S3",), 0.5: ("D3", "N4", "OA"), 1: ("B4", "T3"), 1.5: ("O3", "S4", "D4"),
                             2: ("T4",), 2.5: ("O4",)})}
        for _n in [s.name for s in stages if s.name.startswith("up")]:
            STEPS[_n] = [("X0", 1, 0), ("X1", 2, 0), ("F0", 2, 0), ("X2", 3, 0), ("F1", 3, 0), ("G0", 3, 0),
                         ("X3", 0, 1), ("F2", 0, 1), ("M1", 0, 1), ("F3", 1, 1), ("G2", 1, 1), ("M3", 2, 1)
                         ] if _n[2] == "1" else [("F0", 2, 0), ("F1", 3, 0), ("F2", 0, 1), ("F3", 1, 1)]
        STEPS["out1"] = [("Y0", 3, 0), ("Y1", 5, 0), ("Y2", 7, 0), ("Y3", 1, 1)]
        STEPS[f"dn1_{len(CHUNKS1) - 1}"] = [("Y0", 2, 0), ("Y1", 3, 0), ("Y2", 0, 1), ("Y3", 1, 1)]
        STEPS["out2"] = [(a + s[1], p, w) for s, p, w in STEPS[f"dn1_{len(CHUNKS1) - 1}"] for a in "YH"]

        def carried(engine, st, it, pos, step):
            if st.name in CARRIED and isinstance(it, int) and it == 0:
                source, steps = CARRIED[st.name]
                stage_of[engine] = source
                for name in steps.get(pos, ()):
                    step(name, ST[source].iters - 1)
                stage_of[engine] = st.name

        def run_stage(eng, st, step, mtile, carry=True):
            steps = STEPS.get(st.name, [])
            wraps = any(w == 1 for _, _, w in steps)

            def body(it, first, last):
                for p in range(st.nm):
                    for name, pos, wrap in steps:
                        if pos == p and (wrap == 0 or (wrap == 1 and not first) or (wrap == 2 and first)):
                            step(name, it - 1 if wrap == 1 else it)
                    mtile(st, it, p, last)

            n = st.iters
            lo = 0
            if wraps or n == 1 or st.name == "mix2":
                body(0, True, n == 1)
                lo = 1
            if n - 1 > lo:
                with eng.Fori(lo, n - 1) as it:
                    body(it, False, False)
            if n > 1:
                body(n - 1, False, True)
            for name, pos, wrap in sorted(steps, key=lambda s: s[1]):
                if wrap == 1 and not (carry and st.name in ("in1", "in2")):
                    step(name, n - 1)

        block = ctx.enter_context(nc.Block())

        @block.sync
        def _(sp):
            def load(st, it, k, halves=(0, 1)):
                for half in halves:
                    h = 2 * st.u(it, k) + half
                    slot = (2 * (st.ubase + k) + half) % RAW_SLOTS
                    a, b = (0, st.half) if half == 0 else (st.half, st.blocks)
                    if not (isinstance(it, int) and 2 * st.u(it, k) + half < RAW_SLOTS):
                        sp.wait_ge(lo_done, h - (RAW_SLOTS - 1))
                    row = it * st.units + k
                    src = dram[st.name]
                    src = src[row] if isinstance(row, int) else src[bass.ds(row, 1)].rearrange("a p c -> (a p) c")
                    sp.dma_start(raw[:, slot, 0:(b - a) * P], src[:, a * P:b * P]).then_inc(landed[slot], 16)

            def load_bands(it, slots):
                for s in slots:
                    head = A_SLOTS * s + it if s < 3 else A_HEADS + 2 * it + s - 3
                    src = bass.AP(bias_rows.tensor, head * N_DIST, [[1, P], [1, T]])
                    sp.dma_start(bias5[:, s, :], src).then_inc(bias_in[s], 16)

            def load_x(j):
                sp.dma_start(x[:, 4 * j:4 * j + 4, :], xT_d[:, 4 * j:4 * j + 4, :]).then_inc(x_in[j], 16)

            m0 = CS["causal"]
            sp.dma_start(pv[:, :], pv_d).then_inc(gains_in, 16)
            load_x(0)
            load_x(1)
            load(stages[0], 0, 0, (0,))
            load_x(2)
            load(stages[0], 0, 0, (1,))
            load_x(3)
            sp.dma_start(cs[:, 0:m0], cs_d[:, 0:m0]).then_inc(const_in, 16)

            for st in stages:
                if st.name == "out1":
                    sp.wait_ge(rows_in_sb, 1)
                    sp.dma_start(bias_rows, bias5[0:A_HEADS + B_HEADS, :, :].rearrange(
                        "h a b -> h (a b)")[:, 0:N_DIST]).then_inc(rows_out, 16)
                    sp.wait_ge(rows_out, 16)

                def one(it):
                    if st.name == "in2":
                        if it:
                            sp.wait_ge(bias_used, 5 * (it - 1) + 3)
                        load_bands(it, range(3))
                    for k in range(1 if st.name == "pre" else 0, st.units):
                        if st.name == "in2" and k == 10:
                            if it:
                                sp.wait_ge(bias_used, 5 * it)
                            load_bands(it, range(3, 5))
                        load(st, it, k)

                if st.iters == 1 or st.name == "in2":
                    for i in range(st.iters):
                        one(i)
                    if st.name == "pre":
                        sp.dma_start(cs[:, m0:], cs_d[:, m0:]).then_inc(masks_in, 16)
                        sp.dma_start(tab[:, :], dram["tab"]).then_inc(masks_in, 16)
                else:
                    with sp.Fori(0, st.iters) as it:
                        one(it)
            for m in range(KT):
                sp.wait_ge(x_done, m + 1)
                sp.dma_start(out_d[:, m, :], x[:, m, :]).then_inc(stored, 16)
            sp.wait_ge(stored, 16 * KT)

        EARLY_TILES = {2: range(0, 10), 3: range(10, 14)}
        LAST_TILES = range(14, KT)
        A_BASE = {}
        n_a = 2 * 8
        for c, n in enumerate(CHUNKS1):
            A_BASE[f"up1_{c}"] = n_a
            n_a += n
        A_BASE["in2"] = n_a
        n_a += A_SLOTS + B_HEADS
        for c in range(F2T // KT):
            A_BASE[f"up2_{c}"] = n_a
            n_a += KT
        last1, last2 = f"dn1_{len(CHUNKS1) - 1}", f"dn2_{F2T // KT - 1}"
        NORMS = [("x", D), (0, N_SWA * HD1), (1, N_FOX * HD1), (0, D), ("x", D), (0, D), ("x", D), (0, D)]

        def w0(v):
            return not isinstance(v, int) or v > 0

        @block.tensor
        def _(pe):
            def mm(o, w, m, start, stop):
                return pe.matmul(o, w, m, start=start, stop=stop, skip_group_check=False)

            def wide_start(st):
                for p in range(2):
                    if st.g(0, p) > 1:
                        pe.wait_ge(ev_done, st.g(0, p) - 1)
                for kk in range(KT):
                    pe.wait_ge(h_ready, KT * FILL[st.name] + kk + 1)
                    act = input_of(st, 0)[:, kk, :]
                    for p in range(WIDE):
                        flat = st.start[p] + kk
                        k, within = flat // st.blocks, flat % st.blocks
                        slot = (st.ubase + k) % W_SLOTS
                        if within in (0, st.half):
                            pe.wait_ge(lo_done, 2 * st.u(0, k) + (1 if within == 0 else 2))
                        bank = accumulator(st, 0, p)
                        h_w, l_w = (w[:, slot, within * P:(within + 1) * P] for w in (whi, wlo))
                        if kk < KT - 1:
                            one = mm(bank[:, :], h_w, act, kk == 0, False)
                            mm(bank[:, T:], l_w, act[:, 0:T], False, False)
                            if kk == 0 and p == 0 and st.prev:
                                one.then_inc(unit_used, 1)
                        else:
                            one = mm(bank[:, T:], l_w, act[:, 0:T], False, False)
                            mm(bank[:, :], h_w, act, False, True).then_inc(mt_done, 1)
                            if p:
                                one.then_inc(unit_used, 1)

            def mtile(st, it, p, last):
                if is_wide(st, it) and p < WIDE:
                    if p == 0:
                        wide_start(st)
                        norm_sums(NORM_IN[st.name])
                    return
                carried("pe", st, it, p, step)
                g = st.g(it, p)
                acc_bank = accumulator(st, it, p)
                X = input_of(st, p)
                first_block = {("out1", 1): 8, ("mix2", 3): A_SLOTS}.get((st.name, p % 2 if st.name == "out1" else p), 0)
                f = g - 1
                if st.name == "in2" and p == st.nm - 1 and w0(it):
                    pe.wait_ge(a_ready, A_BASE["in2"] + 3 * it)
                if st.name == "pre" and p == 2:
                    f = 0
                if st.name == "mix2":
                    f = g - 3 if not isinstance(it, int) or it else (f if p < 2 else 0)
                if w0(f) and not (is_wide(st, it) and p == WIDE):
                    pe.wait_ge(ev_done, f)
                n = st.mtiles[p]
                spreads = st.name in NORM_IN and isinstance(it, int) and it == 0 and p == (WIDE if st.wide else 2)
                for kk in range(n):
                    if kk == n // 2:
                        carried("pe", st, it, p + 0.5, step)
                    if st.name == "pre" and p == 2 and kk == 8:
                        norm_sums(NORM_IN["pre"])
                    if spreads and kk == (4 if st.wide else 13):
                        norm_spread(NORM_IN[st.name])
                    flat = st.start[p] + kk
                    k, within = flat // st.blocks, flat % st.blocks
                    slot = (st.ubase + k) % W_SLOTS
                    if within in (0, st.half):
                        pe.wait_ge(lo_done, 2 * st.u(it, k) + (1 if within == 0 else 2))
                    if p == 0 and st.name in FILL and FILL[st.name] is not None:
                        pe.wait_ge(h_ready, KT * FILL[st.name] + kk + 1)
                    if st.name[:2] == "dn" and p == 0:
                        pe.wait_ge(a_ready, A_BASE["up" + st.name[2:]] + kk + 1)
                    if kk == 0 and (st.name, p) in (("mix2", 2), ("mix2", 3)):
                        pe.wait_ge(a_ready, A_BASE["in2"] + A_SLOTS + B_HEADS - (2 if p == 2 else 0))
                    if st.name == "out1" and p < 2 and kk in (0, n - 1):
                        pe.wait_ge(a_ready, 14 if kk == 0 else 15 + p)
                    act = X[:, first_block + kk, :]
                    h_w, l_w = (w[:, slot, within * P:(within + 1) * P] for w in (whi, wlo))
                    if kk < n - 1:
                        one = mm(acc_bank[:, :], h_w, act, kk == 0, False)
                        mm(acc_bank[:, T:], l_w, act[:, 0:T], False, False)
                    else:
                        one = mm(acc_bank[:, T:], l_w, act[:, 0:T], False, False)
                        end = mm(acc_bank[:, :], h_w, act, False, True)
                        end.then_inc(mt_done, 1)
                    if kk == 0 and p == WIDE if is_wide(st, it) and k < W_SLOTS else within == 0 and (st.prev or k):
                        one.then_inc(unit_used, 1)


            def norm_sums(n):
                src, _ = NORMS[n]
                if n == 0:
                    pe.wait_ge(const_in, 16)
                pe.wait_ge(*ACC_DONE[n])
                split_sum = n in (3, 5, 7)
                for c in range(2):
                    total = y[:, 0, c * P:(c + 1) * P] if src == "x" else acc[:, src, c * P:(c + 1) * P]
                    end = mm(SB[4 * c][:, 0:1], total, ones[:, 0:1], True, not split_sum)
                if split_sum:
                    pe.wait_ge(sqy, KT * ((n - 1) // 2))
                    for c in range(2):
                        end = mm(SB[4 * c][:, 0:1], sq2[:, c * P:(c + 1) * P], ones[:, 0:1], False, True)
                end.then_inc(nsum, 1)

            def norm_spread(n):
                pe.wait_ge(npow, n + 1)
                if n:
                    pe.wait_ge(ncopy, n)
                for c in range(2):
                    end = mm(SB[1][:, c * P:(c + 1) * P], rs[:, c:c + 1].to_broadcast([P, P]), ident, True, True)
                end.then_inc(nbc, 1)

            def scores(b, it):
                q = 2 * it + b
                pe.wait_ge(ev_done, ST["in1"].g(it, 0 if b == 0 else 2) + 1)
                if b == 1:
                    pe.wait_ge(pos_done, q + 1)
                if w0(q - 1):
                    pe.wait_ge(t_copy, q - 1)
                qt, kt = (q_swa, k_swa) if b == 0 else (q_fox, k_fox)
                for par_ in range(2):
                    at = slice(64 * par_, 64 * par_ + 64)
                    bank = SB[2 * b + par_]
                    for o, qs, nk in ((bank[:, 0:P], slice(0, P), P), (bank[:, P:P + T], slice(P, T), T)):
                        end = mm(o, qt[at, qs], kt[at, 0:nk], True, b == 0)
                        if b == 1:
                            end = mm(o, l_fox[at, qs], r_fox[at, 0:nk], False, True)
                end.then_inc(s_mm, 1)

            def turn(bank, pr):
                for a in range(3):
                    end = pe.transpose(bank[:, a * P:(a + 1) * P], pr[:, a * P:(a + 1) * P], ident)
                return end

            def step(name, it):
                if name[:4] == "sums":
                    norm_sums(int(name[4]))
                elif name[:6] == "spread":
                    norm_spread(int(name[6]))
                elif name == "P1":
                    pe.wait_ge(rows_in_sb, 1)
                    pe.wait_ge(ev_done, ST["pre"].g(0, 1) + 1)
                    for c in range(2):
                        end = pe.transpose(SB[4][:, c * P:(c + 1) * P], vT[:, c * P:(c + 1) * P], ident)
                    end.then_inc(v_mm, 1)
                elif name == "P2":
                    pe.wait_ge(z_c, 6)
                    pe.wait_ge(v_copy, 1)
                    for c in range(2):
                        end = pe.transpose(SB[4][:, c * P:(c + 1) * P], sq[:, T + c * P:T + (c + 1) * P], ident)
                    end.then_inc(lf_mm, 1)
                elif name == "P3":
                    pe.wait_ge(lf_copy, 1)
                    mm(SB[4][:, 0:P], og[:, 0, 0:P], triu, True, True)
                    mm(SB[4][:, P:T], og[:, 0, 0:P], ones, True, False)
                    mm(SB[4][:, P:T], og[:, 0, P:T], triu, False, True).then_inc(c_mm, 1)
                elif name in ("S0", "S1") and stage_of["pe"] == "in1":
                    scores(int(name[1]), it)
                elif name == "V":
                    pe.wait_ge(ev_done, ST["in1"].g(it, 3) + 1)
                    pe.wait_ge(c_done, 1)
                    pe.wait_ge(v_copy, it + 1)
                    for c in range(2):
                        end = pe.transpose(SB[4][:, c * P:(c + 1) * P], vT[:, c * P:(c + 1) * P], ident)
                    end.then_inc(v_mm, 1)
                elif name in ("T0", "T1"):
                    b = int(name[1])
                    pe.wait_ge(s_norm, 2 * it + b + 1)
                    for s in (2 * b, 2 * b + 1):
                        end = turn(SB[s], probs[s])
                    end.then_inc(t_mm, 1)
                elif name in ("O0", "O1"):
                    b = int(name[1])
                    q = 2 * it + b
                    pe.wait_ge(t_copy, q + 1)
                    pe.wait_ge(v_copy, 1 if b == 0 else it + 2)
                    if w0(q):
                        pe.wait_ge(o_sq, q)
                    for par_ in range(2):
                        at = slice(64 * par_, 64 * par_ + 64)
                        pt = probsT[2 * b + par_]
                        mm(MB[at, 0:T], vN[:, b, 0, at], pt[:, 0:T], True, False)
                        end = mm(MB[at, P:T], vN[:, b, 1, at], pt[:, T:T + P], False, True)
                    end.then_inc(o_mm, 1)
                elif name[0] == "N":
                    s = int(name[1])
                    h = 5 * it + s
                    pe.wait_ge(hn_sq, h + 1)
                    pe.wait_ge(ev_done, ST["in2"].g(it, 3 * s + 2) + 1)
                    if w0(it):
                        pe.wait_ge(copied2, 3 * (it - 1) + max(0, s - 2) + 1)
                    for c in range(4):
                        mm(SB[s][:, c:c + 1], sq[:, c * P:(c + 1) * P], ones[:, 0:1], True, True)
                    for c in range(2):
                        end = pe.transpose(SB[s][:, (1 + c) * P:(2 + c) * P], vT[:, c * P:(c + 1) * P], ident)
                    end.then_inc(hn_mm, 1)
                elif name[0] == "B":
                    s = int(name[1])
                    pe.wait_ge(hn_pow, 5 * it + s + 1)
                    for c in range(4):
                        end = mm(SB[s][:, c * P:(c + 1) * P], rs5[:, s, c:c + 1].to_broadcast([P, P]), ident, True, True)
                    end.then_inc(hn_bc, 1)
                elif name[0] == "S":
                    s = int(name[1])
                    pe.wait_ge(hn_done, 5 * it + s + 1)
                    mm(SB[s][:, 0:P], qk[s][:, 0:P], qk[s][:, T:T + P], True, True)
                    mm(SB[s][:, P:P + T], qk[s][:, P:T], qk[s][:, T:2 * T], True, True).then_inc(scores2, 1)
                elif name[0] == "T":
                    b, ss = GROUP[name[1]]
                    pe.wait_ge(probs2, 3 * it + b + 1)
                    for s in ss:
                        end = turn(SB[s], probs[s])
                    end.then_inc(turned2, 1)
                elif name[0] == "O":
                    b, ss = GROUP[name[1]]
                    q = 3 * it + b
                    pe.wait_ge(copied2, q + 1)
                    pe.wait_ge(a_ready, A_BASE["in2"] + q)
                    if b == 0:
                        pe.wait_ge(ev_done, ST["in2"].g(it, 14) + 1)
                    for s in ss:
                        mm(MB[:, 0:T], vN[:, s, 0, :], probsT[s][:, 0:T], s == ss[0], False)
                        end = mm(MB[:, P:T], vN[:, s, 1, :], probsT[s][:, T:T + P], False, s == ss[-1])
                    end.then_inc(outputs2, 1)

            for st in stages:
                for n in NORM_BEFORE.get(st.name, ()):
                    norm_sums(n)
                    norm_spread(n)
                if st.name == "in1":
                    pe.wait_ge(masks_in, 32)
                    mm(SB[4][0:A_HEADS + B_HEADS, 0:N_DIST], tab[0:N_BUCKETS + 4, 0:A_HEADS + B_HEADS],
                       tab[0:N_BUCKETS + 4, A_HEADS + B_HEADS:], True, True).then_inc(rows_ps, 1)
                stage_of["pe"] = st.name
                run_stage(pe, st, step, mtile)

        @block.scalar
        def _(act):
            def split(st, it, k, halves=(0, 1)):
                slot = (st.ubase + k) % W_SLOTS
                u = st.u(it, k)
                if w0(u - W_SLOTS + 1) and not (isinstance(it, int) and u < W_SLOTS):
                    act.wait_ge(unit_used, u - W_SLOTS + 1)
                for half in halves:
                    h0 = 2 * (st.ubase + k) + half
                    a, b = (0, st.half) if half == 0 else (st.half, st.blocks)
                    act.wait_ge(landed[h0 % RAW_SLOTS],
                                16 * (h0 // RAW_SLOTS + 1) + it * (16 * 2 * st.units // RAW_SLOTS))
                    act.activation(whi[:, slot, a * P:b * P], raw[:, h0 % RAW_SLOTS, 0:(b - a) * P],
                                   ACT.Copy).then_inc(hi_done, 1)

            def splits(st, it, p, last):
                for v in st.splits(p):
                    if v < st.units:
                        split(st, it, v)
                    elif not last:
                        split(st, it + 1, v - st.units)
                    elif st.next:
                        split(st.next, 0, v - st.units)

            def mtile(st, it, p, last):
                carried("act", st, it, p, step)
                when = splits_when(st, it, p, last)
                if when == "before":
                    splits(st, it, p, last)
                carried("act", st, it, p + 0.5, step)
                if st.name in NORM_IN and isinstance(it, int) and it == 0 and p == (1 if st.wide else 2):
                    spread(NORM_IN[st.name])
                if st.name == "mix2" and last and p in EARLY_TILES:
                    act.wait_ge(mt_done, st.g(it, 1) + 1)
                    fill_mixed(EARLY_TILES[p])
                g = st.g(it, p)
                act.wait_ge(mt_done, g + 1)
                if w0(g - 1):
                    act.wait_ge(ev_done, g - 1)
                scale = HD1 ** -0.5 if st.name == "in1" and p < 2 else 1.0
                act.activation(tmp[:, st.bank(p), :], accumulator(st, it, p)[:, T:], ACT.Copy, scale=scale).then_inc(tmp_done, 1)
                if when == "after":
                    if (st.name, p) == ("out1", 1):
                        splits(st, it, 0, last)
                    splits(st, it, p, last)
                if st.name == "pre" and p == 2:
                    act.wait_ge(z_c, 2)
                    act.activation(sq2[:, :], sq2[:, :], ACT.Exp).then_inc(z_c, 1)
                    act.wait_ge(z_c, 3)
                    act.activation(sq2[:, :], sq2[:, :], ACT.Ln, bias=1.0).then_inc(z_c, 1)
                if st.name == "mix2" and p < 2:
                    act.wait_ge(ev_done, g + 1)
                    act.activation(og[:, p, :], og[:, p, :], ACT.Sigmoid).then_inc(sig_done, 1)

            def exps(slots, nms_):
                for s, m in zip(slots, nms_):
                    for n, cols in ((0, slice(0, P)), (1, slice(P, P + T))):
                        end = act.activation(probs[s][:, cols], probs[s][:, cols], ACT.Exp, bias=nm[:, m, n:n + 1],
                                             accum_out=den[:, s, n:n + 1])
                return end

            def scales(slots, nms_):
                for s, m in zip(slots, nms_):
                    for n, cols in ((0, slice(0, P)), (1, slice(P, P + T))):
                        end = act.activation(probs[s][:, cols], probs[s][:, cols], ACT.Copy, scale=rden[:, m, n:n + 1])
                return end

            def step(name, it):
                if name[:6] == "spread":
                    spread(int(name[6]))
                elif name[0] == "Y":
                    stage = stage_of["act"]
                    m = it * 4 + int(name[1])
                    i = m + KT * {"out1": 0, last1: 1, "out2": 2}[stage]
                    if stage == "out2":
                        act.wait_ge(x_added, m + 1)
                    else:
                        act.wait_ge(y_step, 3 * (m + 1) if stage == "out1" else m + (len(CHUNKS1) + 1) * KT + 1)
                    added = i - {"out1": 0, last1: 1, "out2": 2}[stage]
                    if w0(added):
                        act.wait_ge(sqa, added)
                    act.activation(sq2[:, :], tile_of(x if stage == "out2" else y, m), ACT.Square).then_inc(sqy, 1)
                    if stage != "out2":
                        act.activation(tile_of(y, m), tile_of(y, m), ACT.Copy,
                                       scale=par("post_mix" if stage == "out1" else "post_ffn", m)).then_inc(yg, 1)
                elif name[0] == "H":
                    m = it * 4 + int(name[1])
                    act.wait_ge(x_added, m + 1)
                    act.activation(tile_of(aS, m)[:, 0:T], tile_of(x, m), ACT.Copy, scale=par("g_mlp2", m)).then_inc(h_hi, 1)
                elif name[0] == "F":
                    if stage_of["act"][:3] == "up2":
                        p = int(name[1])
                        i = KT * int(stage_of["act"][4]) + it * 4 + p
                        act.wait_ge(r_done, i + 1)
                        act.activation(tile_of(hS, it * 4 + p)[:, 0:T], cv[p], ACT.Copy).then_inc(a_hi, 1)
                elif name == "P1":
                    act.wait_ge(v_mm, 1)
                    act.activation(vN[:, 0, :, :].rearrange("p a b -> p (a b)"), SB[4][:, 0:T], ACT.Copy).then_inc(v_copy, 1)
                elif name == "V":
                    act.wait_ge(v_mm, it + 2)
                    act.activation(vN[:, 1, :, :].rearrange("p a b -> p (a b)"), SB[4][:, 0:T], ACT.Copy).then_inc(v_copy, 1)
                elif stage_of["act"] == "in1" and name[0] == "S":
                    b = int(name[1])
                    q = 2 * it + b
                    act.wait_ge(s_nm, q + 1)
                    if b == 0:
                        for j in range(2):
                            act.activation(esk[:, j, :], nm[:, j, :], ACT.Exp, bias=par("sinks", 8 * j + it))
                    exps((2 * b, 2 * b + 1), (2 * b, 2 * b + 1)).then_inc(s_exp, 1)
                elif stage_of["act"] == "in1" and name[0] == "D":
                    b = int(name[1])
                    act.wait_ge(s_rden, 2 * it + b + 1)
                    scales((2 * b, 2 * b + 1), (2 * b, 2 * b + 1)).then_inc(s_norm, 1)
                elif stage_of["act"] == "in1" and name[0] == "O":
                    b = int(name[1])
                    q = 2 * it + b
                    act.wait_ge(og_done, q + 1)
                    if w0(q):
                        act.wait_ge(o_acc, q)
                    act.activation(sq2[:, :], MB[:, 0:T], ACT.Square).then_inc(o_sq, 1)
                    act.activation(tile_of(aS, 8 * b + it)[:, 0:T], og[:, b, :], ACT.Copy).then_inc(a_hi, 1)
                elif name[0] == "G":
                    p = int(name[1])
                    c = int(stage_of["act"][4])
                    i = 2 * sum(CHUNKS1[:c]) + it * 4 + p
                    act.wait_ge(conv_step, 3 * i + 3)
                    act.activation(cv[p], cv[p], ACT.Gelu_apprx_tanh).then_inc(gelu_done, 1)
                elif name[0] == "Q":
                    s = int(name[1])
                    h = 5 * it + s
                    act.wait_ge(ev_done, ST["in2"].g(it, 3 * s + 1) + 1)
                    if w0(h):
                        act.wait_ge(hn_mm, h)
                    act.activation(sq[:, :], qk[s], ACT.Square).then_inc(hn_sq, 1)
                elif name[0] == "N":
                    s = int(name[1])
                    act.wait_ge(hn_mm, 5 * it + s + 1)
                    act.activation(vN[:, s, :, :].rearrange("p a b -> p (a b)"), SB[s][:, P:P + T], ACT.Copy).then_inc(hn_v, 1)
                elif name in ("S2", "S3", "S4"):
                    b, ss = GROUP["A" if name == "S2" else name[1]]
                    act.wait_ge(maxima2, 3 * it + b + 1)
                    exps(ss, [ss[0]] * len(ss)).then_inc(exps2, 1)
                elif name[0] == "D":
                    b, ss = GROUP[name[1]]
                    act.wait_ge(recips2, 3 * it + b + 1)
                    scales(ss, [ss[0]] * len(ss)).then_inc(probs2, 1)
                elif name[0] == "O":
                    b, ss = GROUP[name[1]]
                    act.wait_ge(outputs2, 3 * it + b + 1)
                    act.activation(tile_of(aS, it if b == 0 else A_SLOTS + 2 * it + b - 1)[:, 0:T], MB[:, 0:T],
                                   ACT.Copy).then_inc(a_hi, 1)

            def spread(n):
                src, _ = NORMS[n]
                act.wait_ge(nbc, n + 1)
                act.activation(rsb[:, src if n in (1, 2) else 0, :], SB[1][:, 0:T], ACT.Copy).then_inc(ncopy, 1)

            def norm(n):
                spread(n)

            def fill_x(f, n):
                def leading(j):
                    for t in range(4 * j, 4 * j + 4):
                        wait_x(act, n, t)
                        act.activation(hS[:, t, 0:T], x[:, t, :], ACT.Copy, scale=par(GAIN[f], t)).then_inc(h_hi, 1)

                def squares(j):
                    act.activation(y[:, 4 * j:4 * j + 4, :], x[:, 4 * j:4 * j + 4, :], ACT.Square).then_inc(nsq, 1)

                if f == 0:
                    act.wait_ge(gains_in, 16)
                    for j in range(4):
                        if j >= 2:
                            split(stages[0], 0, 0, (j - 2,))
                        leading(j)
                    squares(0)
                    squares(1)
                    split(stages[0], 0, 1)
                    squares(2)
                    squares(3)
                    split(stages[0], 0, 2)
                else:
                    for j in range(4):
                        leading(j)
                        squares(j)

            def fill_mixed(tiles):
                for t in tiles:
                    act.wait_ge(mixed_done, t + 1)
                    act.activation(hS[:, t, 0:T], y[:, t, :], ACT.Copy).then_inc(h_hi, 1)

            act.wait_ge(half_set, 1)
            act.activation(warm[:, :], nhalf[:, 0:1], ACT.Copy)
            for st in stages:
                for n in NORM_BEFORE.get(st.name, ()):
                    norm(n)
                if st.name in ("pre", "up1_0", "in2"):
                    fill_x(FILL[st.name], NORM_IN[st.name])
                if st.name == "out2":
                    fill_mixed(LAST_TILES)
                    splits(ST["mix2"], KT - 1, 2, True)
                    splits(ST["mix2"], KT - 1, 3, True)
                if st.name == "in1":
                    act.wait_ge(rows_ps, 1)
                    act.activation(bias5[0:A_HEADS + B_HEADS, :, :].rearrange("h a b -> h (a b)")[:, 0:N_DIST],
                                   SB[4][0:A_HEADS + B_HEADS, 0:N_DIST], ACT.Copy).then_inc(rows_in_sb, 1)
                stage_of["act"] = st.name
                run_stage(act, st, step, mtile)

        @block.vector
        def _(dve):
            def split(st, it, k, halves=(0, 1)):
                slot = (st.ubase + k) % W_SLOTS
                for half in halves:
                    h0 = 2 * (st.ubase + k) + half
                    a, b = (0, st.half) if half == 0 else (st.half, st.blocks)
                    dve.wait_ge(hi_done, 2 * st.u(it, k) + half + 1)
                    dve.tensor_tensor(wlo[:, slot, a * P:b * P], raw[:, h0 % RAW_SLOTS, 0:(b - a) * P],
                                      whi[:, slot, a * P:b * P].bitcast(F32), ALU.subtract).then_inc(lo_done, 1)

            def splits(st, it, p, last):
                for v in st.splits(p):
                    if v < st.units:
                        split(st, it, v)
                    elif not last:
                        split(st, it + 1, v - st.units)
                    elif st.next:
                        split(st.next, 0, v - st.units)

            def mtile(st, it, p, last):
                if st.name != "out1" or p == 0:
                    carried("dve", st, it, p, step)
                when = splits_when(st, it, p, last)
                first = st.name in NORM_IN and isinstance(it, int) and it == 0
                if when == "before" and not (first and (p == 1 or p == 0 and st.name in ("pre", "in2"))):
                    splits(st, it, p, last)
                carried("dve", st, it, p + 0.5, step)
                if st.name == "out1":
                    carried("dve", st, it, p + 1, step)
                if first and p == 0:
                    norm(NORM_IN[st.name])
                    splits(st, it, 0 if st.name == "pre" else 1, last)
                if st.name == "mix2" and last and p in EARLY_TILES:
                    dve.wait_ge(mt_done, st.g(it, 1) + 1)
                    fill_mixed(EARLY_TILES[p])
                read_out(st, it, p)
                if when == "after":
                    if (st.name, p) == ("out1", 1):
                        splits(st, it, 0, last)
                    splits(st, it, p, last)

            def read_out(st, it, p):
                g = st.g(it, p)
                A = accumulator(st, it, p)[:, 0:T]
                B = tmp[:, st.bank(p), :]
                dve.wait_ge(tmp_done, g + 1)

                def add_to(dest):
                    dve.tensor_tensor(dest, A, B, ALU.add).then_inc(ev_done, 1)

                def times_rms(dest):
                    if st.name in NORM_IN and isinstance(it, int) and it == 0 and p == 0:
                        dve.wait_ge(ncopy, NORM_IN[st.name] + 1)
                    dve.wait_ge(summed, it * st.scaled + (st.sbase + p + 1))
                    dve.tensor_tensor(dest, dest, rsb[:, 0, :], ALU.mult).then_inc(ev_done, 1)

                def scaled_to(dest):
                    dve.tensor_tensor(dest, A, B, ALU.add).then_inc(summed, 1)
                    times_rms(dest)

                def self_wait():
                    dve.wait_ge(ev_done, g + 1)

                name = st.name
                if name == "pre":
                    if p < 2:
                        scaled_to((k_swa, vT[:, :])[p])
                    else:
                        z, lf = sq[:, 0:T], sq[:, T:2 * T]
                        scaled_to(z)
                        self_wait()
                        dve.wait_ge(masks_in, 32)
                        dve.tensor_scalar(z, z, par("bf"), None, ALU.add).then_inc(z_c, 1)
                        dve.wait_ge(z_c, 1)
                        dve.scalar_tensor_tensor(sq2[:, :], z, -1.0, z, ALU.mult, ALU.min).then_inc(z_c, 1)
                        dve.wait_ge(z_c, 4)
                        dve.scalar_tensor_tensor(lf, z, 0.0, sq2[:, :], ALU.min, ALU.subtract).then_inc(z_c, 1)
                        dve.wait_ge(z_c, 5)
                        dve.tensor_scalar(lf, lf, cst("sgn"), None, ALU.mult).then_inc(z_c, 1)
                elif name == "in1":
                    if p < 2:
                        dve.scalar_tensor_tensor((q_swa, q_fox)[p], A, HD1 ** -0.5, B, ALU.mult, ALU.add).then_inc(summed, 1)
                        times_rms((q_swa, q_fox)[p])
                    else:
                        scaled_to((k_fox, vT[:, :])[p - 2])
                elif name == "out1":
                    half = og[:, p % 2, :]
                    add_to(half)
                    self_wait()
                    m = it * 4 + p // 2
                    c = Chain(dve, y_step, 3, m)
                    c.n = p % 2
                    if isinstance(it, int) and it == 0 and p < 2:
                        dve.wait_ge(ncopy, p + 2)
                    c(dve.tensor_tensor(half, half, rsb[:, p % 2, :], ALU.mult))
                    if p % 2:
                        c(dve.tensor_tensor(tile_of(y, m), og[:, 0, :], og[:, 1, :], ALU.add))
                        c.end()
                elif name[:3] == "up1":
                    i = 2 * sum(CHUNKS1[:int(name[4])]) + it * 4 + p
                    if w0(i - 1):
                        dve.wait_ge(u_scaled, i - 1)
                    add_to(sq[:, p % 2 * T:(p % 2 + 1) * T])
                elif name[:3] == "dn1":
                    c = int(name[4])
                    m = it * 4 + p
                    if c == 0:
                        add_to(tile_of(y, m))
                    else:
                        add_to(og[:, p % 2, :])
                        self_wait()
                        i = 3 * KT + (c - 1) * KT + m
                        dve.tensor_tensor(tile_of(y, m), tile_of(y, m), og[:, p % 2, :], ALU.add).then_inc(y_step, 1)
                elif name == "in2":
                    s, part = divmod(p, 3)
                    scaled_to((qk[s][:, 0:T], qk[s][:, T:2 * T], vT[:, :])[part])
                elif name == "mix2":
                    if p < 2:
                        scaled_to(og[:, p, :])
                    else:
                        br = sq[:, (p - 2) * T:(p - 1) * T]
                        add_to(br)
                        self_wait()
                        dve.wait_ge(sig_done, 2 * it + p - 1)
                        c = Chain(dve, mix_c, 2, it)
                        c.n = p - 2
                        c(dve.tensor_tensor(br, br, og[:, p - 2, :], ALU.mult))
                        if p == 3:
                            dve.tensor_tensor(tile_of(y, it), sq[:, 0:T], sq[:, T:2 * T], ALU.add).then_inc(mixed_done, 1)
                elif name == "out2" or name[:3] == "dn2":
                    m = it * 4 + p
                    add_to(og[:, p % 2, :])
                    self_wait()
                    dve.tensor_tensor(tile_of(x, m), tile_of(x, m), og[:, p % 2, :], ALU.add).then_inc(
                        x_done if name == last2 else x_added, 1)
                elif name[:3] == "up2":
                    scaled_to(ub[p][:, 0:T])
                    self_wait()
                    dve.scalar_tensor_tensor(cv[p], ub[p][:, 0:T], 0.0, ub[p][:, 0:T], ALU.max, ALU.mult).then_inc(r_done, 1)

            def carry_waits(i):
                dve.memset(carrier[:, i:i + 1], 0.0)

            def logits(s, mask, bank):
                for n, o, m in ((0, slice(0, P), mask[:, P:T]), (1, slice(P, P + T), mask[:, 0:T])):
                    end = dve.tensor_tensor_reduce(probs[s][:, o], bank[:, o], m, 1.0, LOWEST, ALU.add, ALU.max,
                                                   mx[:, s, n:n + 1])
                return end

            def step(name, it):
                st = stage_of["dve"]
                if name[:4] == "sums":
                    norm(int(name[4]))
                    if name == "sums1":
                        dve.memset(acc[:, 0, :], 0.0).then_inc(prep, 1)
                        dve.wait_ge(prep, 2)
                elif name[0] == "H":
                    m = it * 4 + int(name[1])
                    low_part(tile_of(aS, m), m, 4)
                elif name == "P2":
                    dve.wait_ge(lf_mm, 1)
                    dve.tensor_copy(og[:, 0, :], SB[4][:, 0:T]).then_inc(lf_copy, 1)
                elif name == "P3":
                    dve.wait_ge(c_mm, 1)
                    dve.tensor_scalar(l_fox, SB[4][:, 0:T], cst("mA"), cst("cA"), ALU.mult, ALU.add)
                    dve.tensor_scalar(b_fox, SB[4][:, 0:T], cst("mB"), cst("cB"), ALU.mult, ALU.add).then_inc(c_done, 1)
                elif name == "R0":
                    for half in range(2):
                        o = CS["slope"] + 8 * half
                        col = cs[:, o + it:o + it + 1] if isinstance(it, int) else cs[:, bass.ds(it + o, 1)]
                        end = dve.scalar_tensor_tensor(bias_swa[half], cst("dist", T), col, cst("window", T),
                                                       ALU.mult, ALU.add)
                    end.then_inc(pos_done, 1)
                elif name == "R1":
                    o = CS["pick"]
                    col = cs[:, o + it:o + it + 1] if isinstance(it, int) else cs[:, bass.ds(it + o, 1)]
                    if isinstance(it, int) and it == 0:
                        dve.wait_ge(c_done, 1)
                    dve.tensor_scalar(r_fox, b_fox, col, None, ALU.mult).then_inc(pos_done, 1)
                elif st == "in1" and name[0] == "S":
                    b = int(name[1])
                    q = 2 * it + b
                    dve.wait_ge(s_mm, q + 1)
                    if b == 0:
                        dve.wait_ge(pos_done, q + 1)
                    carry_waits(b)
                    m0, m1 = bias_swa if b == 0 else (cst("causal", T), cst("causal", T))
                    c = Chain(dve, smax_c, 1, q)
                    logits(2 * b, m0, SB[2 * b])
                    c(logits(2 * b + 1, m1, SB[2 * b + 1]))
                    c.end()
                    for s in (2 * b, 2 * b + 1):
                        if b == 0:
                            k = 8 * s + it
                            ns = nsink[:, k:k + 1] if isinstance(k, int) else nsink[:, bass.ds(k, 1)]
                            end = dve.tensor_scalar(nm[:, s, :], mx[:, s, :], -1.0, ns, ALU.mult, ALU.min)
                        else:
                            end = dve.tensor_scalar(nm[:, s, :], mx[:, s, :], -1.0, None, ALU.mult)
                    end.then_inc(s_nm, 1)
                elif st == "in1" and name[0] == "E":
                    b = int(name[1])
                    q = 2 * it + b
                    ss = slice(2 * b, 2 * b + 2)
                    dve.wait_ge(s_exp, q + 1)
                    src = den
                    if b == 0:
                        dve.tensor_tensor(dsum[:, ss, :], den[:, ss, :], esk[:, :, :], ALU.add).then_inc(pre_c, 1)
                        dve.wait_ge(pre_c, it + 1)
                        src = dsum
                    dve.reciprocal(rden[:, ss, :], src[:, ss, :]).then_inc(s_rden, 1)
                elif name in ("T0", "T1"):
                    b = int(name[1])
                    dve.wait_ge(t_mm, 2 * it + b + 1)
                    dve.tensor_copy(probsT[2 * b], SB[2 * b][:, 0:384])
                    dve.tensor_copy(probsT[2 * b + 1], SB[2 * b + 1][:, 0:384]).then_inc(t_copy, 1)
                elif name in ("O0", "O1"):
                    b = int(name[1])
                    q = 2 * it + b
                    dve.wait_ge(o_mm, q + 1)
                    dve.tensor_scalar(og[:, b, :], MB[:, 0:T], par("grp", 8 * b + it), None, ALU.mult).then_inc(og_done, 1)
                    dve.wait_ge(o_sq, q + 1)
                    dve.tensor_tensor(acc[:, b, :], acc[:, b, :], sq2[:, :], ALU.add).then_inc(o_acc, 1)
                    dve.wait_ge(a_hi, q + 1)
                    dst = tile_of(aS, 8 * b + it)
                    dve.tensor_tensor(dst[:, T:], og[:, b, :], dst[:, 0:T].bitcast(F32), ALU.subtract).then_inc(a_ready, 1)
                elif name[0] == "M":
                    if last_product(st, name, it):
                        product(dve, st, name, it)
                elif name[0] == "F" and st[:3] == "up1":
                    p = int(name[1])
                    c0 = int(st[4])
                    first = 2 * sum(CHUNKS1[:c0])
                    i = first + it * 4 + p
                    c = Chain(dve, conv_step, 3, i)

                    def w(k):
                        return par("conv", (it * 4 + (first + p)) * 4 + k)

                    n_used = sum(CHUNKS1[:c0]) + it * 2 + p // 2 - 1
                    if w0(n_used):
                        dve.wait_ge(u_used, n_used)
                    dve.wait_ge(u_scaled, i + 1)
                    c(dve.tensor_scalar(cv[p], ub[p][:, 0:T], w(0), w(3), ALU.mult, ALU.add))
                    c(dve.scalar_tensor_tensor(cv[p], ub[p][:, 1:1 + T], w(1), cv[p], ALU.mult, ALU.add))
                    c(dve.scalar_tensor_tensor(cv[p], ub[p][:, 2:2 + T], w(2), cv[p], ALU.mult, ALU.add))
                    c.end()
                elif name[0] == "F":
                    p = int(name[1])
                    i = KT * int(st[4]) + it * 4 + p
                    dst = tile_of(hS, it * 4 + p)
                    dve.wait_ge(a_hi, ATTENTION_TILES + i + 1)
                    dve.tensor_tensor(dst[:, T:], cv[p], dst[:, 0:T].bitcast(F32), ALU.subtract).then_inc(a_ready, 1)
                elif name[0] == "N":
                    s = int(name[1])
                    h = 5 * it + s
                    dve.wait_ge(hn_v, h + 1)
                    dve.tensor_scalar(ms5[:, s, :], SB[s][:, 0:4], 1.0 / HD2, EPS, ALU.mult, ALU.add).then_inc(hn_ms, 1)
                elif name[0] == "B":
                    s = int(name[1])
                    dve.wait_ge(hn_bc, 5 * it + s + 1)
                    gq, gk = (gqs[:, 0:1], par("ka")) if s < 3 else (gqs[:, 1:2], par("kb"))
                    dve.scalar_tensor_tensor(qk[s][:, 0:T], qk[s][:, 0:T], gq, SB[s][:, 0:T], ALU.mult, ALU.mult)
                    dve.scalar_tensor_tensor(qk[s][:, T:], qk[s][:, T:], gk, SB[s][:, T:], ALU.mult, ALU.mult).then_inc(hn_done, 1)
                elif name[0] == "S":
                    s = int(name[1])
                    h = 5 * it + s
                    dve.wait_ge(scores2, h + 1)
                    dve.wait_ge(bias_in[s], 16 * it + 16)
                    carry_waits(s)
                    logits(s, bias5[:, s, ::-1], SB[s]).then_inc(bias_used, 1)
                    if s >= 2:
                        b, ss = GROUP["A" if s == 2 else str(s)]
                        q = 3 * it + b
                        dve.wait_ge(bias_used, h + 1)
                        src = mx[:, s, :]
                        if s == 2:
                            dve.tensor_reduce(mjoin[:, :], mx[:, 0:3, :].rearrange("p s n -> p n s"), AX.X, ALU.max).then_inc(join2, 1)
                            dve.wait_ge(join2, 2 * it + 1)
                            src = mjoin[:, :]
                        dve.tensor_scalar(nm[:, ss[0], :], src, -1.0, None, ALU.mult).then_inc(maxima2, 1)
                elif st == "in2" and name[0] == "D":
                    b, ss = GROUP[name[1]]
                    q = 3 * it + b
                    dve.wait_ge(exps2, q + 1)
                    src = den[:, ss[0], :]
                    if b == 0:
                        dve.tensor_reduce(dsum[:, 0, :], den[:, 0:3, :].rearrange("p s n -> p n s"), AX.X, ALU.add).then_inc(join2, 1)
                        dve.wait_ge(join2, 2 * it + 2)
                        src = dsum[:, 0, :]
                    dve.reciprocal(rden[:, ss[0], :], src).then_inc(recips2, 1)
                elif name[0] == "T":
                    b, ss = GROUP[name[1]]
                    dve.wait_ge(turned2, 3 * it + b + 1)
                    for s in ss:
                        end = dve.tensor_copy(probsT[s], SB[s][:, 0:384])
                    end.then_inc(copied2, 1)
                elif name[0] == "O":
                    b, ss = GROUP[name[1]]
                    q = 3 * it + b
                    dst = tile_of(aS, it if b == 0 else A_SLOTS + 2 * it + b - 1)
                    dve.wait_ge(a_hi, KT + q + 1)
                    dve.tensor_tensor(dst[:, T:], MB[:, 0:T], dst[:, 0:T].bitcast(F32), ALU.subtract).then_inc(a_ready, 1)

            def norm(n):
                _, width = NORMS[n]
                dve.wait_ge(nsum, n + 1)
                for c in range(2):
                    end = dve.tensor_scalar(ms[:, c:c + 1], SB[4 * c][:, 0:1], 1.0 / width, EPS, ALU.mult, ALU.add)
                end.then_inc(nms, 1)

            def low_part(dst, t, f):
                dve.wait_ge(h_hi, t + (KT * f + 1))
                dve.scalar_tensor_tensor(dst[:, T:], tile_of(x, t), par(GAIN[f], t), dst[:, 0:T].bitcast(F32),
                                         ALU.mult, ALU.subtract).then_inc(h_ready, 1)

            def fill_x(f, n):
                if n:
                    dve.wait_ge(ncopy, n)
                    dve.wait_ge(yg, KT * (n // 2 - 1))
                    c = Chain(dve, res_dve, 6, n // 2 - 2)
                for j in range(4):
                    if f == 0 and j >= 2:
                        split(stages[0], 0, 0, (j - 2,))
                    for t in range(4 * j, 4 * j + 4):
                        if n and RESIDUAL.get(t, (0, ""))[1] == "dve":
                            residual(dve, c, t)
                        low_part(hS[:, t, :], t, f)

            def fill_mixed(tiles):
                for t in tiles:
                    dve.wait_ge(h_hi, KT * FILL["out2"] + t + 1)
                    dve.tensor_tensor(hS[:, t, T:], y[:, t, :], hS[:, t, 0:T].bitcast(F32), ALU.subtract).then_inc(h_ready, 1)

            dve.wait_ge(gains_in, 16)
            dve.tensor_scalar(nsink[:, :], par("sinks", 0, N_SWA), -1.0, None, ALU.mult)
            dve.tensor_scalar(gqs[:, 0:1], par("qa"), HD2 ** -0.5, None, ALU.mult)
            dve.tensor_scalar(gqs[:, 1:2], par("qb"), HD2 ** -0.5, None, ALU.mult)
            dve.memset(acc[:, :, :], 0.0).then_inc(prep, 1)
            dve.wait_ge(prep, 1)
            n_memset = 1
            for st in stages:
                for n in NORM_BEFORE.get(st.name, ()):
                    norm(n)
                if st.name == "in1":
                    dve.wait_ge(masks_in, 32)
                if st.name in ("pre", "up1_0", "in2"):
                    n = NORM_IN[st.name]
                    fill_x(FILL[st.name], n)
                    if st.name == "pre":
                        split(st, 0, 1)
                        split(st, 0, 2)
                    if st.name == "in2":
                        splits(st, 0, 0, False)
                    fold(dve, n, 2, 5)
                if st.name == "out2":
                    fill_mixed(LAST_TILES)
                    splits(ST["mix2"], KT - 1, 2, True)
                    splits(ST["mix2"], KT - 1, 3, True)
                if st.name == "out1":
                    n_memset += 1
                if st.name in (last1, "out2"):
                    dve.wait_ge(nsum, {last1: 4, "out2": 6}[st.name])
                    n_memset += 1
                    dve.memset(acc[:, 0, :], 0.0).then_inc(prep, 1)
                    dve.wait_ge(prep, n_memset)
                if st.name == "up1_0":
                    for i in range(4):
                        end = dve.memset(ub[i][:, 0:2], 0.0)
                    n_memset += 1
                    end.then_inc(prep, 1)
                    dve.wait_ge(prep, n_memset)
                stage_of["dve"] = st.name
                run_stage(dve, st, step, mtile)

        @block.gpsimd
        def _(pool):
            pool.memset(nhalf[:, :], -0.5).then_inc(half_set, 1)
            pool.wait_ge(half_set, 1)

            def mtile(st, it, p, last):
                pass

            def power(n):
                pool.wait_ge(nms, n + 1)
                pool.tensor_tensor(rs[:, 0:2], ms[:, 0:2], nhalf[:, 0:2], ALU.pow).then_inc(npow, 1)

            def step(name, it):
                st = stage_of["pool"]
                if st == "in2":
                    if name[0] == "N":
                        s = int(name[1])
                        pool.wait_ge(hn_ms, it * 5 + (s + 1))
                        pool.tensor_tensor(rs5[:, s, :], ms5[:, s, :], nhalf[:, 0:4], ALU.pow).then_inc(hn_pow, 1)
                elif name[0] == "Y":
                    before = {"out1": 0, last1: 1, "out2": 2}[st]
                    if isinstance(it, int) and it == 3 and name == "Y3":
                        return
                    i = it * 4 + (int(name[1]) + KT * before)
                    pool.wait_ge(sqy, i + 1)
                    if w0(i - before):
                        pool.wait_ge(sqa, i - before)
                    pool.tensor_tensor(acc[:, 0, :], acc[:, 0, :], sq2[:, :], ALU.add).then_inc(sqa, 1)
                elif name[0] == "X":
                    p = int(name[1])
                    first = 2 * sum(CHUNKS1[:int(st[4])])
                    i = first + it * 4 + p
                    if isinstance(i, int) and i == 0:
                        pool.wait_ge(ncopy, NORM_IN["up1_0"] + 1)
                    pool.wait_ge(ev_done, ST[st].g(it, p) + 1)
                    if w0(i - 3):
                        pool.wait_ge(conv_step, 3 * (i - 3))
                    pool.tensor_tensor(ub[p][:, 2:2 + T], sq[:, p % 2 * T:(p % 2 + 1) * T], rsb[:, 0, :],
                                       ALU.mult).then_inc(u_scaled, 1)
                elif name[0] == "M":
                    if not last_product(st, name, it):
                        product(pool, st, name, it)

            for st in stages:
                for n in (1, 2) if st.name == "out1" else NORM_BEFORE.get(st.name, ()):
                    power(n)
                if st.name in NORM_IN:
                    n = NORM_IN[st.name]
                    if n in (4, 6):
                        pool.wait_ge(ncopy, n)
                        pool.wait_ge(yg, KT * (n // 2 - 1))
                        c = Chain(pool, res_pool, 4, n // 2 - 2)
                        for t in (4, 12):
                            residual(pool, c, t)
                    if n != 7:
                        fold(pool, n, 0, 2)
                    power(n)
                stage_of["pool"] = st.name
                if st.name in ("out1", last1, "in2", "out2") or st.name[:3] == "up1":
                    run_stage(pool, st, step, mtile, carry=False)


def rel_bucket(d):
    exact = N_BUCKETS // 2
    df = np.maximum(d, 1).astype(np.float32)
    large = exact + (np.log(df / np.float32(exact)) / np.float32(np.log(MAX_DISTANCE / exact))
                     * np.float32(N_BUCKETS - exact)).astype(np.int32)
    return np.where(d < exact, d, np.minimum(large, N_BUCKETS - 1))


def constants():
    c = np.zeros((P, N_CS), np.float32)
    p = np.arange(P)
    row = p % 64
    c[:, CS["ident"]:CS["ident"] + P] = np.eye(P)
    c[:, CS["ones"]:CS["ones"] + P] = 1
    c[:, CS["triu"]:CS["triu"] + P] = p[:, None] <= p[None, :]
    t, j = p[:, None], np.arange(T)[None, :]
    dist = P + t - j
    c[:, CS["causal"]:CS["causal"] + T] = np.where(dist >= 0, 0, -BIG)
    c[:, CS["window"]:CS["window"] + T] = np.where((dist >= 0) & (dist < WINDOW), 0, -BIG)
    c[:, CS["dist"]:CS["dist"] + T] = dist
    c[:, CS["slope"]:CS["slope"] + N_SWA] = -(2.0 ** (-8.0 * np.arange(1, N_SWA + 1) / N_SWA))
    for half in range(2):
        r = 64 * half
        for i in range(8):
            for q in (0, 32):
                c[r + q + 2 * i + half, CS["pick"] + i] = 1
    c[:, CS["mA"]] = (row >= 32) & (row < 48)
    c[:, CS["cA"]] = row < 16
    c[:, CS["mB"]] = row < 16
    c[:, CS["cB"]] = (row >= 32) & (row < 48)
    c[:, CS["sgn"]] = np.where(row < 16, -1.0, np.where((row >= 32) & (row < 48), 1.0, 0.0))
    return c


def distance_rows():
    dist = np.arange(N_DIST) - (P - 1)
    out = np.zeros((N_BUCKETS + 4, N_DIST), np.float32)
    ok = dist >= 0
    out[rel_bucket(np.maximum(dist, 0))[ok], np.arange(N_DIST)[ok]] = 1
    for g, (window, r) in enumerate(GROUPS):
        out[N_BUCKETS + g] = np.where(ok & (dist % r == 0) & (dist <= window), 0, -BIG)
    out[N_BUCKETS + 3] = np.where(ok, 0, -BIG)
    return out


def group_rows():
    out = np.zeros((4, A_HEADS + B_HEADS), np.float32)
    for h in range(A_HEADS + B_HEADS):
        out[min(h // A_SLOTS, 3), h] = 1
    return out


def as_units(parts, blocks):
    b = np.concatenate([w.reshape(-1, P, P) for w in parts])
    return np.ascontiguousarray(b.reshape(-1, blocks, P, P).transpose(0, 2, 1, 3)).reshape(-1, P, blocks * P)


def cols(w, i):
    return w[:, i * P:(i + 1) * P]


def swa_tile(j):
    return np.concatenate([np.arange(HD1) + HD1 * j, np.arange(HD1) + HD1 * (8 + j)])


def lay_out(a):
    w_in, w_out, w_up, w_down = (np.asarray(a[n])[0] for n in ("w_in", "w_out", "w_up", "w_down"))
    o_k = N_SWA * HD1
    o_v = o_k + N_KV * HD1
    o_qf = o_v + N_KV * HD1
    o_kf, o_vf, o_f = o_qf + N_FOX * HD1, o_qf + 2 * N_FOX * HD1, o_qf + 3 * N_FOX * HD1
    gate_cols = np.zeros((D, P), np.float32)
    b_f = np.zeros((P, 1), np.float32)
    for r in (0, 32, 64, 96):
        gate_cols[:, r:r + N_FOX] = w_in[:, o_f:]
        b_f[r:r + N_FOX, 0] = np.asarray(a["b_forget"])[0]
    d = {"pre": as_units([w_in[:, o_k:o_v], w_in[:, o_v:o_qf], gate_cols], 16)}
    d["in1"] = as_units([w for j in range(8) for w in (
        w_in[:, swa_tile(j)], cols(w_in[:, o_qf:], j), cols(w_in[:, o_kf:], j), cols(w_in[:, o_vf:], j))], 16)
    rows = np.concatenate([swa_tile(j) for j in range(8)] + [np.arange(o_k, D)])
    wo = w_out[rows]
    d["out1"] = as_units([cols(wo, m) for m in range(KT)], 16)
    at = 0
    for c, n in enumerate(CHUNKS1):
        d[f"up1_{c}"] = as_units([cols(w_up, i + half * F1T) for i in range(at, at + n) for half in range(2)], 16)
        d[f"dn1_{c}"] = as_units([cols(w_down[at * P:(at + n) * P], m) for m in range(KT)], n)
        at += n
    w2 = np.asarray(a["w_in_2"])
    o_b = 3 * A_HEADS * HD2
    o_ga = o_b + 3 * B_HEADS * HD2
    o_gb = o_ga + D
    d["in2"] = as_units([cols(w2, part * A_HEADS + A_SLOTS * g + i) if g < 3
                         else cols(w2[:, o_b:], part * B_HEADS + 2 * i + g - 3)
                         for i in range(A_SLOTS) for g in range(5) for part in range(3)], 15)
    wa, wb = np.asarray(a["w_branch_a_2"]), np.asarray(a["w_branch_b_2"])
    d["mix2"] = as_units([w for m in range(KT) for w in (
        cols(w2[:, o_ga:], m), cols(w2[:, o_gb:], m), cols(wa, m), cols(wb, m))], 11)
    w_out2, w_up2, w_down2 = (np.asarray(a[n]) for n in ("w_out_2", "w_up_2", "w_down_2"))
    d["out2"] = as_units([cols(w_out2, m) for m in range(KT)], 16)
    for c in range(F2T // KT):
        d[f"up2_{c}"] = as_units([cols(w_up2, c * KT + i) for i in range(KT)], 16)
        d[f"dn2_{c}"] = as_units([cols(w_down2[c * D:(c + 1) * D], m) for m in range(KT)], 16)

    def tiles(v):
        return np.asarray(v).reshape(-1, P).T

    grp = np.concatenate([np.asarray(a["grp_swa_g"])[0], np.asarray(a["grp_fox_g"])[0]])[rows]
    conv = np.concatenate([np.asarray(a["conv_w"])[0], np.asarray(a["conv_b"])])
    conv = conv.reshape(4, 2, F1T, P).transpose(3, 2, 1, 0).reshape(P, -1)
    d["pv"] = np.ascontiguousarray(np.concatenate([
        tiles(a["pre_mix_g"]), tiles(grp), tiles(a["post_mix_g"]), tiles(a["pre_ffn_g"]), tiles(a["post_ffn_g"]),
        tiles(a["g_mix_2"]), tiles(a["g_mlp_2"]), tiles(a["q_norm_a_2"]), tiles(a["k_norm_a_2"]),
        tiles(a["q_norm_b_2"]), tiles(a["k_norm_b_2"]), b_f,
        np.broadcast_to(np.asarray(a["sinks"]), (P, N_SWA)), conv], axis=1))
    d["cs"] = constants()
    tab = np.zeros((P, A_HEADS + B_HEADS + N_DIST), np.float32)
    tab[:N_BUCKETS, :A_HEADS + B_HEADS] = np.asarray(a["rel_bias_2"])
    tab[N_BUCKETS:N_BUCKETS + 4, :A_HEADS + B_HEADS] = group_rows()
    tab[:N_BUCKETS + 4, A_HEADS + B_HEADS:] = distance_rows()
    d["tab"] = tab
    d["xT"] = np.ascontiguousarray(np.asarray(a["x"])[0].T)
    return d


def kernel(**inputs):
    import concourse.bacc as bacc
    from concourse.bass_utils import run_bass_kernel_spmd

    nc = bacc.Bacc("TRN2", target_bir_lowering=False, num_devices=1, dynamic_dma_scratch_size=1024)
    arrays = lay_out(inputs)
    dram = {n: nc.dram_tensor(f"in_{n}", v.shape, F32, kind="ExternalInput").ap() for n, v in arrays.items()}
    out = nc.dram_tensor("out_T", (D, T), F32, kind="ExternalOutput").ap()
    build(nc, dram, out)
    r = run_bass_kernel_spmd(nc, [{f"in_{n}": v for n, v in arrays.items()}], core_ids=[0])
    return np.ascontiguousarray(r.results[0]["out_T"].T)[None]
```
